# Optimizing a Trainium2 kernel written in Bass

```python
import jax, jax.numpy as jnp
from jax import lax
import numpy as np

D_MODEL = 1024
BATCH = 1
SEQ = 256
DEPTH = 2

HEAD_DIM = 64
MIX_WIDTH = D_MODEL
MOBA_HEADS = 6
MLSTM_HEADS = 4
SWA_Q_HEADS = 6
SWA_KV_HEADS = 2
MOBA_WIDTH = MOBA_HEADS * HEAD_DIM
MLSTM_WIDTH = MLSTM_HEADS * HEAD_DIM
SWA_Q_WIDTH = SWA_Q_HEADS * HEAD_DIM
SWA_KV_WIDTH = SWA_KV_HEADS * HEAD_DIM
MOBA_BLOCK = 256
MOBA_TOPK = 3
MOBA_Q_CHUNK = 64
MLSTM_CHUNK = 64
CONV_WIDTH = 4
SWA_WINDOW = 128
ROPE_THETA = 10000.0
D_FF = 4 * D_MODEL
NORM_EPS = 1e-6
IN_SPLITS = (MOBA_WIDTH, MOBA_WIDTH, MOBA_WIDTH, SWA_Q_WIDTH, SWA_KV_WIDTH, SWA_KV_WIDTH, 2 * MLSTM_WIDTH, MLSTM_WIDTH, MLSTM_WIDTH, MLSTM_HEADS, MLSTM_HEADS)
IN_WIDTH = sum(IN_SPLITS)


def rms_norm(x, g):
    xf = x.astype(jnp.float32)
    y = xf * lax.rsqrt(jnp.mean(xf * xf, axis=-1, keepdims=True) + NORM_EPS)
    return (y * g.astype(jnp.float32)).astype(x.dtype)

def rope_tables(seq):
    inv = ROPE_THETA ** (-jnp.arange(0, HEAD_DIM, 2, dtype=jnp.float32) / HEAD_DIM)
    ang = jnp.arange(seq, dtype=jnp.float32)[:, None] * inv[None, :]
    return jnp.cos(ang), jnp.sin(ang)

def apply_rope(x, cos, sin):
    c = cos[:, None, :].astype(x.dtype)
    s = sin[:, None, :].astype(x.dtype)
    x1, x2 = jnp.split(x, 2, axis=-1)
    return jnp.concatenate([x1 * c - x2 * s, x2 * c + x1 * s], axis=-1)

def causal_depthwise_conv(x, w, b):
    C = x.shape[-1]
    y = lax.conv_general_dilated(x, w[:, None, :].astype(x.dtype), (1,), [(w.shape[0] - 1, 0)],
                                 dimension_numbers=('NWC', 'WIO', 'NWC'), feature_group_count=C)
    return y + b.astype(x.dtype)

def moba_attention(q, k, v):
    B, H, S, D = q.shape
    L = MOBA_BLOCK
    n_blocks = -(-S // L)
    s_pad = n_blocks * L
    if s_pad != S:
        padw = ((0, 0), (0, 0), (0, s_pad - S), (0, 0))
        q, k, v = jnp.pad(q, padw), jnp.pad(k, padw), jnp.pad(v, padw)
    k_blk = k.reshape(B, H, n_blocks, L, D)
    v_blk = v.reshape(B, H, n_blocks, L, D)
    k_mean = jnp.mean(k_blk.astype(jnp.float32), axis=3)
    top = min(MOBA_TOPK, n_blocks)
    scale = D ** -0.5
    Qc = MOBA_Q_CHUNK
    b_idx = jnp.arange(B)[:, None, None, None]
    h_idx = jnp.arange(H)[None, :, None, None]

    def one_chunk(c):
        start = c * Qc
        blk = start // L
        qc = lax.dynamic_slice_in_dim(q, start, Qc, axis=2)
        gate = jnp.einsum('bhqd,bhnd->bhqn', qc.astype(jnp.float32), k_mean)
        gate = jnp.where(jnp.arange(n_blocks) < blk, gate, -jnp.inf)
        _, sel = lax.top_k(gate, top)
        sel_ok = jnp.arange(top) < blk
        k_sel = k_blk[b_idx, h_idx, sel]
        v_sel = v_blk[b_idx, h_idx, sel]
        s_sel = jnp.einsum('bhqd,bhqrld->bhqrl', qc, k_sel).astype(jnp.float32) * scale
        s_sel = jnp.where(sel_ok[:, None], s_sel, -jnp.inf).reshape(B, H, Qc, top * L)
        k_own = lax.dynamic_slice_in_dim(k, blk * L, L, axis=2)
        v_own = lax.dynamic_slice_in_dim(v, blk * L, L, axis=2)
        s_own = jnp.einsum('bhqd,bhld->bhql', qc, k_own).astype(jnp.float32) * scale
        q_pos = start + jnp.arange(Qc)
        k_pos = blk * L + jnp.arange(L)
        s_own = jnp.where(k_pos[None, :] <= q_pos[:, None], s_own, -jnp.inf)
        p = jax.nn.softmax(jnp.concatenate([s_sel, s_own], axis=-1), axis=-1).astype(v.dtype)
        p_sel = p[..., :top * L].reshape(B, H, Qc, top, L)
        p_own = p[..., top * L:]
        return (jnp.einsum('bhqrl,bhqrld->bhqd', p_sel, v_sel)
                + jnp.einsum('bhql,bhld->bhqd', p_own, v_own))

    outs = lax.map(one_chunk, jnp.arange(s_pad // Qc))
    out = jnp.moveaxis(outs, 0, 2).reshape(B, H, s_pad, D)
    return out[:, :, :S]

def mlstm_chunkwise(q, k, v, i_pre, f_pre):
    B, H, S, D = q.shape
    L = MLSTM_CHUNK
    nc = S // L
    k = k * (D ** -0.5)
    log_f = jax.nn.log_sigmoid(f_pre)

    def chunks(a):
        return jnp.moveaxis(a.reshape(B, H, nc, L, *a.shape[3:]), 2, 0)

    causal = jnp.tril(jnp.ones((L, L), dtype=bool))

    def step(carry, inp):
        C, n, m = carry
        qc, kc, vc, ic, lfc = inp
        b = jnp.cumsum(lfc, axis=-1)
        a = b[..., -1]
        d = b[..., :, None] - b[..., None, :] + ic[..., None, :]
        d = jnp.where(causal, d, -jnp.inf)
        inter = b + m[..., None]
        m_t = jnp.maximum(inter, jnp.max(d, axis=-1))
        w_intra = jnp.exp(d - m_t[..., None])
        w_inter = jnp.exp(inter - m_t)
        qk = jnp.einsum('bhtd,bhsd->bhts', qc, kc) * w_intra
        num = (w_inter[..., None] * jnp.einsum('bhtd,bhde->bhte', qc, C)
               + jnp.einsum('bhts,bhse->bhte', qk, vc))
        den = w_inter * jnp.einsum('bhtd,bhd->bht', qc, n) + jnp.sum(qk, axis=-1)
        h = num / jnp.maximum(jnp.abs(den), jnp.exp(-m_t))[..., None]
        g = a[..., None] - b + ic
        m_new = jnp.maximum(a + m, jnp.max(g, axis=-1))
        w_s = jnp.exp(g - m_new[..., None])
        decay = jnp.exp(a + m - m_new)
        C_new = decay[..., None, None] * C + jnp.einsum('bhsd,bhse->bhde', kc * w_s[..., None], vc)
        n_new = decay[..., None] * n + jnp.einsum('bhs,bhsd->bhd', w_s, kc)
        return (C_new, n_new, m_new), h

    init = (jnp.zeros((B, H, D, D), jnp.float32), jnp.zeros((B, H, D), jnp.float32),
            jnp.zeros((B, H), jnp.float32))
    _, h = lax.scan(step, init, (chunks(q), chunks(k), chunks(v), chunks(i_pre), chunks(log_f)))
    return jnp.moveaxis(h, 0, 2).reshape(B, H, S, D)

def swa_attention(q, k, v, sinks):
    B, S, Hq, D = q.shape
    Hkv = k.shape[2]
    G = Hq // Hkv
    W = SWA_WINDOW
    nb = S // W
    qb = q.reshape(B, nb, W, Hkv, G, D)

    def band(a):
        ab = a.reshape(B, nb, W, Hkv, D)
        prev = jnp.pad(ab, ((0, 0), (1, 0), (0, 0), (0, 0), (0, 0)))[:, :-1]
        return jnp.concatenate([prev, ab], axis=2)

    kb, vb = band(k), band(v)
    s = jnp.einsum('bnqkgd,bnjkd->bnkgqj', qb, kb).astype(jnp.float32) * (D ** -0.5)
    qi = jnp.arange(W)[:, None] + W
    kj = jnp.arange(2 * W)[None, :]
    in_window = (qi - kj >= 0) & (qi - kj < W)
    exists = (jnp.arange(nb)[:, None, None] > 0) | (kj[None] >= W)
    mask = in_window[None] & exists
    s = jnp.where(mask[None, :, None, None], s, -jnp.inf)
    sink = jnp.broadcast_to(sinks.astype(jnp.float32).reshape(1, 1, Hkv, G, 1, 1), s.shape[:-1] + (1,))
    p = jax.nn.softmax(jnp.concatenate([s, sink], axis=-1), axis=-1)[..., :-1].astype(v.dtype)
    o = jnp.einsum('bnkgqj,bnjkd->bnqkgd', p, vb)
    return o.reshape(B, S, Hq, D)

def hybrid_layer(x, cos, sin, ln1, w_in, conv_w, conv_b, igate_b, fgate_b, mlstm_norm,
                 moba_q_norm, moba_k_norm, swa_q_norm, swa_k_norm, swa_sinks, w_out,
                 ln2, w_up, w_down):
    B, S, _ = x.shape
    hn = rms_norm(x, ln1)
    proj = hn @ w_in
    idx = np.cumsum(IN_SPLITS)[:-1].tolist()
    mq, mk, mv, sq, sk, sv, xqk, xv, xo, xi, xf = jnp.split(proj, idx, axis=-1)

    def heads(a):
        return a.reshape(B, S, -1, HEAD_DIM)

    def bhsd(a):
        return a.transpose(0, 2, 1, 3)

    mq = apply_rope(rms_norm(heads(mq), moba_q_norm), cos, sin)
    mk = apply_rope(rms_norm(heads(mk), moba_k_norm), cos, sin)
    y_moba = bhsd(moba_attention(bhsd(mq), bhsd(mk), bhsd(heads(mv)))).reshape(B, S, MOBA_WIDTH)

    qk = jax.nn.silu(causal_depthwise_conv(xqk, conv_w, conv_b))
    lq, lk = jnp.split(qk, 2, axis=-1)
    i_pre = (xi + igate_b).astype(jnp.float32).transpose(0, 2, 1)
    f_pre = (xf + fgate_b).astype(jnp.float32).transpose(0, 2, 1)
    h = mlstm_chunkwise(bhsd(heads(lq)).astype(jnp.float32), bhsd(heads(lk)).astype(jnp.float32),
                        bhsd(heads(xv)).astype(jnp.float32), i_pre, f_pre)
    h = bhsd(h).astype(x.dtype) * heads(jax.nn.sigmoid(xo))
    y_mlstm = rms_norm(h, mlstm_norm).reshape(B, S, MLSTM_WIDTH)

    sq = apply_rope(rms_norm(heads(sq), swa_q_norm), cos, sin)
    sk = apply_rope(rms_norm(heads(sk), swa_k_norm), cos, sin)
    y_swa = swa_attention(sq, sk, heads(sv), swa_sinks).reshape(B, S, SWA_Q_WIDTH)

    x = x + jnp.concatenate([y_moba, y_mlstm, y_swa], axis=-1) @ w_out
    u = rms_norm(x, ln2) @ w_up
    return x + jnp.square(jax.nn.relu(u)) @ w_down

def first_inputs(seed: int = 0) -> dict:
    key = jax.random.key(seed)
    ks = jax.random.split(key, 17)
    f32 = jnp.float32

    def nrm(k, shape, scale):
        return jax.random.normal(k, shape, f32) * scale

    return {
        'x': nrm(ks[0], (BATCH, SEQ, D_MODEL), 1.0),
        'ln1': 1.0 + nrm(ks[1], (DEPTH, D_MODEL), 0.02),
        'w_in': nrm(ks[2], (DEPTH, D_MODEL, IN_WIDTH), D_MODEL ** -0.5),
        'conv_w': nrm(ks[3], (DEPTH, CONV_WIDTH, 2 * MLSTM_WIDTH), CONV_WIDTH ** -0.5),
        'conv_b': nrm(ks[4], (DEPTH, 2 * MLSTM_WIDTH), 0.02),
        'igate_b': nrm(ks[5], (DEPTH, MLSTM_HEADS), 0.1),
        'fgate_b': jnp.linspace(3.0, 6.0, MLSTM_HEADS, dtype=f32)[None] + nrm(ks[6], (DEPTH, MLSTM_HEADS), 0.1),
        'mlstm_norm': 1.0 + nrm(ks[7], (DEPTH, MLSTM_HEADS, HEAD_DIM), 0.02),
        'moba_q_norm': 1.0 + nrm(ks[8], (DEPTH, HEAD_DIM), 0.02),
        'moba_k_norm': 1.0 + nrm(ks[9], (DEPTH, HEAD_DIM), 0.02),
        'swa_q_norm': 1.0 + nrm(ks[10], (DEPTH, HEAD_DIM), 0.02),
        'swa_k_norm': 1.0 + nrm(ks[11], (DEPTH, HEAD_DIM), 0.02),
        'swa_sinks': nrm(ks[12], (DEPTH, SWA_Q_HEADS), 1.0),
        'w_out': nrm(ks[13], (DEPTH, MIX_WIDTH, D_MODEL), MIX_WIDTH ** -0.5),
        'ln2': 1.0 + nrm(ks[14], (DEPTH, D_MODEL), 0.02),
        'w_up': nrm(ks[15], (DEPTH, D_MODEL, D_FF), D_MODEL ** -0.5),
        'w_down': nrm(ks[16], (DEPTH, D_FF, D_MODEL), D_FF ** -0.5),
    }

def first_block(x, ln1, w_in, conv_w, conv_b, igate_b, fgate_b, mlstm_norm, moba_q_norm,
              moba_k_norm, swa_q_norm, swa_k_norm, swa_sinks, w_out, ln2, w_up, w_down):
    cos, sin = rope_tables(x.shape[1])
    for l in range(DEPTH):
        x = hybrid_layer(x, cos, sin, ln1[l], w_in[l], conv_w[l], conv_b[l], igate_b[l], fgate_b[l],
                         mlstm_norm[l], moba_q_norm[l], moba_k_norm[l], swa_q_norm[l], swa_k_norm[l],
                         swa_sinks[l], w_out[l], ln2[l], w_up[l], w_down[l])
    return x


RET_HEADS = D_MODEL // 128
RET_QK_DIM = 64
RET_V_DIM = 128
RET_QK = RET_HEADS * RET_QK_DIM
RET_V = RET_HEADS * RET_V_DIM
CHUNK = 128
ROPE_BASE = 10000.0
POOL_WINDOWS = (2, 4, 8, 16)
POOL_GROUPS = len(POOL_WINDOWS)
POOL_DIM = D_MODEL // 2
POOL_GROUP_DIM = POOL_DIM // POOL_GROUPS
N_BRANCH = 2
IN_COLS = 2 * RET_QK + 2 * RET_V + POOL_DIM + N_BRANCH * D_MODEL
IN_SPLITS_2 = (RET_QK, 2 * RET_QK, 2 * RET_QK + RET_V, 2 * RET_QK + 2 * RET_V,
             2 * RET_QK + 2 * RET_V + POOL_DIM)
_FF_RAW = -(-8 * D_MODEL // 3)
D_FF_2 = -(-_FF_RAW // 256) * 256
N_MOD = 6
EPS = 1e-6


def rmsnorm(x, w):
    xf = x.astype(jnp.float32)
    y = xf * lax.rsqrt(jnp.mean(xf * xf, axis=-1, keepdims=True) + EPS)
    return (y * w.astype(jnp.float32)).astype(x.dtype)

def head_rmsnorm(x):
    xf = x.astype(jnp.float32)
    y = xf * lax.rsqrt(jnp.mean(xf * xf, axis=-1, keepdims=True) + EPS)
    return y.astype(x.dtype)

def modulate(h, shift, scale):
    return h * (1.0 + scale[:, None, :]) + shift[:, None, :]

def rotary(x, cos, sin):
    x1, x2 = jnp.split(x, 2, axis=-1)
    return jnp.concatenate([x1 * cos - x2 * sin, x2 * cos + x1 * sin], axis=-1)

def retention_chunkwise(q, k, v):
    bsz, s, h, dk = q.shape
    dv = v.shape[-1]
    n = s // CHUNK
    dt = q.dtype
    log_g = jnp.log1p(-(2.0 ** (-5.0 - jnp.arange(h, dtype=jnp.float32))))
    idx = jnp.arange(CHUNK, dtype=jnp.float32)
    diff = idx[:, None] - idx[None, :]
    intra = jnp.where(diff >= 0, jnp.exp(log_g[:, None, None] * jnp.maximum(diff, 0.0)), 0.0).astype(dt)
    q_dec = jnp.exp(log_g[:, None] * (idx + 1.0)).astype(dt)
    k_dec = jnp.exp(log_g[:, None] * (CHUNK - 1.0 - idx)).astype(dt)
    chunk_dec = jnp.exp(log_g * CHUNK).astype(dt)
    qc = (q * (dk ** -0.5)).reshape(bsz, n, CHUNK, h, dk)
    kc = k.reshape(bsz, n, CHUNK, h, dk)
    vc = v.reshape(bsz, n, CHUNK, h, dv)
    scores = jnp.einsum('bncha,bnmha->bnhcm', qc, kc) * intra[None, None]
    inner = jnp.einsum('bnhcm,bnmhd->bnchd', scores, vc)
    kv = jnp.einsum('bnmha,hm,bnmhd->bnhad', kc, k_dec, vc)

    def step(state, kv_i):
        return state * chunk_dec[None, :, None, None] + kv_i, state

    init = jnp.zeros((bsz, h, dk, dv), dtype=kv.dtype)
    _, prev = lax.scan(step, init, jnp.moveaxis(kv, 1, 0))
    prev = jnp.moveaxis(prev, 0, 1)
    cross = jnp.einsum('bncha,hc,bnhad->bnchd', qc, q_dec, prev)
    return (inner + cross).reshape(bsz, s, h, dv)

def causal_multiscale_pool(p):
    bsz, s, _ = p.shape
    pg = p.reshape(bsz, s, POOL_GROUPS, POOL_GROUP_DIM)
    cs = jnp.cumsum(pg.astype(jnp.float32), axis=1)
    t = jnp.arange(s, dtype=jnp.float32)
    outs = []
    for g, w in enumerate(POOL_WINDOWS):
        csg = cs[:, :, g]
        lag = jnp.pad(csg[:, :s - w], ((0, 0), (w, 0), (0, 0)))
        cnt = jnp.minimum(t + 1.0, float(w))
        outs.append((csg - lag) / cnt[None, :, None])
    mean = jnp.stack(outs, axis=2).astype(p.dtype)
    return mean - pg

def second_inputs(seed: int = 0) -> dict:
    key = jax.random.key(seed)
    ks = jax.random.split(key, 16)
    f32 = jnp.float32
    d = D_MODEL

    def w(k, shape, fan_in, mult=1.0):
        return jax.random.normal(k, shape, f32) * (mult * fan_in ** -0.5)

    return {
        "x": jax.random.normal(ks[0], (BATCH, SEQ, d), f32),
        "c": jax.random.normal(ks[1], (BATCH, d), f32),
        "w_ada": w(ks[2], (DEPTH, d, N_MOD * d), d, 0.5),
        "b_ada": 0.01 * jax.random.normal(ks[3], (DEPTH, N_MOD * d), f32),
        "norm1": 1.0 + 0.02 * jax.random.normal(ks[4], (DEPTH, d), f32),
        "w_in": w(ks[5], (DEPTH, d, IN_COLS), d),
        "w_ret_o": w(ks[6], (DEPTH, RET_V, d), RET_V),
        "w_pool_grp": w(ks[7], (DEPTH, POOL_GROUPS, POOL_GROUP_DIM, POOL_GROUP_DIM), POOL_GROUP_DIM),
        "pool_scale": 1.0 + 0.1 * jax.random.normal(ks[8], (DEPTH, POOL_DIM), f32),
        "w_pool_o": w(ks[9], (DEPTH, POOL_DIM, d), POOL_DIM),
        "w_out": w(ks[10], (DEPTH, d, d), d),
        "norm2": 1.0 + 0.02 * jax.random.normal(ks[11], (DEPTH, d), f32),
        "w_ffn_in": w(ks[12], (DEPTH, d, 2 * D_FF_2), d),
        "w_ffn_out": w(ks[13], (DEPTH, D_FF_2, d), D_FF_2),
        "final_norm": 1.0 + 0.02 * jax.random.normal(ks[14], (d,), f32),
    }

def second_block(x, c, w_ada, b_ada, norm1, w_in, w_ret_o, w_pool_grp, pool_scale, w_pool_o,
              w_out, norm2, w_ffn_in, w_ffn_out, final_norm):
    bsz, s, _ = x.shape
    half = RET_QK_DIM // 2
    inv_freq = ROPE_BASE ** (-jnp.arange(half, dtype=jnp.float32) / half)
    ang = jnp.arange(s, dtype=jnp.float32)[:, None] * inv_freq[None, :]
    cos = jnp.cos(ang)[:, None, :].astype(x.dtype)
    sin = jnp.sin(ang)[:, None, :].astype(x.dtype)
    c_act = jax.nn.silu(c)

    for l in range(DEPTH):
        mod = c_act @ w_ada[l] + b_ada[l]
        sh1, sc1, g1, sh2, sc2, g2 = jnp.split(mod, N_MOD, axis=-1)

        h = modulate(rmsnorm(x, norm1[l]), sh1, sc1)
        proj = h @ w_in[l]
        q, k, v, g_sw, p_in, gates = jnp.split(proj, IN_SPLITS_2, axis=-1)
        q = rotary(q.reshape(bsz, s, RET_HEADS, RET_QK_DIM), cos, sin)
        k = rotary(k.reshape(bsz, s, RET_HEADS, RET_QK_DIM), cos, sin)
        v = v.reshape(bsz, s, RET_HEADS, RET_V_DIM)
        ret = head_rmsnorm(retention_chunkwise(q, k, v)).reshape(bsz, s, RET_V)
        ret_d = (jax.nn.silu(g_sw) * ret) @ w_ret_o[l]

        pooled = causal_multiscale_pool(p_in)
        pooled = jnp.einsum('bsgi,gio->bsgo', pooled, w_pool_grp[l]).reshape(bsz, s, POOL_DIM)
        pool_d = (pooled * pool_scale[l]) @ w_pool_o[l]

        a_ret, a_pool = jnp.split(gates, N_BRANCH, axis=-1)
        merged = jax.nn.sigmoid(a_ret) * ret_d + jax.nn.sigmoid(a_pool) * pool_d
        x = x + g1[:, None, :] * (merged @ w_out[l])

        h2 = modulate(rmsnorm(x, norm2[l]), sh2, sc2)
        gate, up = jnp.split(h2 @ w_ffn_in[l], 2, axis=-1)
        x = x + g2[:, None, :] * ((jax.nn.silu(gate) * up) @ w_ffn_out[l])

    return rmsnorm(x, final_norm)


def setup_inputs(seed=0):
    out = dict(first_inputs(seed))
    for name, value in second_inputs(seed + 1).items():
        if name != "x":
            out[name + "_2"] = value
    return out


def reference(
    x, ln1, w_in, conv_w, conv_b, igate_b, fgate_b, mlstm_norm, moba_q_norm, moba_k_norm,
    swa_q_norm, swa_k_norm, swa_sinks, w_out, ln2, w_up, w_down, c_2, w_ada_2, b_ada_2, norm1_2,
    w_in_2, w_ret_o_2, w_pool_grp_2, pool_scale_2, w_pool_o_2, w_out_2, norm2_2, w_ffn_in_2,
    w_ffn_out_2, final_norm_2,
):
    x = first_block(
        x, ln1, w_in, conv_w, conv_b, igate_b, fgate_b, mlstm_norm, moba_q_norm, moba_k_norm,
        swa_q_norm, swa_k_norm, swa_sinks, w_out, ln2, w_up, w_down,
    )
    return second_block(
        x, c_2, w_ada_2, b_ada_2, norm1_2, w_in_2, w_ret_o_2, w_pool_grp_2, pool_scale_2,
        w_pool_o_2, w_out_2, norm2_2, w_ffn_in_2, w_ffn_out_2, final_norm_2,
    )


_drawn_inputs = setup_inputs


def setup_inputs(seed=0):
    import zlib

    import numpy as np

    out = dict(_drawn_inputs(seed))
    spreads = {}
    factors = {'conv_b': 4.173,
     'igate_b': 35.783,
     'mlstm_norm': 4.624,
     'moba_q_norm': 8.0,
     'moba_k_norm': 8.0,
     'swa_q_norm': 8.0,
     'swa_k_norm': 8.0,
     'swa_sinks': 3.728,
     'b_ada_2': 8.0,
     'norm1_2': 8.0,
     'pool_scale_2': 6.306,
     'norm2_2': 8.0,
     'final_norm_2': 8.151}
    for name, (base, spread) in spreads.items():
        noise = np.random.default_rng([zlib.crc32(name.encode()), seed]).standard_normal(out[name].shape)
        drawn = base * np.exp(spread * noise) if base else spread * noise
        out[name] = __import__('jax').numpy.asarray(drawn.astype(out[name].dtype))
    for name, factor in factors.items():
        out[name] = (out[name] * factor).astype(out[name].dtype)
    return out
```

```python
from contextlib import ExitStack

import concourse.bass as bass
from concourse import mybir

F32 = mybir.dt.float32
F32R = mybir.dt.float32r
ACT = mybir.ActivationFunctionType
ALU = mybir.AluOpType
AX = mybir.AxisListType.X
ds = bass.ds

P = 128
D = 1024
S = 256
KT = D // P
LAYERS = 2
SLOTS = 4
EPS = 1e-6
HD = 64
BIG = 1e30

A_PROJ, A_OUT, A_UP, A_DOWN = 24, 8, 32, 32
A_QUADS = (A_PROJ + A_OUT + A_UP + A_DOWN) // 4
A_UNITS = A_PROJ + A_OUT + A_UP + A_DOWN // 4
C_MQ, C_MK, C_MV, C_SQ, C_SK, C_SV, C_XQK, C_XV, C_XO, C_GATES = 0, 3, 6, 9, 12, 13, 14, 18, 20, 22
FF2 = 2816
B_PROJ, B_RET, B_POOL, B_OUT, B_FFN, B_FFO = 44, 8, 4, 8, 44, 32
B_QUADS = (B_PROJ + B_RET + B_POOL + B_OUT + B_FFN + B_FFO) // 4
B_UNITS = B_PROJ + B_RET + B_POOL + B_OUT + B_FFN + B_FFO // 4
B_Q, B_K, B_V, B_G, B_PIN, B_ARET, B_APOOL = 0, 4, 8, 16, 24, 28, 36
FFO_PARTS = (6, 6, 5, 5)
FFO_AT = (0, 6, 12, 17)
MOD = 6 * KT
ADA = MOD // 2

V_LN1, V_LN2, V_N1, V_N2, V_FIN, V_C, V_CONVB, V_PSC, V_CONVW = 0, 16, 32, 48, 64, 72, 80, 88, 96
V_BADA, V_MLN, V_HN = 128, 224, 228
VECS = 236
CHAIN_A, CHAIN_B = 256, 128
K_ID, K_ONE, K_BLK, K_ROT, K_SWP, K_COS, K_SIN = 0, 128, 256, 384, 512, 640, 896
K_MCA, K_MSW, K_MT, K_SEL, K_PAIR = 1152, 1536, 1920, 2176, 2688
K_DEC, K_CNT = 2944, 4992
NCONST = 5056


def shape_constants():
    import numpy as np

    f = np.float32
    c = np.zeros((P, NCONST), f)
    p = np.arange(P)
    t = np.arange(S)
    c[:, K_ID:K_ID + P] = np.eye(P, dtype=f)
    c[:, K_ONE:K_ONE + P] = 1.0
    c[:, K_BLK:K_BLK + P] = (p[:, None] // HD == p[None, :] // HD)
    for m in range(P):
        low = m % HD < HD // 2
        c[m + HD // 2 if low else m - HD // 2, K_ROT + m] = -1.0 if low else 1.0
        c[(m + HD) % P, K_SWP + m] = 1.0
    inv = f(10000.0) ** (-np.arange(0, HD, 2, dtype=f) / f(HD))
    ang = t.astype(f)[None, :] * inv[p % (HD // 2)][:, None]
    c[:, K_COS:K_COS + S] = np.cos(ang)
    c[:, K_SIN:K_SIN + S] = np.sin(ang)
    q1 = p[:, None] + P
    c[:, K_MCA:K_MCA + P] = np.where(p[None, :] <= p[:, None], 0.0, -BIG)
    c[:, K_MCA + P:K_MCA + 3 * P] = np.where(t[None, :] <= q1, 0.0, -BIG)
    c[:, K_MSW:K_MSW + P] = c[:, K_MCA:K_MCA + P]
    c[:, K_MSW + P:K_MSW + 3 * P] = np.where((t[None, :] <= q1) & (q1 - t[None, :] < P), 0.0, -BIG)
    c[:, K_MT:K_MT + S] = np.where(t[None, :] >= p[:, None], 0.0, BIG)
    for h in range(4):
        c[h, K_SEL + h * P:K_SEL + (h + 1) * P] = 1.0
        c[h, K_PAIR + h * HD:K_PAIR + (h + 1) * HD] = 1.0
    for h in range(8):
        g = np.log1p(-(f(2.0) ** (f(-5.0) - f(h))))
        d = (t[None, :] - p[:, None]).astype(f)
        c[:, K_DEC + h * S:K_DEC + (h + 1) * S] = np.where(d >= 0, np.exp(g * np.maximum(d, 0)), 0.0) * f(0.125)
    for g, w in enumerate((2, 4, 8, 16)):
        c[:, K_CNT + g * 16:K_CNT + (g + 1) * 16] = f(1.0) / np.minimum(t[:16] + 1, w).astype(f)
    return c


class Chain:

    def __init__(self, eng, sem, base):
        self.eng, self.sem, self.base, self.n = eng, sem, base, 0

    def done(self, ins):
        ins.then_inc(self.sem, 1)
        self.n += 1
        return self.n

    def wait(self, mark):
        self.eng.wait_ge(self.sem, self.base + mark)

    def link(self, ins):
        self.wait(self.done(ins))


def program(nc, consts, x, ln1, w_in, conv_w, conv_b, igate_b, fgate_b, mlstm_norm, moba_q_norm, moba_k_norm,
            swa_q_norm, swa_k_norm, swa_sinks, w_out, ln2, w_up, w_down, c_2, w_ada_2, b_ada_2, norm1_2, w_in_2,
            w_ret_o_2, w_pool_grp_2, pool_scale_2, w_pool_o_2, w_out_2, norm2_2, w_ffn_in_2, w_ffn_out_2,
            final_norm_2, out):
    ctx = ExitStack()
    with ctx:
        def sb(name, shape, dt=F32, stack=ctx):
            return stack.enter_context(nc.sbuf_tensor(name, shape, dt))

        def sem(name):
            return ctx.enter_context(nc.semaphore(name))

        raw = sb("raw", [P, SLOTS, KT, P])
        w_hi = sb("w_hi", [P, SLOTS, KT, P], F32R)
        w_lo = sb("w_lo", [P, SLOTS, KT, P], F32R)
        con = sb("con", [P, NCONST])
        xT = sb("xT", [P, KT, S])
        h_hi = sb("h_hi", [P, KT, S], F32R)
        h_lo = sb("h_lo", [P, KT, S], F32R)
        y_hi = sb("y_hi", [P, KT, S], F32R)
        y_lo = sb("y_lo", [P, KT, S], F32R)
        tmp4 = sb("tmp4", [P, 4, S])
        vecT = sb("vecT", [P, VECS])
        modT = sb("modT", [P, LAYERS * MOD])
        lv = sb("lv", [P, 64])
        lm = sb("lm", [P, MOD])
        gate_b = sb("gate_b", [4, 4])
        lgate = sb("lgate", [4, 2])
        ones4 = sb("ones4", [4, S])
        sinkrow = sb("sinkrow", [1, 12])
        sink = sb("sink", [P, 12])
        lsink = sb("lsink", [P, 6])
        lnegsink = sb("lnegsink", [P, 6])
        cact = sb("cact", [P, KT])
        rstd = sb("rstd", [P, S])
        var = sb("var", [P, S])
        rs_tmp = sb("rs_tmp", [P, S])
        spare = sb("spare", [P, 2])
        wgrp = sb("wgrp", [P, LAYERS * 4, P])
        with ExitStack() as first:
            ada = sb("ada", [P, 2, KT, 256], F32, first)
            ada_acc = sb("ada_acc", [P, 2, 256], F32, first)
        with ExitStack() as second:
            rotb = sb("rotb", [P, 512], F32, second)
            pb = sb("pb", [P, 2, 384], F32, second)
            sqb = sb("sqb", [P, 512], F32, second)
            rb = sb("rb", [P, 512], F32, second)
            bv = sb("bv", [P, 512], F32, second)
            b_tmp = sb("b_tmp", [P, 512], F32, second)
            pad = sb("pad", [P, 2, 16 + S], F32, second)
            lgrp = sb("lgrp", [P, 4, P], F32, second)
        sb("reserve_turns", [P, 4608])
        with ExitStack() as mlp:
            u_hi = sb("u_hi", [P, 32, S], F32R, mlp)
            u_lo = sb("u_lo", [P, 32, S], F32R, mlp)
        with ExitStack() as ends:
            xtok = sb("xtok", [P, 2, D], F32, ends)
            rows = sb("rows", [P, 2, P], F32, ends)
        with ExitStack() as norms:
            hf = sb("hf", [P, KT, S], F32, norms)
        with ExitStack() as mix_a:
            proj = sb("proj", [P, 22, S], F32, mix_a)
            gi = sb("gi", [4, S], F32, mix_a)
            gf = sb("gf", [4, S], F32, mix_a)
            g_a = sb("g_a", [4, S], F32, mix_a)
            g_e = sb("g_e", [4, S], F32, mix_a)
            g_F = sb("g_F", [4, S], F32, mix_a)
            g_u = sb("g_u", [4, S], F32, mix_a)
            g_M = sb("g_M", [4, S], F32, mix_a)
            g_G = sb("g_G", [4, S], F32, mix_a)
            g_E = sb("g_E", [4, S], F32, mix_a)
            vtok = sb("vtok", [P, 3, 4, P], F32, mix_a)
            skswap = sb("skswap", [P, S], F32, mix_a)
            rv = sb("rv", [P, 2, 512], F32, mix_a)
            rr = sb("rr", [P, 2, 512], F32, mix_a)
            r_tmp = sb("r_tmp", [P, 512], F32, mix_a)
            st_mx = sb("st_mx", [P, 2, 2], F32, mix_a)
            st_nb = sb("st_nb", [P, 2, 2], F32, mix_a)
            st_den = sb("st_den", [P, 2, 2], F32, mix_a)
            st_es = sb("st_es", [P, 2, 2], F32, mix_a)
            st_rec = sb("st_rec", [P, 2, 2], F32, mix_a)
            nucol = sb("nucol", [P, 8], F32, mix_a)
            cv = sb("cv", [P, 4, S], F32, mix_a)
            sqq = sb("sqq", [P, 2, 512], F32, mix_a)
            mbc = sb("mbc", [P, 4, S], F32, mix_a)
            marg = sb("marg", [P, 2, 384], F32, mix_a)
            mw = sb("mw", [P, 2, 384], F32, mix_a)
        with ExitStack() as mix_b:
            projb = sb("projb", [P, 44, S], F32, mix_b)
            vtokb = sb("vtokb", [P, 4, 4, P], F32, mix_b)
        sm, pr = marg, mw
        pT = sqq[:, :, 0:384]
        rot = r_tmp
        ebc, mh = rv[:, 1], rr[:, 1]

        one = con[:, K_ONE:K_ONE + P]
        ident = con[:, K_ID:K_ID + P]
        blk = con[:, K_BLK:K_BLK + P]
        rotm = con[:, K_ROT:K_ROT + P]
        swpm = con[:, K_SWP:K_SWP + P]
        cos = con[:, K_COS:K_COS + S]
        sin = con[:, K_SIN:K_SIN + S]
        cos2 = cos.unsqueeze(1).to_broadcast([P, 2, S])
        sin2 = sin.unsqueeze(1).to_broadcast([P, 2, S])

        acc = ctx.enter_context(nc.psum_tensor("acc", [P, SLOTS, 512], F32))
        mx = ctx.enter_context(nc.psum_tensor("mx", [P, 4, 512], F32))

        landed = [sem(f"landed{j}") for j in range(SLOTS)]
        hi_ready = sem("hi_ready")
        lo_ready = sem("lo_ready")
        slab_used = sem("slab_used")
        acc_free = sem("acc_free")
        ada_landed = [sem(f"ada_landed{j}") for j in range(2)]
        ada_sum = sem("ada_sum")
        ada_col = sem("ada_col")
        ada_out = sem("ada_out")
        s_con = sem("s_con")
        s_con2 = sem("s_con2")
        s_x = sem("s_x")
        s_rows = sem("s_rows")
        s_small = sem("s_small")
        s_grp = sem("s_grp")
        boot_t = sem("boot_t")
        boot_v = sem("boot_v")
        boot_a = sem("boot_a")
        n_sq = sem("n_sq")
        n_var = sem("n_var"); n_ln = sem("n_ln"); n_rs = sem("n_rs")
        n_ss = sem("n_ss")
        h_ready = sem("h_ready")
        chain_n = sem("chain_n")
        chain_a = sem("chain_a")
        chain_b = sem("chain_b")
        chain_up = sem("chain_up")
        chain_ffn = sem("chain_ffn")
        chain_ret = sem("chain_ret")
        chain_pool = sem("chain_pool")
        chain_ada = sem("chain_ada")
        v_t = sem("v_t"); v_sb = sem("v_sb")
        qk_sq = sem("qk_sq"); qk_ss = sem("qk_ss"); qk_r = sem("qk_r"); qk_ln = sem("qk_ln"); qk_s = sem("qk_s"); qk_n = sem("qk_n")
        qk_rot = sem("qk_rot"); qk_rope = sem("qk_rope")
        swp_t = sem("swp_t"); swp_sb = sem("swp_sb")
        cv_ready = sem("cv_ready"); cv_silu = sem("cv_silu")
        f_abs = sem("f_abs"); f_ln = sem("f_ln"); f_M = sem("f_M"); f_G = sem("f_G"); f_E = sem("f_E")
        f_bc = sem("f_bc"); f_bcsb = sem("f_bcsb"); f_uc = sem("f_uc"); f_ucsb = sem("f_ucsb")
        f_exp = sem("f_exp"); ml_v = sem("ml_v"); ml_ln = sem("ml_ln"); ml_rs = sem("ml_rs")
        ml_s = sem("ml_s"); ml_arg = sem("ml_arg"); ml_w = sem("ml_w"); ml_p = sem("ml_p"); ml_nd = sem("ml_nd")
        ml_xo = sem("ml_xo"); ml_h = sem("ml_h"); ml_sq = sem("ml_sq"); ml_ss = sem("ml_ss"); ml_y = sem("ml_y")
        at_s = sem("at_s"); at_m = sem("at_m"); at_nb = sem("at_nb"); at_e = sem("at_e"); at_p = sem("at_p")
        at_t = sem("at_t"); at_pt = sem("at_pt"); at_o = sem("at_o"); at_y = sem("at_y")
        b_ln = sem("b_ln"); b_rs = sem("b_rs")
        g_used = sem("g_used")
        u_ready = sem("u_ready")
        b_rot = sem("b_rot"); b_rope = sem("b_rope"); b_vt = sem("b_vt"); b_vsb = sem("b_vsb")
        b_s = sem("b_s"); b_p = sem("b_p"); b_ret = sem("b_ret"); b_sq = sem("b_sq"); b_ss = sem("b_ss")
        b_r = sem("b_r"); b_y = sem("b_y"); b_gx = sem("b_gx"); b_ax = sem("b_ax")
        b_pool = sem("b_pool"); b_grp = sem("b_grp"); b_z = sem("b_z"); b_mrg = sem("b_mrg")
        g_exp = sem("g_exp")
        fin_h = sem("fin_h"); fin_t = sem("fin_t"); fin_sb = sem("fin_sb"); s_out = sem("s_out")

        with_k = lambda w: w.rearrange("l (k p) n -> p (l k) n", p=P)
        win_v, wout_v, wup_v, wdown_v = map(with_k, (w_in, w_out, w_up, w_down))
        ada_v, win2_v, ret_v, pool_v, wout2_v, ffn_v, ffo_v = map(
            with_k, (w_ada_2, w_in_2, w_ret_o_2, w_pool_o_2, w_out_2, w_ffn_in_2, w_ffn_out_2))

        block = ctx.enter_context(nc.Block())

        @block.sync
        def _(sp):
            def load(Q, j, dst, src):
                sp.wait_ge(lo_ready, Q * 4 + j + 1)
                sp.dma_start(dst, src).then_inc(landed[j], 16)

            def load_ada(l, a, slot):
                sp.wait_ge(ada_sum, l * ADA + a + 1)
                sp.dma_start(ada[:, slot], ada_v[:, ds(l * KT, KT), ds(a * 256, 256)]).then_inc(ada_landed[slot], 16)

            sp.dma_start(xtok[:], x[0].rearrange("(t p) d -> p t d", p=P)).then_inc(s_x, 16)
            sp.dma_start(con[:, 0:K_DEC], consts[:, 0:K_DEC]).then_inc(s_con, 16)
            r = 0
            for v, n in ((ln1, 16), (ln2, 16), (norm1_2, 16), (norm2_2, 16)):
                sp.dma_start(rows[r:r + n, 0, :], v.rearrange("l (k p) -> (l k) p", p=P)).then_inc(s_rows, 16)
                r += n
            sp.dma_start(rows[64:72, 0, :], final_norm_2.rearrange("(k p) -> k p", p=P)).then_inc(s_rows, 16)
            sp.dma_start(rows[72:80, 0, :], c_2[0].rearrange("(k p) -> k p", p=P)).then_inc(s_rows, 16)
            sp.dma_start(rows[80:88, 0, :], conv_b.rearrange("l (k p) -> (l k) p", p=P)).then_inc(s_rows, 16)
            sp.dma_start(rows[88:96, 0, :], pool_scale_2.rearrange("l (k p) -> (l k) p", p=P)).then_inc(s_rows, 16)
            sp.dma_start(rows[96:128, 0, :], conv_w.rearrange("l j (k p) -> (l j k) p", p=P)).then_inc(s_rows, 16)
            sp.dma_start(rows[0:96, 1, :], b_ada_2.rearrange("l (k p) -> (l k) p", p=P)).then_inc(s_rows, 16)
            sp.dma_start(rows[96:100, 1, :], mlstm_norm.rearrange("l (k h) d -> (l k) (h d)", h=2)).then_inc(s_rows, 16)
            for n, v in enumerate((moba_q_norm, moba_k_norm, swa_q_norm, swa_k_norm)):
                for half in range(2):
                    sp.dma_start(rows[100 + 2 * n:102 + 2 * n, 1, half * HD:(half + 1) * HD], v).then_inc(s_rows, 16)

            with sp.Fori(0, LAYERS) as l:
                q0 = l * A_QUADS
                with sp.Fori(0, 5) as it:
                    for j in range(4):
                        load(q0 + it, j, raw[:, j], win_v[:, ds(l * KT, KT), ds(it * 512 + j * P, P)])
                for j in range(2):
                    load(q0 + 5, j, raw[:, j], win_v[:, ds(l * KT, KT), (20 + j) * P:(21 + j) * P])
                for j in range(2):
                    load(q0 + 5, 2 + j, raw[:, 2 + j, :, 0:4],
                         win_v[:, ds(l * KT, KT), C_GATES * P + 4 * j:C_GATES * P + 4 * j + 4])
                with sp.Fori(0, A_OUT // 4) as it:
                    for j in range(4):
                        load(q0 + 6 + it, j, raw[:, j], wout_v[:, ds(l * KT, KT), ds(it * 512 + j * P, P)])
                with sp.Fori(0, A_UP // 8) as it:
                    for half in range(2):
                        for j in range(4):
                            load(q0 + 8 + it * 2 + half, j, raw[:, j],
                                 wup_v[:, ds(l * KT, KT), ds(it * 1024 + half * 512 + j * P, P)])
                        load_ada(l, it * 2 + half, half)
                with sp.Fori(0, KT // 4) as it:
                    for n in range(4):
                        for j in range(4):
                            load(q0 + 16 + it * 4 + n, j, raw[:, j],
                                 wdown_v[:, ds(l * 32 + j * KT, KT), ds(it * 512 + n * P, P)])
                        for r in range(2):
                            load_ada(l, it * 8 + 8 + 2 * n + r, r)

            with sp.Fori(0, LAYERS) as l:
                q0 = l * B_QUADS + LAYERS * A_QUADS
                for v, q, n in ((win2_v, 0, 11), (ret_v, 11, 2)):
                    with sp.Fori(0, n) as it:
                        for j in range(4):
                            load(q0 + q + it, j, raw[:, j], v[:, ds(l * KT, KT), ds(it * 512 + j * P, P)])
                for j in range(4):
                    load(q0 + 13, j, raw[:, j].rearrange("p k n -> p (k n)").rearrange("p (k n) -> p k n", k=4),
                         pool_v[:, ds(l * 4, 4), j * 256:(j + 1) * 256])
                with sp.Fori(0, 2) as it:
                    for j in range(4):
                        load(q0 + 14 + it, j, raw[:, j], wout2_v[:, ds(l * KT, KT), ds(it * 512 + j * P, P)])
                with sp.Fori(0, 11) as it:
                    for j in range(4):
                        load(q0 + 16 + it, j, raw[:, j],
                             ffn_v[:, ds(l * KT, KT), ds(it * 256 + (j // 2) * P + (j % 2) * FF2, P)])
                with sp.Fori(0, 2) as it:
                    for n in range(4):
                        for j in range(4):
                            k = FFO_PARTS[j]
                            load(q0 + 27 + it * 4 + n, j, raw[:, j, 0:k, :],
                                 ffo_v[:, ds(l * 22 + FFO_AT[j], k), ds(it * 512 + n * P, P)])

            sp.wait_ge(fin_sb, 4)
            sp.dma_start(out[0].rearrange("(t p) d -> p t d", p=P), raw[:, 0:2].rearrange("p t k n -> p t (k n)")).then_inc(s_out, 16)
            sp.wait_ge(s_out, 16)

        @block.gpsimd
        def _(pool):
            nc.gpsimd.memset(ada_acc[:, 0, 0:2], 0.0).then_inc(lo_ready, SLOTS)
            nc.gpsimd.memset(ada_acc[:, 0, 2:4], 0.0).then_inc(slab_used, SLOTS)
            nc.gpsimd.memset(ada_acc[:, 0, 6:8], 0.0).then_inc(ada_sum, 2)
            nc.gpsimd.memset(ada_acc[:, 0, 8:10], 0.0).then_inc(g_used, 2)
            with pool.Fori(0, LAYERS * (A_QUADS + B_QUADS)) as Q:
                for j in range(4):
                    pool.wait_ge(hi_ready, Q * 4 + j + 1)
                    nc.gpsimd.tensor_tensor(w_lo[:, j], raw[:, j], w_hi[:, j].bitcast(F32),
                                            ALU.subtract).then_inc(lo_ready, 1)

        @block.scalar
        def _(act):
            def split(Q, js=(0, 1, 2, 3)):
                for j in js:
                    act.wait_ge(landed[j], Q * 16 + 16)
                    act.wait_ge(slab_used, Q * 4 + j + 1)
                    nc.scalar.activation(w_hi[:, j], raw[:, j], ACT.Copy).then_inc(hi_ready, 1)

            def norm_squares(v, x0):
                for kt in range(KT):
                    act.wait_ge(acc_free, x0 + kt + 1)
                    if kt >= 4:
                        act.wait_ge(n_ss, v * KT + kt - 3)
                    nc.scalar.activation(tmp4[:, kt % 4], xT[:, kt], ACT.Square).then_inc(n_sq, 1)
                act.wait_ge(n_var, v + 1)
                rsqrt_seed(rstd[:], var[:], n_ln, n_rs, v)

            def rsqrt_seed(r, x, ln_done, done, n):
                nc.scalar.activation(r, x, ACT.Ln).then_inc(ln_done, 1)
                act.wait_ge(ln_done, n + 1)
                nc.scalar.activation(r, r, ACT.Exp, scale=-0.5).then_inc(done, 1)

            LOG_EXP = "natural_log_exp_and_others"

            act.dma_start(gate_b[:, 0:2], igate_b.rearrange("l h -> h l"), allow_slow_non_contiguous=True).then_inc(s_small, 16)
            act.dma_start(gate_b[:, 2:4], fgate_b.rearrange("l h -> h l"), allow_slow_non_contiguous=True).then_inc(s_small, 16)
            act.dma_start(sinkrow[:], swa_sinks.rearrange("l h -> (l h)").rearrange("(a n) -> a n", a=1)).then_inc(s_small, 16)
            act.dma_start(wgrp[:], w_pool_grp_2.rearrange("l g i o -> i (l g) o")).then_inc(s_grp, 16)
            act.dma_start(con[:, K_DEC:], consts[:, K_DEC:]).then_inc(s_con2, 16)
            act.wait_ge(boot_v, 1)
            nc.scalar.activation(cact[:], vecT[:, V_C:V_C + KT], ACT.Silu).then_inc(boot_a, 1)
            nc.scalar.preload_act_table_set(LOG_EXP)

            with act.Fori(0, LAYERS) as l:
                q0 = l * A_QUADS
                norm_squares(l * 2, l * A_UNITS)
                with act.Fori(0, 7) as it:
                    split(q0 + it)
                for b in range(3):
                    act.wait_ge(v_t, l * 3 + b + 1)
                    nc.scalar.activation(vtok[:, b].rearrange("p a n -> p (a n)"), mx[:, 1 + b], ACT.Copy).then_inc(v_sb, 1)
                nc.scalar.activation(proj[:, C_XO:C_XO + 2], proj[:, C_XO:C_XO + 2], ACT.Sigmoid).then_inc(ml_xo, 1)
                act.wait_ge(cv_ready, l + 1)
                nc.scalar.activation(cv[:], cv[:], ACT.Silu).then_inc(cv_silu, 1)
                nc.scalar.preload_act_table_set(LOG_EXP)
                act.wait_ge(f_abs, l + 1)
                nc.scalar.activation(g_e[:], g_a[:], ACT.Exp).then_inc(f_exp, 1)
                act.wait_ge(f_exp, l + 1)
                nc.scalar.activation(g_a[:], g_e[:], ACT.Ln, bias=1.0).then_inc(f_ln, 1)

                def head_seed(g):
                    act.wait_ge(qk_r, l * 5 + g + 1)
                    if g >= 2:
                        act.wait_ge(qk_n, l * 5 + g - 1)
                    rsqrt_seed(rr[:, g % 2], rv[:, g % 2], qk_ln, qk_s, l * 5 + g)

                for g, k in enumerate((0, 2, 4, 9, 11)):
                    if g >= 2:
                        act.wait_ge(qk_ss, l * 5 + g - 1)
                    nc.scalar.activation(sqq[:, g % 2], proj[:, k:k + 2].rearrange("p c t -> p (c t)"),
                                         ACT.Square).then_inc(qk_sq, 1)
                    if g >= 1:
                        head_seed(g - 1)
                head_seed(4)
                act.wait_ge(swp_t, l + 1)
                nc.scalar.activation(skswap[:], mx[:, 3, 0:S], ACT.Copy).then_inc(swp_sb, 1)
                act.wait_ge(f_G, l + 1)
                nc.scalar.activation(g_E[:], g_G[:], ACT.Exp, scale=-1.0).then_inc(f_E, 1)
                for n in range(2):
                    act.wait_ge(f_bc, l * 3 + n + 1)
                    nc.scalar.activation(mbc[:, 2 * n:2 * n + 2].rearrange("p h t -> p (h t)"), mx[:, 1 + n],
                                         ACT.Copy).then_inc(f_bcsb, 1)
                act.wait_ge(f_bc, l * 3 + 3)
                nc.scalar.activation(ebc, mx[:, 0], ACT.Copy).then_inc(f_bcsb, 1)
                for h in range(4):
                    act.wait_ge(ml_arg, l * 4 + h + 1)
                    if h >= 2:
                        act.wait_ge(ml_nd, l * 4 + h - 1)
                    nc.scalar.activation(mw[:, h % 2], marg[:, h % 2], ACT.Exp, scale=-1.0).then_inc(ml_w, 1)
                act.wait_ge(ml_h, l + 1)
                nc.scalar.activation(sqq[:, 0], mh, ACT.Square).then_inc(ml_sq, 1)
                act.wait_ge(ml_v, l + 1)
                rsqrt_seed(rr[:, 0], rv[:, 0], ml_ln, ml_rs, l)

                def exps(h):
                    i = h % 2
                    act.wait_ge(at_nb, l * 12 + h + 1)
                    if h >= 2:
                        act.wait_ge(at_t, l * 12 + h - 1)
                    for t, (a, b) in enumerate(((0, P), (P, 3 * P))):
                        nc.scalar.activation(pr[:, i, a:b], sm[:, i, a:b], ACT.Exp, bias=st_nb[:, i, t:t + 1],
                                             scale=HD ** -0.5, accum_out=st_den[:, i, t:t + 1])
                    if h >= 6:
                        nc.scalar.activation(st_es[:, i], st_nb[:, i], ACT.Exp,
                                             bias=lsink[:, h - 6:h - 5]).then_inc(at_e, 1)
                    else:
                        nc.scalar.activation(st_es[:, i], lsink[:, 0:2], ACT.Copy, scale=0.0).then_inc(at_e, 1)

                exps(0)
                for h in range(12):
                    if h + 1 < 12:
                        exps(h + 1)
                    act.wait_ge(at_t, l * 12 + h + 1)
                    if h >= 2:
                        act.wait_ge(at_o, l * 12 + h - 1)
                    nc.scalar.activation(pT[:, h % 2], mx[:, 2, 0:384], ACT.Copy).then_inc(at_pt, 1)
                split(q0 + 7)
                split(q0 + 8)
                norm_squares(l * 2 + 1, l * A_UNITS + A_PROJ + KT)
                with act.Fori(9, A_QUADS) as q:
                    split(q0 + q)

            with act.Fori(0, LAYERS) as l:
                q0 = l * B_QUADS + LAYERS * A_QUADS
                norm_squares(l * 2 + 4, l * B_UNITS + LAYERS * A_UNITS)
                with act.Fori(0, 12) as it:
                    split(q0 + it)
                for g in range(4):
                    act.wait_ge(b_vt, l * 4 + g + 1)
                    nc.scalar.activation(vtokb[:, g].rearrange("p a n -> p (a n)"), mx[:, 2 + g % 2], ACT.Copy).then_inc(b_vsb, 1)
                swish = projb[:, B_G:B_G + 8]
                nc.scalar.activation(swish, swish, ACT.Silu).then_inc(b_gx, 1)
                branch = projb[:, B_ARET:B_ARET + 16]
                nc.scalar.activation(branch, branch, ACT.Sigmoid).then_inc(b_ax, 1)
                nc.scalar.preload_act_table_set(LOG_EXP)
                for q in range(4):
                    act.wait_ge(b_ret, l * 4 + q + 1)
                    if q >= 1:
                        act.wait_ge(b_ss, l * 4 + q)
                    nc.scalar.activation(sqb[:], mx[:, 2], ACT.Square).then_inc(b_sq, 1)
                    act.wait_ge(b_r, l * 4 + q + 1)
                    rsqrt_seed(rb[:], bv[:], b_ln, b_rs, l * 4 + q)
                with act.Fori(12, 17) as q:
                    split(q0 + q)
                norm_squares(l * 2 + 5, l * B_UNITS + LAYERS * A_UNITS + 56 + KT)
                nc.scalar.preload_act_table(ACT.Silu)
                with act.Fori(0, 11) as it:
                    for i in range(2):
                        act.wait_ge(slab_used, (q0 + 16 + it) * 4 + 2 * i + 1 + SLOTS)
                        act.wait_ge(g_used, l * 22 + it * 2 + i + 1)
                        nc.scalar.activation(tmp4[:, i], acc[:, 2 * i, 0:S], ACT.Silu).then_inc(g_exp, 1)
                        split(q0 + 17 + it, (2 * i, 2 * i + 1))
                with act.Fori(28, B_QUADS) as q:
                    split(q0 + q)
                nc.scalar.preload_act_table_set(LOG_EXP)
            norm_squares(8, LAYERS * (A_UNITS + B_UNITS))

        @block.vector
        def _(dve):
            V = nc.vector

            def refine(c, r, x, t, last=None):
                c.link(V.tensor_tensor(t, r, r, ALU.mult))
                c.link(V.scalar_tensor_tensor(t, t, -0.5, x, ALU.mult, ALU.mult))
                c.link(V.scalar_tensor_tensor(r, t, 1.5, r, ALU.add, ALU.mult))

            def norm_rstd(c, v):
                dve.wait_ge(n_ss, v * KT + KT)
                V.tensor_scalar(var[:], mx[:, 0, 0:S], D * EPS, None, ALU.add).then_inc(n_var, 1)
                dve.wait_ge(n_rs, v + 1)
                refine(c, rstd[:], var[:], rs_tmp[:])

            def norm(v, gain, shift=None):
                c = Chain(dve, chain_n, v * 19)
                norm_rstd(c, v)
                marks = {}

                def parts(k):
                    c.wait(marks[k])
                    if shift is None:
                        m = c.done(V.tensor_copy(h_hi[:, k], hf[:, k]))
                        c.wait(m)
                        V.tensor_tensor(h_lo[:, k], hf[:, k], h_hi[:, k].bitcast(F32), ALU.subtract).then_inc(h_ready, 1)
                    else:
                        m = c.done(V.tensor_scalar(h_hi[:, k], hf[:, k], shift(k), None, ALU.add))
                        c.wait(m)
                        V.scalar_tensor_tensor(h_lo[:, k], hf[:, k], shift(k), h_hi[:, k].bitcast(F32),
                                               ALU.add, ALU.subtract).then_inc(h_ready, 1)

                for k in range(KT):
                    marks[k] = c.done(V.scalar_tensor_tensor(hf[:, k], xT[:, k], gain(k), rstd[:], ALU.mult, ALU.mult))
                    if k >= 1:
                        parts(k - 1)
                parts(KT - 1)

            def ada_products(l, a, slot, turn):
                e = l * ADA + a
                c = Chain(dve, chain_ada, e * 7)
                dve.wait_ge(ada_landed[slot], l * (ADA * 8) + turn * 16 + 16)
                c.link(V.tensor_scalar(ada_acc[:, slot], ada[:, slot, 0], cact[:, 0:1], None, ALU.mult))
                for k in range(1, KT):
                    ins = V.scalar_tensor_tensor(ada_acc[:, slot], ada[:, slot, k], cact[:, k:k + 1], ada_acc[:, slot],
                                                 ALU.mult, ALU.add)
                    if k < KT - 1:
                        c.link(ins)
                    else:
                        ins.then_inc(ada_sum, 1)

            def ada_columns(l, a, slot):
                e = l * ADA + a
                dve.wait_ge(ada_col, e + 1)
                V.tensor_tensor(modT[:, ds(e * 2, 2)], mx[:, 3, 2 * slot:2 * slot + 2],
                                vecT[:, ds(e * 2 + V_BADA, 2)], ALU.add).then_inc(ada_out, 1)

            boot = Chain(dve, boot_v, 0)
            V.memset(ones4[:], 1.0)
            for b in range(4):
                dve.wait_ge(boot_t, b + 1)
                V.tensor_copy(xT[:, 2 * b:2 * b + 2].rearrange("p k t -> p (k t)"), mx[:, b]).then_inc(acc_free, 2)
            dve.wait_ge(boot_t, 5)
            boot.link(V.tensor_copy(vecT[:], acc[:, 0, 0:VECS]))
            boot.link(V.tensor_scalar(vecT[:, 0:V_C], vecT[:, 0:V_C], float(D) ** 0.5, None, ALU.mult))
            boot.link(V.tensor_scalar(vecT[:, V_MLN:VECS], vecT[:, V_MLN:VECS], float(HD) ** 0.5, None, ALU.mult))
            dve.wait_ge(boot_t, 6)
            boot.link(V.tensor_copy(sink[:], acc[:, 1, 0:12]))
            dve.wait_ge(boot_a, 1)
            dve.wait_ge(s_small, 48)

            with dve.Fori(0, LAYERS) as l:
                c = Chain(dve, chain_a, l * CHAIN_A)
                q0 = l * A_QUADS
                for at, v, n in ((0, V_LN1, 8), (8, V_LN2, 8), (16, V_CONVB, 4), (20, V_CONVW, 16), (36, V_MLN, 2)):
                    c.done(V.tensor_copy(lv[:, at:at + n], vecT[:, ds(l * n + v, n)]))
                for n in range(4):
                    c.done(V.tensor_copy(lv[:, 38 + n:39 + n], vecT[:, ds(l + V_HN + 2 * n, 1)]))
                c.done(V.tensor_copy(lsink[:], sink[:, ds(l * 6, 6)]))
                for n in range(2):
                    c.done(V.tensor_copy(lgate[:, n:n + 1], gate_b[:, ds(l + 2 * n, 1)]))
                c.link(V.tensor_scalar(lnegsink[:], sink[:, ds(l * 6, 6)], -1.0, None, ALU.mult))
                norm(l * 2, lambda k: lv[:, k:k + 1])

                with dve.Fori(0, 5) as it:
                    for j in range(4):
                        dve.wait_ge(slab_used, (q0 + it) * 4 + j + 1 + SLOTS)
                        V.tensor_copy(proj[:, ds(it * 4 + j, 1)], acc[:, j, 0:S].unsqueeze(1)).then_inc(acc_free, 1)
                for j in range(4):
                    dve.wait_ge(slab_used, (q0 + 5) * 4 + j + 1 + SLOTS)
                    if j < 2:
                        V.tensor_copy(proj[:, 20 + j], acc[:, j, 0:S]).then_inc(acc_free, 1)
                    else:
                        V.tensor_scalar((gi, gf)[j - 2][:], acc[0:4, j, 0:S], lgate[:, j - 2:j - 1], None,
                                        ALU.add).then_inc(acc_free, 1)
                dve.wait_ge(acc_free, l * A_UNITS + A_PROJ + KT)

                V.scalar_tensor_tensor(g_a[:], gf[:], -1.0, gf[:], ALU.mult, ALU.min).then_inc(f_abs, 1)
                dve.wait_ge(f_abs, l + 1)
                marks = {}
                for j in range(4):
                    for k in range(4):
                        src = proj[:, C_XQK + k]
                        w = lambda tap: lv[:, 20 + tap * 4 + k:21 + tap * 4 + k]
                        if j == 0:
                            marks[k] = c.done(V.tensor_scalar(cv[:, k], src, w(3), lv[:, 16 + k:17 + k], ALU.mult, ALU.add))
                        else:
                            c.wait(marks[k])
                            ins = V.scalar_tensor_tensor(cv[:, k, j:], src[:, 0:S - j], w(3 - j), cv[:, k, j:],
                                                         ALU.mult, ALU.add)
                            if j < 3 or k < 3:
                                marks[k] = c.done(ins)
                            else:
                                ins.then_inc(cv_ready, 1)
                                dve.wait_ge(cv_ready, l + 1)
                groups = (0, 2, 4, 9, 11)

                def gain_of(chunk):
                    n = 0 if chunk < C_MK else 1 if chunk < C_MV else 2 if chunk < C_SK else 3
                    return lv[:, 38 + n:39 + n]

                def head_squares(g):
                    dve.wait_ge(qk_ss, l * 5 + g + 1)
                    V.tensor_scalar(rv[:, g % 2], mx[:, 0], HD * EPS, None, ALU.add).then_inc(qk_r, 1)
                    dve.wait_ge(qk_r, l * 5 + g + 1)

                def head_norm(g):
                    dve.wait_ge(qk_s, l * 5 + g + 1)
                    refine(c, rr[:, g % 2], rv[:, g % 2], r_tmp[:])
                    for i in range(2):
                        ch = groups[g] + i
                        ins = V.scalar_tensor_tensor(proj[:, ch], proj[:, ch], gain_of(ch), rr[:, g % 2, i * S:(i + 1) * S],
                                                     ALU.mult, ALU.mult)
                    ins.then_inc(qk_n, 1)
                    dve.wait_ge(qk_n, l * 5 + g + 1)

                def rope(g):
                    pair = proj[:, groups[g]:groups[g] + 2]
                    dve.wait_ge(qk_n, l * 5 + g + 1)
                    dve.wait_ge(qk_rot, l * 5 + g + 1)
                    c.done(V.tensor_tensor(rot[:].rearrange("p (c t) -> p c t", c=2),
                                           mx[:, 1 + g % 2].rearrange("p (c t) -> p c t", c=2), sin2, ALU.mult))
                    c.link(V.tensor_tensor(pair, pair, cos2, ALU.mult))
                    V.tensor_tensor(pair, pair, rot[:].rearrange("p (c t) -> p c t", c=2), ALU.add).then_inc(qk_rope, 1)
                    dve.wait_ge(qk_rope, l * 5 + g + 1)

                head_squares(0)
                for g in range(5):
                    if g + 1 < 5:
                        head_squares(g + 1)
                    head_norm(g)
                    if g >= 1:
                        rope(g - 1)
                rope(4)

                dve.wait_ge(f_ln, l + 1)
                c.link(V.scalar_tensor_tensor(gf[:], gf[:], 0.0, g_a[:], ALU.min, ALU.subtract))
                c.link(V.tensor_tensor_scan(g_F[:], ones4[:], gf[:], 0.0, ALU.mult, ALU.add))
                c.link(V.tensor_tensor(g_u[:], gi[:], g_F[:], ALU.subtract))
                V.tensor_tensor_scan(g_M[:], ones4[:], g_u[:], 0.0, ALU.mult, ALU.max).then_inc(f_M, 1)
                dve.wait_ge(f_M, l + 1)
                V.tensor_tensor(g_G[:], g_F[:], g_M[:], ALU.add).then_inc(f_G, 1)
                dve.wait_ge(f_G, l + 1)
                dve.wait_ge(f_uc, l + 1)
                V.tensor_scalar(nucol[:], mx[:, 3, 0:8], -1.0, None, ALU.mult).then_inc(f_ucsb, 1)
                dve.wait_ge(f_ucsb, l + 1)

                def arguments(h):
                    i = h % 2
                    dve.wait_ge(f_bcsb, l * 3 + h // 2 + 1)
                    if h >= 2:
                        dve.wait_ge(ml_w, l * 4 + h - 1)
                    V.scalar_tensor_tensor(marg[:, i, 0:S], mbc[:, h], nucol[:, h:h + 1], con[:, K_MT:K_MT + S],
                                           ALU.add, ALU.add)
                    V.scalar_tensor_tensor(marg[:, i, S:384], mbc[:, h, P:S], nucol[:, 4 + h:5 + h], con[:, K_MT:K_MT + P],
                                           ALU.add, ALU.add).then_inc(ml_arg, 1)
                    dve.wait_ge(ml_arg, l * 4 + h + 1)

                arguments(0)
                for h in range(4):
                    if h + 1 < 4:
                        arguments(h + 1)
                    dve.wait_ge(ml_s, l * 4 + h + 1)
                    dve.wait_ge(ml_w, l * 4 + h + 1)
                    V.scalar_tensor_tensor(mw[:, h % 2], mx[:, h % 2, 0:384], HD ** -0.5, mw[:, h % 2],
                                           ALU.mult, ALU.mult).then_inc(ml_p, 1)
                    dve.wait_ge(ml_p, l * 4 + h + 1)
                dve.wait_ge(ml_nd, l * 4 + 4)
                dve.wait_ge(f_bcsb, l * 3 + 3)
                c.link(V.scalar_tensor_tensor(r_tmp[:], mx[:, 3], -1.0, ebc, ALU.mult, ALU.max))
                c.link(V.tensor_tensor(r_tmp[:], mx[:, 3], r_tmp[:], ALU.max))
                c.link(V.reciprocal(r_tmp[:], r_tmp[:]))
                c.link(V.tensor_tensor(mh, mx[:, 2], r_tmp[:], ALU.mult))
                dve.wait_ge(ml_xo, l + 1)
                V.tensor_tensor(mh, mh, proj[:, C_XO:C_XO + 2].rearrange("p c t -> p (c t)"),
                                ALU.mult).then_inc(ml_h, 1)
                dve.wait_ge(ml_h, l + 1)
                dve.wait_ge(ml_ss, l + 1)
                V.tensor_scalar(rv[:, 0], mx[:, 0], HD * EPS, None, ALU.add).then_inc(ml_v, 1)
                dve.wait_ge(ml_v, l + 1)
                dve.wait_ge(ml_rs, l + 1)
                refine(c, rr[:, 0], rv[:, 0], r_tmp[:])
                for k in range(2):
                    c.link(V.scalar_tensor_tensor(mh[:, k * S:(k + 1) * S], mh[:, k * S:(k + 1) * S], lv[:, 36 + k:37 + k],
                                                  rr[:, 0, k * S:(k + 1) * S], ALU.mult, ALU.mult))
                mh2 = mh.rearrange("p (c t) -> p c t", c=2)
                c.link(V.tensor_copy(y_hi[:, 3:5], mh2))
                V.tensor_tensor(y_lo[:, 3:5], mh2, y_hi[:, 3:5].bitcast(F32), ALU.subtract).then_inc(ml_y, 1)
                dve.wait_ge(ml_y, l + 1)

                def maxima(h):
                    i = h % 2
                    mask = K_MCA if h < 6 else K_MSW
                    dve.wait_ge(at_s, l * 12 + h + 1)
                    if h >= 2:
                        dve.wait_ge(at_e, l * 12 + h - 1)
                    V.tensor_tensor(sm[:, i], mx[:, i, 0:384], con[:, mask:mask + 384], ALU.add).then_inc(at_m, 1)
                    dve.wait_ge(at_m, l * 12 + h + 1)
                    c.done(V.tensor_reduce(st_mx[:, i, 0:1], sm[:, i, 0:P], AX, ALU.max))
                    c.link(V.tensor_reduce(st_mx[:, i, 1:2], sm[:, i, P:384], AX, ALU.max))
                    if h >= 6:
                        ins = V.tensor_scalar(st_nb[:, i], st_mx[:, i], -HD ** -0.5, lnegsink[:, h - 6:h - 5], ALU.mult, ALU.min)
                    else:
                        ins = V.tensor_scalar(st_nb[:, i], st_mx[:, i], -HD ** -0.5, None, ALU.mult)
                    ins.then_inc(at_nb, 1)
                    dve.wait_ge(at_nb, l * 12 + h + 1)

                def probabilities(h):
                    i = h % 2
                    dve.wait_ge(at_e, l * 12 + h + 1)
                    c.link(V.tensor_tensor(st_rec[:, i], st_den[:, i], st_es[:, i], ALU.add))
                    c.link(V.reciprocal(st_rec[:, i], st_rec[:, i]))
                    V.tensor_scalar(pr[:, i, 0:P], pr[:, i, 0:P], st_rec[:, i, 0:1], None, ALU.mult)
                    V.tensor_scalar(pr[:, i, P:384], pr[:, i, P:384], st_rec[:, i, 1:2], None, ALU.mult).then_inc(at_p, 1)
                    dve.wait_ge(at_p, l * 12 + h + 1)

                def outputs(h):
                    k = h // 2 if h < 6 else 5 + (h - 6) // 2
                    b = h % 2 * HD
                    dve.wait_ge(at_o, l * 12 + h + 1)
                    o = mx[b:b + HD, 3, 0:S]
                    c.link(V.tensor_copy(y_hi[b:b + HD, k], o))
                    V.tensor_tensor(y_lo[b:b + HD, k], o, y_hi[b:b + HD, k].bitcast(F32), ALU.subtract).then_inc(at_y, 1)
                    dve.wait_ge(at_y, l * 12 + h + 1)

                maxima(0)
                maxima(1)
                for h in range(12):
                    probabilities(h)
                    if h + 2 < 12:
                        maxima(h + 2)
                    if h >= 1:
                        outputs(h - 1)
                outputs(11)
                V.memset(spare[:], 0.0).then_inc(chain_a, CHAIN_A - c.n)
                assert c.n < CHAIN_A

                u0 = l * A_UNITS + KT
                with dve.Fori(0, 2) as it:
                    for j in range(4):
                        dve.wait_ge(slab_used, (q0 + 6 + it) * 4 + j + 1 + SLOTS)
                        k = ds(it * 4 + j, 1)
                        V.tensor_tensor(xT[:, k], acc[:, j, 0:S].unsqueeze(1), xT[:, k], ALU.add).then_inc(acc_free, 1)
                norm(l * 2 + 1, lambda k: lv[:, 8 + k:9 + k])
                with dve.Fori(0, 4) as it:
                    for half in range(2):
                        a = it * 2 + half
                        ada_products(l, a, half, it)
                        for j in range(4):
                            i = j % 2
                            unit = it * 8 + half * 4 + j
                            e = Chain(dve, chain_up, (l * 32 + unit) * 2)
                            dve.wait_ge(slab_used, (q0 + 8) * 4 + unit + 1 + SLOTS)
                            V.tensor_scalar(tmp4[:, i], acc[:, j, 0:S], 0.0, None, ALU.max).then_inc(acc_free, 1)
                            dve.wait_ge(acc_free, u0 + 32 + unit + 1)
                            e.link(V.tensor_tensor(tmp4[:, 2 + i], tmp4[:, i], tmp4[:, i], ALU.mult))
                            to = ds(unit, 1)
                            e.link(V.tensor_copy(u_hi[:, to], tmp4[:, 2 + i:3 + i]))
                            V.tensor_tensor(u_lo[:, to], tmp4[:, 2 + i:3 + i], u_hi[:, to].bitcast(F32),
                                            ALU.subtract).then_inc(u_ready, 1)
                        ada_columns(l, a, half)
                with dve.Fori(0, 2) as it:
                    for n in range(4):
                        for r in range(2):
                            ada_products(l, it * 8 + 8 + 2 * n + r, r, it * 4 + 4 + n)
                            if r == 0:
                                ada_columns(l, it * 8 + 8 + 2 * n, 0)
                        k = ds(it * 4 + n, 1)
                        dve.wait_ge(slab_used, (q0 + 16 + it * 4 + n) * 4 + 4 + SLOTS)
                        V.tensor_tensor(xT[:, k], acc[:, n, 0:S].unsqueeze(1), xT[:, k], ALU.add).then_inc(acc_free, 1)
                        ada_columns(l, it * 8 + 9 + 2 * n, 1)

            dve.wait_ge(s_con2, 16)
            dve.wait_ge(s_grp, 16)
            dve.wait_ge(ada_out, LAYERS * ADA)
            with dve.Fori(0, LAYERS) as l:
                c = Chain(dve, chain_b, l * CHAIN_B)
                q0 = l * B_QUADS + LAYERS * A_QUADS
                u0 = l * B_UNITS + LAYERS * A_UNITS + KT
                dve.wait_ge(acc_free, u0)
                c.done(V.tensor_copy(lgrp[:], wgrp[:, ds(l * 4, 4)]))
                c.done(V.tensor_copy(lv[:, 0:4], vecT[:, ds(l * 4 + V_PSC, 4)]))
                c.link(V.tensor_copy(lm[:], modT[:, ds(l * MOD, MOD)]))
                c.done(V.scalar_tensor_tensor(lv[:, 8:16], lm[:, 8:16], 1.0, vecT[:, ds(l * 8 + V_N1, 8)], ALU.add, ALU.mult))
                c.link(V.scalar_tensor_tensor(lv[:, 16:24], lm[:, 32:40], 1.0, vecT[:, ds(l * 8 + V_N2, 8)], ALU.add, ALU.mult))
                norm(l * 2 + 4, lambda k: lv[:, 8 + k:9 + k], lambda k: lm[:, k:k + 1])
                with dve.Fori(0, 11) as it:
                    for j in range(4):
                        dve.wait_ge(slab_used, (q0 + it) * 4 + j + 1 + SLOTS)
                        V.tensor_copy(projb[:, ds(it * 4 + j, 1)], acc[:, j, 0:S].unsqueeze(1)).then_inc(acc_free, 1)
                dve.wait_ge(acc_free, u0 + B_PROJ)

                def rope2(g):
                    pair = projb[:, 2 * g:2 * g + 2]
                    r3 = rotb[:].rearrange("p (c t) -> p c t", c=2)
                    dve.wait_ge(b_rot, l * 4 + g + 1)
                    c.done(V.tensor_tensor(r3, mx[:, g % 2].rearrange("p (c t) -> p c t", c=2), sin2, ALU.mult))
                    c.link(V.tensor_tensor(pair, pair, cos2, ALU.mult))
                    V.tensor_tensor(pair, pair, r3, ALU.add).then_inc(b_rope, 1)
                    dve.wait_ge(b_rope, l * 4 + g + 1)

                for g in range(4):
                    rope2(g)

                def decayed(h):
                    i = h % 2
                    dec = con[:, K_DEC + h * S:K_DEC + (h + 1) * S]
                    dve.wait_ge(b_s, l * 8 + h + 1)
                    if h >= 2:
                        dve.wait_ge(b_ret, l * 4 + h // 2)
                    V.tensor_tensor(pb[:, i, 0:S], mx[:, i, 0:S], dec, ALU.mult)
                    V.tensor_tensor(pb[:, i, S:384], mx[:, i, S:384], dec[:, 0:P], ALU.mult).then_inc(b_p, 1)
                    dve.wait_ge(b_p, l * 8 + h + 1)

                for q in range(4):
                    decayed(2 * q)
                    decayed(2 * q + 1)
                    g2 = projb[:, B_G + 2 * q:B_G + 2 * q + 2].rearrange("p c t -> p (c t)")
                    dve.wait_ge(b_ss, l * 4 + q + 1)
                    V.tensor_scalar(bv[:], mx[:, 3], 1.0 / P, EPS, ALU.mult, ALU.add).then_inc(b_r, 1)
                    dve.wait_ge(b_r, l * 4 + q + 1)
                    dve.wait_ge(b_rs, l * 4 + q + 1)
                    refine(c, rb[:], bv[:], b_tmp[:])
                    c.link(V.tensor_tensor(rb[:], mx[:, 2], rb[:], ALU.mult))
                    dve.wait_ge(b_gx, l + 1)
                    c.link(V.tensor_tensor(rb[:], rb[:], g2, ALU.mult))
                    r3 = rb[:].rearrange("p (c t) -> p c t", c=2)
                    c.link(V.tensor_copy(y_hi[:, 2 * q:2 * q + 2], r3))
                    V.tensor_tensor(y_lo[:, 2 * q:2 * q + 2], r3, y_hi[:, 2 * q:2 * q + 2].bitcast(F32),
                                    ALU.subtract).then_inc(b_y, 1)
                    dve.wait_ge(b_y, l * 4 + q + 1)

                c.link(V.memset(pad[:], 0.0))
                for g in range(4):
                    src = projb[:, B_PIN + g]
                    c.link(V.tensor_copy(pad[:, 0, 16:], src))
                    for n in range(g + 1):
                        a, b = n % 2, 1 - n % 2
                        step = 1 << n
                        c.link(V.tensor_tensor(pad[:, b, 16:], pad[:, a, 16:], pad[:, a, 16 - step:16 + S - step], ALU.add))
                    sums = pad[:, (g + 1) % 2, 16:]
                    cnt = con[:, K_CNT + 16 * g:K_CNT + 16 * (g + 1)]
                    c.done(V.tensor_tensor(rb[:, 0:16], sums[:, 0:16], cnt, ALU.mult))
                    c.link(V.scalar_tensor_tensor(src[:, 16:], sums[:, 16:], 1.0 / (2 << g), src[:, 16:], ALU.mult, ALU.subtract))
                    V.tensor_tensor(src[:, 0:16], rb[:, 0:16], src[:, 0:16], ALU.subtract).then_inc(b_pool, 1)
                    dve.wait_ge(b_pool, l * 4 + g + 1)
                for g in range(4):
                    dve.wait_ge(b_grp, l * 4 + g + 1)
                    c.link(V.tensor_scalar(rb[:, 0:S], mx[:, g, 0:S], lv[:, g:g + 1], None, ALU.mult))
                    c.link(V.tensor_copy(h_hi[:, g], rb[:, 0:S]))
                    V.tensor_tensor(h_lo[:, g], rb[:, 0:S], h_hi[:, g].bitcast(F32), ALU.subtract).then_inc(b_z, 1)
                    dve.wait_ge(b_z, l * 4 + g + 1)
                V.memset(spare[:], 0.0).then_inc(chain_b, CHAIN_B - c.n)
                assert c.n < CHAIN_B

                with dve.Fori(0, 2) as it:
                    for j in range(4):
                        k = ds(it * 4 + j + B_ARET, 1)
                        dve.wait_ge(b_ax, l + 1)
                        dve.wait_ge(slab_used, (q0 + 11 + it) * 4 + j + 1 + SLOTS)
                        V.tensor_tensor(projb[:, k], acc[:, j, 0:S].unsqueeze(1), projb[:, k], ALU.mult).then_inc(acc_free, 1)
                for j in range(4):
                    e = Chain(dve, chain_pool, (l * 4 + j) * 2)
                    ap2 = projb[:, B_APOOL + 2 * j:B_APOOL + 2 * j + 2]
                    ar2 = projb[:, B_ARET + 2 * j:B_ARET + 2 * j + 2]
                    dve.wait_ge(slab_used, (q0 + 13) * 4 + j + 1 + SLOTS)
                    V.tensor_tensor(ap2, acc[:, j].rearrange("p (c t) -> p c t", c=2), ap2, ALU.mult).then_inc(acc_free, 1)
                    dve.wait_ge(acc_free, u0 + B_PROJ + B_RET + j + 1)
                    e.link(V.tensor_tensor(ap2, ap2, ar2, ALU.add))
                    e.link(V.tensor_copy(y_hi[:, 2 * j:2 * j + 2], ap2))
                    V.tensor_tensor(y_lo[:, 2 * j:2 * j + 2], ap2, y_hi[:, 2 * j:2 * j + 2].bitcast(F32),
                                    ALU.subtract).then_inc(b_mrg, 1)
                    dve.wait_ge(b_mrg, l * 4 + j + 1)
                for j in range(8):
                    dve.wait_ge(slab_used, (q0 + 14) * 4 + j + 1 + SLOTS)
                    V.scalar_tensor_tensor(xT[:, j], acc[:, j % 4, 0:S], lm[:, 16 + j:17 + j], xT[:, j], ALU.mult,
                                           ALU.add).then_inc(acc_free, 1)
                norm(l * 2 + 5, lambda k: lv[:, 16 + k:17 + k], lambda k: lm[:, 24 + k:25 + k])
                with dve.Fori(0, 11) as it:
                    for i in range(2):
                        unit = it * 2 + i
                        e = Chain(dve, chain_ffn, l * 22 + unit)
                        to = ds(unit, 1)
                        dve.wait_ge(g_exp, l * 22 + unit + 1)
                        dve.wait_ge(slab_used, (q0 + 16 + it) * 4 + 2 * i + 2 + SLOTS)
                        V.tensor_tensor(tmp4[:, 2 + i], acc[:, 2 * i + 1, 0:S], tmp4[:, i], ALU.mult).then_inc(acc_free, 2)
                        dve.wait_ge(acc_free, u0 + 64 + unit * 2 + 2)
                        e.link(V.tensor_copy(u_hi[:, to], tmp4[:, 2 + i:3 + i]))
                        V.tensor_tensor(u_lo[:, to], tmp4[:, 2 + i:3 + i], u_hi[:, to].bitcast(F32),
                                        ALU.subtract).then_inc(g_used, 1)
                for n in range(8):
                    dve.wait_ge(slab_used, (q0 + 27 + n) * 4 + 4 + SLOTS)
                    V.scalar_tensor_tensor(xT[:, n], acc[:, n % 4, 0:S], lm[:, 40 + n:41 + n], xT[:, n], ALU.mult,
                                           ALU.add).then_inc(acc_free, 1)

            norm_rstd(Chain(dve, chain_n, 8 * 19), 8)
            for k in range(KT):
                V.scalar_tensor_tensor(hf[:, k], xT[:, k], vecT[:, V_FIN + k:V_FIN + k + 1], rstd[:], ALU.mult,
                                       ALU.mult).then_inc(fin_h, 1)
            for b in range(4):
                dve.wait_ge(fin_t, b + 1)
                V.tensor_copy(raw[:, b // 2, b % 2 * 4:(b % 2 + 1) * 4].rearrange("p k n -> p (k n)"), acc[:, b]).then_inc(fin_sb, 1)

        @block.tensor
        def _(pe):
            mm = nc.tensor.matmul

            def slab(Q, j, rhs_hi, rhs_lo, outp, first=True, last=True, kts=KT, lhs=None):
                pe.wait_ge(lo_ready, Q * 4 + j + 1 + SLOTS)
                for k in range(kts):
                    wh, wl = (w_hi[:, j, k], w_lo[:, j, k]) if lhs is None else lhs(k)
                    mm(outp, wh, rhs_hi(k), start=first and k == 0, stop=False)
                    mm(outp, wh, rhs_lo(k), start=False, stop=False)
                    ins = mm(outp, wl, rhs_hi(k), start=False, stop=last and k == kts - 1)
                return ins

            def norm_sums(v):
                for kt in range(KT):
                    pe.wait_ge(n_sq, v * KT + kt + 1)
                    mm(mx[:, 0, 0:S], one, tmp4[:, kt % 4], start=kt == 0, stop=kt == KT - 1).then_inc(n_ss, 1)

            def dense(q, n, rhs, unit0, ready):
                with pe.Fori(0, n) as it:
                    pe.wait_ge(*ready)
                    for j in range(4):
                        pe.wait_ge(acc_free, unit0 + it * 4 + j + 1)
                        slab(q + it, j, lambda k: rhs[0][:, k], lambda k: rhs[1][:, k], acc[:, j, 0:S]).then_inc(slab_used, 1)

            def ada_partitions(l, a, slot):
                pe.wait_ge(ada_sum, l * ADA + a + 1 + 2)
                for half in range(2):
                    ins = mm(mx[:, 3, 2 * slot + half:2 * slot + half + 1], ada_acc[:, slot, half * P:(half + 1) * P],
                             one[:, 0:1], start=True, stop=True)
                ins.then_inc(ada_col, 1)

            pe.wait_ge(s_con, 16)
            pe.wait_ge(s_x, 16)
            for b in range(4):
                for k in range(2):
                    for t in range(2):
                        kt = 2 * b + k
                        ins = nc.tensor.transpose(mx[:, b, (2 * k + t) * P:(2 * k + t + 1) * P],
                                                  xtok[:, t, kt * P:(kt + 1) * P], ident)
                ins.then_inc(boot_t, 1)
            pe.wait_ge(s_rows, 19 * 16)
            nc.tensor.transpose(acc[:, 0, 0:P], rows[:, 0], ident)
            nc.tensor.transpose(acc[:, 0, P:VECS], rows[0:VECS - P, 1], con[0:VECS - P, K_ID:K_ID + VECS - P]).then_inc(boot_t, 1)
            pe.wait_ge(s_small, 48)
            mm(acc[:, 1, 0:12], one[0:1, :], sinkrow[:], start=True, stop=True).then_inc(boot_t, 1)
            pe.wait_ge(boot_v, 4)

            with pe.Fori(0, LAYERS) as l:
                q0 = l * A_QUADS
                u0 = l * A_UNITS + KT - SLOTS
                norm_sums(l * 2)
                dense(q0, A_PROJ // 4, (h_hi, h_lo), u0, (h_ready, l * 16 + KT))

                pe.wait_ge(acc_free, u0 + A_PROJ + SLOTS)
                for b, pair in enumerate(((C_MV, C_MV + 1), (C_MV + 2, C_SV), (C_XV, C_XV + 1))):
                    for n, ch in enumerate(pair):
                        for t in range(2):
                            ins = nc.tensor.transpose(mx[:, 1 + b, (2 * n + t) * P:(2 * n + t + 1) * P],
                                                      proj[:, ch, t * P:(t + 1) * P], ident)
                    ins.then_inc(v_t, 1)

                groups = (0, 2, 4, 9, 11)

                def sums(g):
                    pe.wait_ge(qk_sq, l * 5 + g + 1)
                    if g >= 1:
                        pe.wait_ge(qk_r, l * 5 + g)
                    mm(mx[:, 0], blk, sqq[:, g % 2], start=True, stop=True).then_inc(qk_ss, 1)

                def partners(g):
                    pe.wait_ge(qk_n, l * 5 + g + 1)
                    if g < 2:
                        pe.wait_ge(v_sb, l * 3 + g + 1)
                    else:
                        pe.wait_ge(qk_rope, l * 5 + g - 1)
                    mm(mx[:, 1 + g % 2], rotm, proj[:, groups[g]:groups[g] + 2].rearrange("p c t -> p (c t)"),
                       start=True, stop=True).then_inc(qk_rot, 1)

                sums(0)
                for g in range(5):
                    if g + 1 < 5:
                        sums(g + 1)
                    partners(g)
                pe.wait_ge(qk_rope, l * 5 + 5)
                pe.wait_ge(v_sb, l * 3 + 3)
                mm(mx[:, 3, 0:S], swpm, proj[:, C_SK], start=True, stop=True).then_inc(swp_t, 1)

                pe.wait_ge(f_M, l + 1)
                for n in range(2):
                    for i in range(2):
                        h = 2 * n + i
                        ins = mm(mx[:, 1 + n, i * S:(i + 1) * S], con[0:4, K_SEL + h * P:K_SEL + (h + 1) * P], g_M[:],
                                 start=True, stop=True)
                    ins.then_inc(f_bc, 1)
                pe.wait_ge(swp_sb, l + 1)
                for t in range(2):
                    ins = mm(mx[:, 3, 4 * t:4 * t + 4], g_u[:, t * P:(t + 1) * P], con[0:4, K_ID:K_ID + 4], start=True, stop=True)
                ins.then_inc(f_uc, 1)
                pe.wait_ge(f_E, l + 1)
                for n in range(2):
                    ins = mm(mx[:, 0, n * S:(n + 1) * S], con[0:4, K_PAIR + n * P:K_PAIR + (n + 1) * P], g_E[:],
                             start=True, stop=True)
                ins.then_inc(f_bc, 1)

                def ml_scores(h):
                    k, b = h // 2, h % 2 * HD
                    if h == 0:
                        pe.wait_ge(cv_silu, l + 1)
                        pe.wait_ge(f_bcsb, l * 3 + 3)
                    if h >= 2:
                        pe.wait_ge(ml_p, l * 4 + h - 1)
                    for a, t, n in ((0, 0, S), (S, P, P)):
                        ins = mm(mx[:, h % 2, a:a + n], cv[b:b + HD, 2 + k, t:t + P], cv[b:b + HD, k, t:t + n],
                                 start=True, stop=True)
                    ins.then_inc(ml_s, 1)

                ml_scores(0)
                for h in range(4):
                    if h + 1 < 4:
                        ml_scores(h + 1)
                    k, b = h // 2, h % 2 * HD
                    pe.wait_ge(ml_p, l * 4 + h + 1)
                    if h == 0:
                        pe.wait_ge(f_ucsb, l + 1)
                    for bank in (2, 3):
                        for t, (a, n) in enumerate(((0, S), (S, P))):
                            lhs = vtok[:, 2, 2 * k + t, b:b + HD] if bank == 2 else one[:, 0:HD]
                            ins = mm(mx[b:b + HD, bank, k * S + t * P:(k + 1) * S], lhs, mw[:, h % 2, a:a + n],
                                     start=t == 0, stop=t == 1)
                    ins.then_inc(ml_nd, 1)
                pe.wait_ge(ml_sq, l + 1)
                mm(mx[:, 0], blk, sqq[:, 0], start=True, stop=True).then_inc(ml_ss, 1)

                def at_scores(h):
                    i, b = h % 2, h % 2 * HD
                    if h == 0:
                        pe.wait_ge(ml_y, l + 1)
                    if h >= 2:
                        pe.wait_ge(at_m, l * 12 + h - 1)
                    if h < 6:
                        q, key = proj[b:b + HD, C_MQ + h // 2], proj[b:b + HD, C_MK + h // 2]
                    else:
                        g = h - 6
                        q = proj[b:b + HD, C_SQ + g // 2]
                        key = proj[b:b + HD, C_SK] if g // 3 * HD == b else skswap[b:b + HD]
                    mm(mx[:, i, 0:P], q[:, 0:P], key[:, 0:P], start=True, stop=True)
                    mm(mx[:, i, P:384], q[:, P:S], key, start=True, stop=True).then_inc(at_s, 1)

                at_scores(0)
                at_scores(1)
                for h in range(12):
                    i, b = h % 2, h % 2 * HD
                    pe.wait_ge(at_p, l * 12 + h + 1)
                    if h >= 1:
                        pe.wait_ge(at_pt, l * 12 + h)
                    for n, a in enumerate((0, P, 2 * P)):
                        ins = nc.tensor.transpose(mx[:, 2, a:a + P], pr[:, i, a:a + P], ident)
                    ins.then_inc(at_t, 1)
                    if h + 2 < 12:
                        at_scores(h + 2)
                    pe.wait_ge(at_pt, l * 12 + h + 1)
                    if h >= 2:
                        pe.wait_ge(at_y, l * 12 + h - 1)
                    if h < 6:
                        v = lambda t: vtok[:, h // 4, 2 * (h // 2 % 2) + t, b:b + HD]
                    else:
                        v = lambda t: vtok[:, 1, 2 + t, (h - 6) // 3 * HD:(h - 6) // 3 * HD + HD]
                    mm(mx[b:b + HD, 3, 0:S], v(0), pT[:, i, 0:S], start=True, stop=False)
                    mm(mx[b:b + HD, 3, P:S], v(1), pT[:, i, S:384], start=False, stop=True).then_inc(at_o, 1)

                dense(q0 + 6, 2, (y_hi, y_lo), u0 + 24, (at_y, l * 12 + 12))
                norm_sums(l * 2 + 1)
                with pe.Fori(0, 4) as it:
                    pe.wait_ge(h_ready, l * 16 + 2 * KT)
                    for half in range(2):
                        for j in range(4):
                            pe.wait_ge(acc_free, u0 + 32 + it * 8 + half * 4 + j + 1)
                            slab(q0 + 8 + it * 2 + half, j, lambda k: h_hi[:, k], lambda k: h_lo[:, k],
                                 acc[:, j, 0:S]).then_inc(slab_used, 1)
                        ada_partitions(l, it * 2 + half, half)
                with pe.Fori(0, 2) as it:
                    pe.wait_ge(u_ready, l * 32 + 32)
                    for n in range(4):
                        pe.wait_ge(acc_free, u0 + 64 + it * 4 + n + 1)
                        for j in range(4):
                            slab(q0 + 16 + it * 4 + n, j, lambda k: u_hi[:, j * KT + k], lambda k: u_lo[:, j * KT + k],
                                 acc[:, n, 0:S], j == 0, j == 3).then_inc(slab_used, 1)
                            if j % 2:
                                ada_partitions(l, it * 8 + 8 + 2 * n + j // 2, j // 2)

            with pe.Fori(0, LAYERS) as l:
                q0 = l * B_QUADS + LAYERS * A_QUADS
                u0 = l * B_UNITS + LAYERS * A_UNITS + KT - SLOTS
                norm_sums(l * 2 + 4)
                dense(q0, B_PROJ // 4, (h_hi, h_lo), u0, (h_ready, l * 16 + 32 + KT))
                pe.wait_ge(acc_free, u0 + B_PROJ + SLOTS)
                for g in range(4):
                    if g >= 2:
                        pe.wait_ge(b_rope, l * 4 + g - 1)
                        pe.wait_ge(b_vsb, l * 4 + g - 1)
                    mm(mx[:, g % 2], rotm, projb[:, 2 * g:2 * g + 2].rearrange("p c t -> p (c t)"),
                       start=True, stop=True).then_inc(b_rot, 1)
                    for n in range(2):
                        for t in range(2):
                            ins = nc.tensor.transpose(mx[:, 2 + g % 2, (2 * n + t) * P:(2 * n + t + 1) * P],
                                                      projb[:, B_V + 2 * g + n, t * P:(t + 1) * P], ident)
                    ins.then_inc(b_vt, 1)
                pe.wait_ge(b_rope, l * 4 + 4)
                pe.wait_ge(b_vsb, l * 4 + 4)

                def ret_scores(h):
                    k, b = h // 2, h % 2 * HD
                    if h >= 2:
                        pe.wait_ge(b_p, l * 8 + h - 1)
                    for a, t, n in ((0, 0, S), (S, P, P)):
                        ins = mm(mx[:, h % 2, a:a + n], projb[b:b + HD, B_K + k, t:t + P], projb[b:b + HD, B_Q + k, t:t + n],
                                 start=True, stop=True)
                    ins.then_inc(b_s, 1)

                ret_scores(0)
                ret_scores(1)
                for q in range(4):
                    if q >= 1:
                        pe.wait_ge(b_y, l * 4 + q)
                    for i in range(2):
                        h = 2 * q + i
                        pe.wait_ge(b_p, l * 8 + h + 1)
                        for t, (a, n) in enumerate(((0, S), (S, P))):
                            ins = mm(mx[:, 2, i * S + t * P:(i + 1) * S], vtokb[:, h // 2, 2 * (h % 2) + t], pb[:, i, a:a + n],
                                     start=t == 0, stop=t == 1)
                    ins.then_inc(b_ret, 1)
                    if q + 1 < 4:
                        ret_scores(2 * q + 2)
                        ret_scores(2 * q + 3)
                    pe.wait_ge(b_sq, l * 4 + q + 1)
                    mm(mx[:, 3], one, sqb[:], start=True, stop=True).then_inc(b_ss, 1)
                for g in range(4):
                    pe.wait_ge(b_pool, l * 4 + g + 1)
                    mm(mx[:, g, 0:S], lgrp[:, g], projb[:, B_PIN + g], start=True, stop=True).then_inc(b_grp, 1)
                dense(q0 + 11, 2, (y_hi, y_lo), u0 + 44, (b_y, l * 4 + 4))
                pe.wait_ge(b_z, l * 4 + 4)
                for j in range(4):
                    pe.wait_ge(acc_free, u0 + 52 + j + 1)
                    flat = [w[:, j].rearrange("p k n -> p (k n)") for w in (w_hi, w_lo)]
                    for n in range(2):
                        ins = slab(q0 + 13, j, lambda k: h_hi[:, k], lambda k: h_lo[:, k], acc[:, j, n * S:(n + 1) * S], kts=4,
                                   lhs=lambda k: [f[:, k * 256 + n * P:k * 256 + (n + 1) * P] for f in flat])
                    ins.then_inc(slab_used, 1)
                dense(q0 + 14, 2, (y_hi, y_lo), u0 + 56, (b_mrg, l * 4 + 4))
                norm_sums(l * 2 + 5)
                dense(q0 + 16, 11, (h_hi, h_lo), u0 + 64, (h_ready, l * 16 + 32 + 2 * KT))
                with pe.Fori(0, 2) as it:
                    pe.wait_ge(g_used, l * 22 + 22 + 2)
                    for n in range(4):
                        pe.wait_ge(acc_free, u0 + 108 + it * 4 + n + 1)
                        for j in range(4):
                            slab(q0 + 27 + it * 4 + n, j, lambda k: u_hi[:, FFO_AT[j] + k], lambda k: u_lo[:, FFO_AT[j] + k],
                                 acc[:, n, 0:S], j == 0, j == 3, kts=FFO_PARTS[j]).then_inc(slab_used, 1)

            norm_sums(8)
            pe.wait_ge(acc_free, LAYERS * (A_UNITS + B_UNITS) + KT)
            pe.wait_ge(fin_h, KT)
            for b in range(4):
                for n in range(4):
                    kt, t = 4 * (b % 2) + n, b // 2
                    ins = nc.tensor.transpose(acc[:, b, n * P:(n + 1) * P], hf[:, kt, t * P:(t + 1) * P], ident)
                ins.then_inc(fin_t, 1)


_INS = ["x", "ln1", "w_in", "conv_w", "conv_b", "igate_b", "fgate_b", "mlstm_norm", "moba_q_norm", "moba_k_norm",
        "swa_q_norm", "swa_k_norm", "swa_sinks", "w_out", "ln2", "w_up", "w_down", "c_2", "w_ada_2", "b_ada_2",
        "norm1_2", "w_in_2", "w_ret_o_2", "w_pool_grp_2", "pool_scale_2", "w_pool_o_2", "w_out_2", "norm2_2",
        "w_ffn_in_2", "w_ffn_out_2", "final_norm_2"]


def kernel(**inputs):
    import numpy as np
    import concourse.bacc as bacc
    from concourse.bass_utils import run_bass_kernel_spmd

    nc = bacc.Bacc("TRN2", target_bir_lowering=False, num_devices=1)
    arrays = {"consts": shape_constants()}
    for name in _INS:
        arrays["in_" + name] = np.ascontiguousarray(inputs[name])
    args = [nc.dram_tensor(n, a.shape, mybir.dt.from_np(a.dtype), kind="ExternalInput").ap() for n, a in arrays.items()]
    result = nc.dram_tensor("out_0", (1, S, D), F32, kind="ExternalOutput").ap()
    program(nc, *args, result)
    r = run_bass_kernel_spmd(nc, [arrays], core_ids=[0])
    return r.results[0]["out_0"]
```

```python
from contextlib import ExitStack

import concourse.bass as bass
from concourse import mybir

F32 = mybir.dt.float32
F32R = mybir.dt.float32r
ACT = mybir.ActivationFunctionType
ALU = mybir.AluOpType
AX = mybir.AxisListType.X
ds = bass.ds

P = 128
D = 1024
S = 256
KT = D // P
LAYERS = 2
SLOTS = 4
EPS = 1e-6
HD = 64
BIG = 1e30

A_PROJ, A_OUT, A_UP, A_DOWN = 24, 8, 32, 32
A_QUADS = (A_PROJ + A_OUT + A_UP + A_DOWN) // 4
A_UNITS = A_PROJ + A_OUT + A_UP + A_DOWN // 4
C_MQ, C_MK, C_MV, C_SQ, C_SK, C_SV, C_XQK, C_XV, C_XO, C_GATES = 0, 3, 6, 9, 12, 13, 14, 18, 20, 22
A_ORDER = (22, 22, 14, 15, 16, 17, 20, 21, 18, 19, *range(14))
W_ORDER = (3, 4, 0, 1, 2, 5, 6, 7)
QK_GROUPS = (0, 2, 4, 9, 11)
V_PAIRS = ((C_XV, C_XV + 1), (C_MV, C_MV + 1), (C_MV + 2, C_SV))
FF2 = 2816
B_PROJ, B_RET, B_POOL, B_OUT, B_FFN, B_FFO = 44, 8, 4, 8, 44, 32
B_QUADS = (B_PROJ + B_RET + B_POOL + B_OUT + B_FFN + B_FFO) // 4
B_UNITS = B_PROJ + B_RET + B_POOL + B_OUT + B_FFN + B_FFO // 4
B_Q, B_K, B_V, B_G, B_PIN, B_ARET, B_APOOL = 0, 4, 8, 16, 24, 28, 36
FFO_PARTS = (6, 6, 5, 5)
FFO_AT = (0, 6, 12, 17)
MOD = 6 * KT
ADA = MOD // 2

V_LN1, V_LN2, V_N1, V_N2, V_FIN, V_C, V_CONVB, V_PSC, V_CONVW = 0, 16, 32, 48, 64, 72, 80, 88, 96
V_BADA, V_MLN, V_HN = 128, 224, 228
VECS = 236
CHAIN_A, CHAIN_B = 256, 128
K_ID, K_ONE, K_BLK, K_ROT, K_SWP, K_COS, K_SIN = 0, 128, 256, 384, 512, 640, 896
K_MCA, K_MSW, K_MT, K_SEL, K_PAIR = 1152, 1536, 1920, 2176, 2688
K_DEC, K_CNT = 2944, 4992
NCONST = 5056


def shape_constants():
    import numpy as np

    f = np.float32
    c = np.zeros((P, NCONST), f)
    p = np.arange(P)
    t = np.arange(S)
    c[:, K_ID:K_ID + P] = np.eye(P, dtype=f)
    c[:, K_ONE:K_ONE + P] = 1.0
    c[:, K_BLK:K_BLK + P] = (p[:, None] // HD == p[None, :] // HD)
    for m in range(P):
        low = m % HD < HD // 2
        c[m + HD // 2 if low else m - HD // 2, K_ROT + m] = -1.0 if low else 1.0
        c[(m + HD) % P, K_SWP + m] = 1.0
    inv = f(10000.0) ** (-np.arange(0, HD, 2, dtype=f) / f(HD))
    ang = t.astype(f)[None, :] * inv[p % (HD // 2)][:, None]
    c[:, K_COS:K_COS + S] = np.cos(ang)
    c[:, K_SIN:K_SIN + S] = np.sin(ang)
    q1 = p[:, None] + P
    c[:, K_MCA:K_MCA + P] = np.where(p[None, :] <= p[:, None], 0.0, -BIG)
    c[:, K_MCA + P:K_MCA + 3 * P] = np.where(t[None, :] <= q1, 0.0, -BIG)
    c[:, K_MSW:K_MSW + P] = c[:, K_MCA:K_MCA + P]
    c[:, K_MSW + P:K_MSW + 3 * P] = np.where((t[None, :] <= q1) & (q1 - t[None, :] < P), 0.0, -BIG)
    c[:, K_MT:K_MT + S] = np.where(t[None, :] >= p[:, None], 0.0, BIG)
    for h in range(4):
        c[h, K_SEL + h * P:K_SEL + (h + 1) * P] = 1.0
        c[h, K_PAIR + h * HD:K_PAIR + (h + 1) * HD] = 1.0
    for h in range(8):
        g = np.log1p(-(f(2.0) ** (f(-5.0) - f(h))))
        d = (t[None, :] - p[:, None]).astype(f)
        c[:, K_DEC + h * S:K_DEC + (h + 1) * S] = np.where(d >= 0, np.exp(g * np.maximum(d, 0)), 0.0) * f(0.125)
    for g, w in enumerate((2, 4, 8, 16)):
        c[:, K_CNT + g * 16:K_CNT + (g + 1) * 16] = f(1.0) / np.minimum(t[:16] + 1, w).astype(f)
    return c


class Chain:

    def __init__(self, eng, sem, base):
        self.eng, self.sem, self.base, self.n = eng, sem, base, 0

    def done(self, ins):
        ins.then_inc(self.sem, 1)
        self.n += 1
        return self.n

    def wait(self, mark):
        self.eng.wait_ge(self.sem, self.base + mark)

    def link(self, ins):
        self.wait(self.done(ins))


def program(nc, consts, x, ln1, w_in, conv_w, conv_b, igate_b, fgate_b, mlstm_norm, moba_q_norm, moba_k_norm,
            swa_q_norm, swa_k_norm, swa_sinks, w_out, ln2, w_up, w_down, c_2, w_ada_2, b_ada_2, norm1_2, w_in_2,
            w_ret_o_2, w_pool_grp_2, pool_scale_2, w_pool_o_2, w_out_2, norm2_2, w_ffn_in_2, w_ffn_out_2,
            final_norm_2, out):
    ctx = ExitStack()
    with ctx:
        def sb(name, shape, dt=F32, stack=ctx):
            return stack.enter_context(nc.sbuf_tensor(name, shape, dt))

        def sem(name):
            return ctx.enter_context(nc.semaphore(name))

        raw = sb("raw", [P, SLOTS, KT, P])
        w_hi = sb("w_hi", [P, SLOTS, KT, P], F32R)
        w_lo = sb("w_lo", [P, SLOTS, KT, P], F32R)
        con = sb("con", [P, NCONST])
        xT = sb("xT", [P, KT, S])
        h_hi = sb("h_hi", [P, KT, S], F32R)
        h_lo = sb("h_lo", [P, KT, S], F32R)
        y_hi = sb("y_hi", [P, KT, S], F32R)
        y_lo = sb("y_lo", [P, KT, S], F32R)
        tmp4 = sb("tmp4", [P, 4, S])
        vecT = sb("vecT", [P, VECS])
        modT = sb("modT", [P, LAYERS * MOD])
        lv = sb("lv", [P, 64])
        lm = sb("lm", [P, MOD])
        gate_b = sb("gate_b", [4, 4])
        lgate = sb("lgate", [4, 2])
        ones4 = sb("ones4", [4, S])
        sinkrow = sb("sinkrow", [1, 12])
        sink = sb("sink", [P, 12])
        lsink = sb("lsink", [P, 6])
        lnegsink = sb("lnegsink", [P, 6])
        cact = sb("cact", [P, KT])
        rstd = sb("rstd", [P, S])
        var = sb("var", [P, S])
        rs_tmp = sb("rs_tmp", [P, S])
        spare = sb("spare", [P, 2])
        wgrp = sb("wgrp", [P, LAYERS * 4, P])
        with ExitStack() as first:
            ada = sb("ada", [P, 2, KT, 256], F32, first)
            ada_acc = sb("ada_acc", [P, 2, 256], F32, first)
        with ExitStack() as second:
            rotb = sb("rotb", [P, 512], F32, second)
            pb = sb("pb", [P, 2, 384], F32, second)
            sqb = sb("sqb", [P, 512], F32, second)
            rb = sb("rb", [P, 512], F32, second)
            bv = sb("bv", [P, 512], F32, second)
            b_tmp = sb("b_tmp", [P, 512], F32, second)
            pad = sb("pad", [P, 2, 16 + S], F32, second)
            lgrp = sb("lgrp", [P, 4, P], F32, second)
        sb("reserve_turns", [P, 4608])
        with ExitStack() as mlp:
            u_hi = sb("u_hi", [P, 32, S], F32R, mlp)
            u_lo = sb("u_lo", [P, 32, S], F32R, mlp)
        with ExitStack() as ends:
            xtok = sb("xtok", [P, 2, D], F32, ends)
            rows = sb("rows", [P, 2, P], F32, ends)
        with ExitStack() as norms:
            hf = sb("hf", [P, KT, S], F32, norms)
        with ExitStack() as mix_a:
            proj = sb("proj", [P, 22, S], F32, mix_a)
            gi = sb("gi", [4, S], F32, mix_a)
            gf = sb("gf", [4, S], F32, mix_a)
            g_a = sb("g_a", [4, S], F32, mix_a)
            g_e = sb("g_e", [4, S], F32, mix_a)
            g_F = sb("g_F", [4, S], F32, mix_a)
            g_u = sb("g_u", [4, S], F32, mix_a)
            g_M = sb("g_M", [4, S], F32, mix_a)
            g_G = sb("g_G", [4, S], F32, mix_a)
            g_E = sb("g_E", [4, S], F32, mix_a)
            vtok = sb("vtok", [P, 3, 4, P], F32, mix_a)
            skswap = sb("skswap", [P, S], F32, mix_a)
            rv = sb("rv", [P, 2, 512], F32, mix_a)
            rr = sb("rr", [P, 2, 512], F32, mix_a)
            r_tmp = sb("r_tmp", [P, 512], F32, mix_a)
            st_mx = sb("st_mx", [P, 2, 2], F32, mix_a)
            st_nb = sb("st_nb", [P, 2, 2], F32, mix_a)
            st_den = sb("st_den", [P, 2, 2], F32, mix_a)
            st_es = sb("st_es", [P, 2, 2], F32, mix_a)
            st_rec = sb("st_rec", [P, 2, 2], F32, mix_a)
            nucol = sb("nucol", [P, 8], F32, mix_a)
            cv = sb("cv", [P, 4, S], F32, mix_a)
            sqq = sb("sqq", [P, 2, 512], F32, mix_a)
            mbc = sb("mbc", [P, 4, S], F32, mix_a)
            marg = sb("marg", [P, 2, 384], F32, mix_a)
            mw = sb("mw", [P, 2, 384], F32, mix_a)
        with ExitStack() as mix_b:
            projb = sb("projb", [P, 44, S], F32, mix_b)
            vtokb = sb("vtokb", [P, 4, 4, P], F32, mix_b)
        sm, pr = marg, mw
        pT = sqq[:, :, 0:384]
        rot = r_tmp
        ebc, mh = rv[:, 1], rr[:, 1]

        one = con[:, K_ONE:K_ONE + P]
        ident = con[:, K_ID:K_ID + P]
        blk = con[:, K_BLK:K_BLK + P]
        rotm = con[:, K_ROT:K_ROT + P]
        swpm = con[:, K_SWP:K_SWP + P]
        cos = con[:, K_COS:K_COS + S]
        sin = con[:, K_SIN:K_SIN + S]
        cos2 = cos.unsqueeze(1).to_broadcast([P, 2, S])
        sin2 = sin.unsqueeze(1).to_broadcast([P, 2, S])

        acc = ctx.enter_context(nc.psum_tensor("acc", [P, SLOTS, 512], F32))
        mx = ctx.enter_context(nc.psum_tensor("mx", [P, 4, 512], F32))

        landed = [sem(f"landed{j}") for j in range(SLOTS)]
        hi_ready = sem("hi_ready")
        lo_ready = sem("lo_ready")
        slab_used = sem("slab_used")
        acc_free = sem("acc_free")
        ada_landed = [sem(f"ada_landed{j}") for j in range(2)]
        ada_sum = sem("ada_sum")
        ada_col = sem("ada_col")
        ada_out = sem("ada_out")
        s_con = sem("s_con")
        s_con2 = sem("s_con2")
        s_x = sem("s_x")
        s_rows = sem("s_rows")
        s_small = sem("s_small")
        s_grp = sem("s_grp")
        boot_t = sem("boot_t")
        boot_v = sem("boot_v")
        boot_a = sem("boot_a")
        g_ready = sem("g_ready")
        n_hi = sem("n_hi")
        u_hi_ready = sem("u_hi_ready")
        n_sq = sem("n_sq")
        n_var = sem("n_var"); n_ln = sem("n_ln"); n_rs = sem("n_rs")
        n_ss = sem("n_ss")
        h_ready = sem("h_ready")
        chain_n = sem("chain_n")
        chain_a = sem("chain_a")
        chain_b = sem("chain_b")
        chain_up = sem("chain_up")
        chain_ffn = sem("chain_ffn")
        chain_ret = sem("chain_ret")
        chain_pool = sem("chain_pool")
        chain_ada = sem("chain_ada")
        v_t = sem("v_t"); v_sb = sem("v_sb")
        qk_sq = sem("qk_sq"); qk_ss = sem("qk_ss"); qk_r = sem("qk_r"); qk_ln = sem("qk_ln"); qk_s = sem("qk_s"); qk_n = sem("qk_n")
        qk_rot = sem("qk_rot"); qk_rope = sem("qk_rope")
        swp_t = sem("swp_t"); swp_sb = sem("swp_sb")
        cv_ready = sem("cv_ready"); cv_silu = sem("cv_silu")
        f_abs = sem("f_abs"); f_ln = sem("f_ln"); f_M = sem("f_M"); f_G = sem("f_G"); f_E = sem("f_E")
        f_bc = sem("f_bc"); f_bcsb = sem("f_bcsb"); f_uc = sem("f_uc"); f_ucsb = sem("f_ucsb")
        f_exp = sem("f_exp"); ml_v = sem("ml_v"); ml_ln = sem("ml_ln"); ml_rs = sem("ml_rs")
        ml_s = sem("ml_s"); ml_arg = sem("ml_arg"); ml_w = sem("ml_w"); ml_p = sem("ml_p"); ml_nd = sem("ml_nd")
        ml_xo = sem("ml_xo"); ml_h = sem("ml_h"); ml_sq = sem("ml_sq"); ml_ss = sem("ml_ss"); ml_y = sem("ml_y")
        at_s = sem("at_s"); at_m = sem("at_m"); at_nb = sem("at_nb"); at_e = sem("at_e"); at_p = sem("at_p")
        at_t = sem("at_t"); at_pt = sem("at_pt"); at_o = sem("at_o"); at_y = sem("at_y")
        b_ln = sem("b_ln"); b_rs = sem("b_rs")
        g_used = sem("g_used")
        u_ready = sem("u_ready")
        b_rot = sem("b_rot"); b_rope = sem("b_rope"); b_vt = sem("b_vt"); b_vsb = sem("b_vsb")
        b_s = sem("b_s"); b_p = sem("b_p"); b_ret = sem("b_ret"); b_sq = sem("b_sq"); b_ss = sem("b_ss")
        b_r = sem("b_r"); b_y = sem("b_y"); b_gx = sem("b_gx"); b_ax = sem("b_ax")
        b_pool = sem("b_pool"); b_grp = sem("b_grp"); b_z = sem("b_z"); b_mrg = sem("b_mrg")
        g_exp = sem("g_exp")
        fin_h = sem("fin_h"); fin_t = sem("fin_t"); fin_sb = sem("fin_sb"); s_out = sem("s_out")

        with_k = lambda w: w.rearrange("l (k p) n -> p (l k) n", p=P)
        win_v, wout_v, wup_v, wdown_v = map(with_k, (w_in, w_out, w_up, w_down))
        ada_v, win2_v, ret_v, pool_v, wout2_v, ffn_v, ffo_v = map(
            with_k, (w_ada_2, w_in_2, w_ret_o_2, w_pool_o_2, w_out_2, w_ffn_in_2, w_ffn_out_2))

        block = ctx.enter_context(nc.Block())

        @block.sync
        def _(sp):
            def load(Q, j, dst, src):
                sp.wait_ge(lo_ready, Q * 4 + j + 1)
                sp.dma_start(dst, src).then_inc(landed[j], 16)

            def load_ada(l, a, slot):
                sp.wait_ge(ada_sum, l * ADA + a + 1)
                sp.dma_start(ada[:, slot], ada_v[:, ds(l * KT, KT), ds(a * 256, 256)]).then_inc(ada_landed[slot], 16)

            sp.dma_start(xtok[:], x[0].rearrange("(t p) d -> p t d", p=P)).then_inc(s_x, 16)
            sp.dma_start(con[:, 0:K_DEC], consts[:, 0:K_DEC]).then_inc(s_con, 16)
            r = 0
            for v, n in ((ln1, 16), (ln2, 16), (norm1_2, 16), (norm2_2, 16)):
                sp.dma_start(rows[r:r + n, 0, :], v.rearrange("l (k p) -> (l k) p", p=P)).then_inc(s_rows, 16)
                r += n
            sp.dma_start(rows[64:72, 0, :], final_norm_2.rearrange("(k p) -> k p", p=P)).then_inc(s_rows, 16)
            sp.dma_start(rows[72:80, 0, :], c_2[0].rearrange("(k p) -> k p", p=P)).then_inc(s_rows, 16)
            sp.dma_start(rows[80:88, 0, :], conv_b.rearrange("l (k p) -> (l k) p", p=P)).then_inc(s_rows, 16)
            sp.dma_start(rows[88:96, 0, :], pool_scale_2.rearrange("l (k p) -> (l k) p", p=P)).then_inc(s_rows, 16)
            sp.dma_start(rows[96:128, 0, :], conv_w.rearrange("l j (k p) -> (l j k) p", p=P)).then_inc(s_rows, 16)
            sp.dma_start(rows[0:96, 1, :], b_ada_2.rearrange("l (k p) -> (l k) p", p=P)).then_inc(s_rows, 16)
            sp.dma_start(rows[96:100, 1, :], mlstm_norm.rearrange("l (k h) d -> (l k) (h d)", h=2)).then_inc(s_rows, 16)
            for n, v in enumerate((moba_q_norm, moba_k_norm, swa_q_norm, swa_k_norm)):
                for half in range(2):
                    sp.dma_start(rows[100 + 2 * n:102 + 2 * n, 1, half * HD:(half + 1) * HD], v).then_inc(s_rows, 16)

            with sp.Fori(0, LAYERS) as l:
                q0 = l * A_QUADS
                for j in range(2):
                    load(q0, j, raw[:, j, :, 0:4],
                         win_v[:, ds(l * KT, KT), C_GATES * P + 4 * j:C_GATES * P + 4 * j + 4])
                for j in (2, 3):
                    load(q0, j, raw[:, j], win_v[:, ds(l * KT, KT), A_ORDER[j] * P:(A_ORDER[j] + 1) * P])
                with sp.Fori(0, 2) as it:
                    for j in range(4):
                        at, step = A_ORDER[4 + j] * P, (A_ORDER[8 + j] - A_ORDER[4 + j]) * P
                        load(q0 + 1 + it, j, raw[:, j], win_v[:, ds(l * KT, KT), ds(it * step + at, P)])
                with sp.Fori(0, 3) as it:
                    for j in range(4):
                        load(q0 + 3 + it, j, raw[:, j], win_v[:, ds(l * KT, KT), ds(it * 512 + (2 + j) * P, P)])
                with sp.Fori(0, 2) as it:
                    for j in range(4):
                        at, step = W_ORDER[j], W_ORDER[4 + j] - W_ORDER[j]
                        load(q0 + 6 + it, j, raw[:, j].rearrange("p k n -> p (k n)").unsqueeze(1),
                             wout_v[:, ds(l * KT + it * step + at, 1), :])
                with sp.Fori(0, A_UP // 8) as it:
                    for half in range(2):
                        for j in range(4):
                            load(q0 + 8 + it * 2 + half, j, raw[:, j],
                                 wup_v[:, ds(l * KT, KT), ds(it * 1024 + half * 512 + j * P, P)])
                        load_ada(l, it * 2 + half, half)
                with sp.Fori(0, KT // 4) as it:
                    for n in range(4):
                        for j in range(4):
                            load(q0 + 16 + it * 4 + n, j, raw[:, j],
                                 wdown_v[:, ds(l * 32 + j * KT, KT), ds(it * 512 + n * P, P)])
                        for r in range(2):
                            load_ada(l, it * 8 + 8 + 2 * n + r, r)

            with sp.Fori(0, LAYERS) as l:
                q0 = l * B_QUADS + LAYERS * A_QUADS
                for v, q, n in ((win2_v, 0, 11), (ret_v, 11, 2)):
                    with sp.Fori(0, n) as it:
                        for j in range(4):
                            load(q0 + q + it, j, raw[:, j], v[:, ds(l * KT, KT), ds(it * 512 + j * P, P)])
                for j in range(4):
                    load(q0 + 13, j, raw[:, j].rearrange("p k n -> p (k n)").rearrange("p (k n) -> p k n", k=4),
                         pool_v[:, ds(l * 4, 4), j * 256:(j + 1) * 256])
                with sp.Fori(0, 2) as it:
                    for j in range(4):
                        load(q0 + 14 + it, j, raw[:, j], wout2_v[:, ds(l * KT, KT), ds(it * 512 + j * P, P)])
                with sp.Fori(0, 11) as it:
                    for j in range(4):
                        load(q0 + 16 + it, j, raw[:, j],
                             ffn_v[:, ds(l * KT, KT), ds(it * 256 + (j // 2) * P + (j % 2) * FF2, P)])
                with sp.Fori(0, 2) as it:
                    for n in range(4):
                        for j in range(4):
                            k = FFO_PARTS[j]
                            load(q0 + 27 + it * 4 + n, j, raw[:, j, 0:k, :],
                                 ffo_v[:, ds(l * 22 + FFO_AT[j], k), ds(it * 512 + n * P, P)])

            sp.wait_ge(fin_sb, 4)
            sp.dma_start(out[0].rearrange("(t p) d -> p t d", p=P), raw[:, 0:2].rearrange("p t k n -> p t (k n)")).then_inc(s_out, 16)
            sp.wait_ge(s_out, 16)

        @block.gpsimd
        def _(pool):
            nc.gpsimd.memset(raw[:, 0:2], 0.0).then_inc(lo_ready, SLOTS)
            nc.gpsimd.memset(ada_acc[:, 0, 2:4], 0.0).then_inc(slab_used, SLOTS)
            nc.gpsimd.memset(ada_acc[:, 0, 6:8], 0.0).then_inc(ada_sum, 2)
            nc.gpsimd.memset(ada_acc[:, 0, 8:10], 0.0).then_inc(g_used, 2)
            with pool.Fori(0, LAYERS * (A_QUADS + B_QUADS)) as Q:
                for j in range(4):
                    pool.wait_ge(hi_ready, Q * 4 + j + 1)
                    nc.gpsimd.tensor_tensor(w_lo[:, j], raw[:, j], w_hi[:, j].bitcast(F32),
                                            ALU.subtract).then_inc(lo_ready, 1)

        @block.scalar
        def _(act):
            def split(Q, js=(0, 1, 2, 3)):
                for j in js:
                    act.wait_ge(landed[j], Q * 16 + 16)
                    act.wait_ge(slab_used, Q * 4 + j + 1)
                    nc.scalar.activation(w_hi[:, j], raw[:, j], ACT.Copy).then_inc(hi_ready, 1)

            def norm_squares(v, x0):
                for kt in range(KT):
                    act.wait_ge(acc_free, x0 + kt + 1)
                    if kt >= 4:
                        act.wait_ge(n_ss, v * KT + kt - 3)
                    nc.scalar.activation(tmp4[:, kt % 4], xT[:, kt], ACT.Square).then_inc(n_sq, 1)
                act.wait_ge(n_var, v + 1)
                rsqrt_seed(rstd[:], var[:], n_ln, n_rs, v)

            def norm_scaled(v, x0, gains, gain, early):
                def hi(kt):
                    act.wait_ge(acc_free, x0 + kt + 1)
                    if kt == 0:
                        act.wait_ge(g_ready, gains)
                    nc.scalar.activation(h_hi[:, kt], xT[:, kt], ACT.Copy, scale=gain(kt)).then_inc(n_hi, 1)

                def square(kt):
                    if kt >= 4:
                        act.wait_ge(n_ss, v * KT + kt - 3)
                    nc.scalar.activation(tmp4[:, kt % 4], xT[:, kt], ACT.Square).then_inc(n_sq, 1)

                for kt in range(4):
                    hi(kt)
                    square(kt)
                for kt in range(4, 7):
                    hi(kt)
                early()
                square(4)
                hi(7)
                for kt in range(5, KT):
                    square(kt)
                act.wait_ge(n_var, v + 1)
                rsqrt_seed(rstd[:], var[:], n_ln, n_rs, v)

            def rsqrt_seed(r, x, ln_done, done, n):
                nc.scalar.activation(r, x, ACT.Ln).then_inc(ln_done, 1)
                act.wait_ge(ln_done, n + 1)
                nc.scalar.activation(r, r, ACT.Exp, scale=-0.5).then_inc(done, 1)

            LOG_EXP = "natural_log_exp_and_others"

            act.dma_start(gate_b[:, 0:2], igate_b.rearrange("l h -> h l"), allow_slow_non_contiguous=True).then_inc(s_small, 16)
            act.dma_start(gate_b[:, 2:4], fgate_b.rearrange("l h -> h l"), allow_slow_non_contiguous=True).then_inc(s_small, 16)
            act.dma_start(sinkrow[:], swa_sinks.rearrange("l h -> (l h)").rearrange("(a n) -> a n", a=1)).then_inc(s_small, 16)
            act.dma_start(wgrp[:], w_pool_grp_2.rearrange("l g i o -> i (l g) o")).then_inc(s_grp, 16)
            act.dma_start(con[:, K_DEC:], consts[:, K_DEC:]).then_inc(s_con2, 16)
            act.wait_ge(boot_v, 1)
            nc.scalar.activation(cact[:], vecT[:, V_C:V_C + KT], ACT.Silu).then_inc(boot_a, 1)
            nc.scalar.preload_act_table_set(LOG_EXP)

            with act.Fori(0, LAYERS) as l:
                q0 = l * A_QUADS
                u0 = l * A_UNITS + KT

                def split_one(i):
                    split(q0 + i // 4, (i % 4,))

                def values(b):
                    act.wait_ge(v_t, l * 3 + b + 1)
                    nc.scalar.activation(vtok[:, b].rearrange("p a n -> p (a n)"), mx[:, 3 if b else 2], ACT.Copy).then_inc(v_sb, 1)

                def head_square(g):
                    act.wait_ge(acc_free, u0 + (12, 14, 16, 21, 23)[g])
                    if g == 0:
                        act.wait_ge(ml_ss, l + 1)
                    if g >= 2:
                        act.wait_ge(qk_ss, l * 5 + g - 1)
                    nc.scalar.activation(sqq[:, g % 2], proj[:, QK_GROUPS[g]:QK_GROUPS[g] + 2].rearrange("p c t -> p (c t)"),
                                         ACT.Square).then_inc(qk_sq, 1)

                def head_seed(g):
                    act.wait_ge(qk_r, l * 5 + g + 1)
                    if g >= 2:
                        act.wait_ge(qk_n, l * 5 + g - 1)
                    rsqrt_seed(rr[:, g % 2], rv[:, g % 2], qk_ln, qk_s, l * 5 + g)

                def weights(h):
                    act.wait_ge(ml_arg, l * 4 + h + 1)
                    if h >= 2:
                        act.wait_ge(ml_nd, l * 4 + h - 1)
                    nc.scalar.activation(mw[:, h % 2], marg[:, h % 2], ACT.Exp, scale=-1.0).then_inc(ml_w, 1)

                norm_scaled(l * 2, l * A_UNITS, l + 1, lambda k: lv[:, k:k + 1], lambda: split(q0, (0, 1, 2)))
                for i in range(3, 6):
                    split_one(i)
                act.wait_ge(f_abs, l + 1)
                nc.scalar.activation(g_e[:], g_a[:], ACT.Exp).then_inc(f_exp, 1)
                act.wait_ge(f_exp, l + 1)
                nc.scalar.activation(g_a[:], g_e[:], ACT.Ln, bias=1.0).then_inc(f_ln, 1)
                for i in (6, 7, 8):
                    split_one(i)
                act.wait_ge(f_G, l + 1)
                nc.scalar.activation(g_E[:], g_G[:], ACT.Exp, scale=-1.0).then_inc(f_E, 1)
                split_one(9)
                for n in range(2):
                    act.wait_ge(f_bc, l * 3 + n + 1)
                    nc.scalar.activation(mbc[:, 2 * n:2 * n + 2].rearrange("p h t -> p (h t)"), mx[:, 1 + n],
                                         ACT.Copy).then_inc(f_bcsb, 1)
                split_one(10)
                act.wait_ge(f_bc, l * 3 + 3)
                nc.scalar.activation(ebc, mx[:, 0], ACT.Copy).then_inc(f_bcsb, 1)
                split_one(11)
                act.wait_ge(cv_ready, l + 1)
                nc.scalar.activation(cv[:], cv[:], ACT.Silu).then_inc(cv_silu, 1)
                act.wait_ge(acc_free, u0 + 8)
                nc.scalar.activation(proj[:, C_XO:C_XO + 2], proj[:, C_XO:C_XO + 2], ACT.Sigmoid).then_inc(ml_xo, 1)
                nc.scalar.preload_act_table_set(LOG_EXP)
                weights(0)
                split_one(12)
                values(0)
                weights(1)
                split_one(13)
                split_one(14)
                weights(2)
                split_one(15)
                weights(3)
                for i in (16, 17, 18):
                    split_one(i)
                act.wait_ge(ml_h, l + 1)
                nc.scalar.activation(sqq[:, 0], mh, ACT.Square).then_inc(ml_sq, 1)
                split_one(19)
                act.wait_ge(ml_v, l + 1)
                rsqrt_seed(rr[:, 0], rv[:, 0], ml_ln, ml_rs, l)
                head_square(0)
                split_one(20)
                head_square(1)
                head_seed(0)
                split_one(21)
                head_square(2)
                head_seed(1)
                split_one(22)
                split_one(23)
                values(1)
                head_seed(2)
                split_one(24)
                head_square(3)
                split_one(25)
                head_seed(3)
                split_one(26)
                head_square(4)
                split_one(27)
                head_seed(4)
                values(2)
                act.wait_ge(swp_t, l + 1)
                nc.scalar.activation(skswap[:], mx[:, 3, 0:S], ACT.Copy).then_inc(swp_sb, 1)

                def exps(h):
                    i = h % 2
                    act.wait_ge(at_nb, l * 12 + h + 1)
                    if h >= 2:
                        act.wait_ge(at_t, l * 12 + h - 1)
                    for t, (a, b) in enumerate(((0, P), (P, 3 * P))):
                        nc.scalar.activation(pr[:, i, a:b], sm[:, i, a:b], ACT.Exp, bias=st_nb[:, i, t:t + 1],
                                             scale=HD ** -0.5, accum_out=st_den[:, i, t:t + 1])
                    if h >= 6:
                        nc.scalar.activation(st_es[:, i], st_nb[:, i], ACT.Exp,
                                             bias=lsink[:, h - 6:h - 5]).then_inc(at_e, 1)
                    else:
                        nc.scalar.activation(st_es[:, i], lsink[:, 0:2], ACT.Copy, scale=0.0).then_inc(at_e, 1)

                exps(0)
                for h in range(12):
                    if h + 1 < 12:
                        exps(h + 1)
                    act.wait_ge(at_t, l * 12 + h + 1)
                    if h >= 2:
                        act.wait_ge(at_o, l * 12 + h - 1)
                    nc.scalar.activation(pT[:, h % 2], mx[:, 2, 0:384], ACT.Copy).then_inc(at_pt, 1)
                    if h in (2, 3, 4, 6, 8, 10):
                        split_one((28, 29, 30, 31, 32, 33)[(2, 3, 4, 6, 8, 10).index(h)])
                norm_scaled(l * 2 + 1, u0 + A_PROJ, l + 1, lambda k: lv[:, 8 + k:9 + k], lambda: split_one(34))
                split_one(35)
                with act.Fori(0, 8) as it:
                    for j in range(4):
                        split(q0 + 9 + it, (j,))
                        act.wait_ge(acc_free, u0 + 32 + it * 4 + j + 1)
                        nc.scalar.activation(u_hi[:, ds(it * 4 + j, 1)], tmp4[:, j % 2].unsqueeze(1), ACT.Square).then_inc(u_hi_ready, 1)
                with act.Fori(17, A_QUADS) as q:
                    split(q0 + q)

            with act.Fori(0, LAYERS) as l:
                q0 = l * B_QUADS + LAYERS * A_QUADS
                u0 = l * B_UNITS + LAYERS * A_UNITS + KT
                norm_squares(l * 2 + 4, l * B_UNITS + LAYERS * A_UNITS)
                with act.Fori(0, 5) as it:
                    split(q0 + it)

                def split_one(i):
                    split(q0 + i // 4, (i % 4,))

                def values(g):
                    act.wait_ge(b_vt, l * 4 + g + 1)
                    nc.scalar.activation(vtokb[:, g].rearrange("p a n -> p (a n)"), mx[:, 2 + g % 2], ACT.Copy).then_inc(b_vsb, 1)

                split_one(20)
                values(0)
                values(1)
                for i in (21, 22, 23):
                    split_one(i)
                values(2)
                values(3)
                for i in (24, 25):
                    split_one(i)
                for q in range(4):
                    act.wait_ge(b_ret, l * 4 + q + 1)
                    if q >= 1:
                        act.wait_ge(b_ss, l * 4 + q)
                    nc.scalar.activation(sqb[:], mx[:, 2], ACT.Square).then_inc(b_sq, 1)
                    split_one(26 + 4 * q)
                    split_one(27 + 4 * q)
                    act.wait_ge(b_r, l * 4 + q + 1)
                    rsqrt_seed(rb[:], bv[:], b_ln, b_rs, l * 4 + q)
                    if q == 0:
                        act.wait_ge(acc_free, u0 + 24)
                        swish = projb[:, B_G:B_G + 8]
                        nc.scalar.activation(swish, swish, ACT.Silu).then_inc(b_gx, 1)
                        nc.scalar.preload_act_table_set(LOG_EXP)
                    split_one(28 + 4 * q)
                    split_one(29 + 4 * q)
                for i in range(42, 48):
                    split_one(i)
                act.wait_ge(acc_free, u0 + B_PROJ)
                branch = projb[:, B_ARET:B_ARET + 16]
                nc.scalar.activation(branch, branch, ACT.Sigmoid).then_inc(b_ax, 1)
                nc.scalar.preload_act_table_set(LOG_EXP)
                with act.Fori(12, 17) as q:
                    split(q0 + q)
                norm_squares(l * 2 + 5, l * B_UNITS + LAYERS * A_UNITS + 56 + KT)
                nc.scalar.preload_act_table(ACT.Silu)
                with act.Fori(0, 11) as it:
                    for i in range(2):
                        act.wait_ge(slab_used, (q0 + 16 + it) * 4 + 2 * i + 1 + SLOTS)
                        act.wait_ge(g_used, l * 22 + it * 2 + i + 1)
                        nc.scalar.activation(tmp4[:, i], acc[:, 2 * i, 0:S], ACT.Silu).then_inc(g_exp, 1)
                        split(q0 + 17 + it, (2 * i, 2 * i + 1))
                with act.Fori(28, B_QUADS) as q:
                    split(q0 + q)
                nc.scalar.preload_act_table_set(LOG_EXP)
            norm_squares(8, LAYERS * (A_UNITS + B_UNITS))

        @block.vector
        def _(dve):
            V = nc.vector

            def refine(c, r, x, t, wait=True):
                c.link(V.tensor_tensor(t, r, r, ALU.mult))
                c.link(V.scalar_tensor_tensor(t, t, -0.5, x, ALU.mult, ALU.mult))
                m = c.done(V.scalar_tensor_tensor(r, t, 1.5, r, ALU.add, ALU.mult))
                if wait:
                    c.wait(m)

            def norm_rstd(c, v, wait=True):
                dve.wait_ge(n_ss, v * KT + KT)
                V.tensor_scalar(var[:], mx[:, 0, 0:S], D * EPS, None, ALU.add).then_inc(n_var, 1)
                dve.wait_ge(n_rs, v + 1)
                refine(c, rstd[:], var[:], rs_tmp[:], wait)

            def norm_scaled(v, gain):
                for k in range(KT):
                    dve.wait_ge(n_hi, v * KT + k + 1)
                    V.scalar_tensor_tensor(h_lo[:, k], xT[:, k], gain(k), h_hi[:, k].bitcast(F32),
                                           ALU.mult, ALU.subtract).then_inc(h_ready, 1)
                norm_rstd(Chain(dve, chain_n, v * 3), v, wait=False)

            def norm(v, gain, shift):
                c = Chain(dve, chain_n, (v - 4) * 19 + 12)
                norm_rstd(c, v)
                marks = {}

                def parts(k):
                    c.wait(marks[k])
                    m = c.done(V.tensor_scalar(h_hi[:, k], hf[:, k], shift(k), None, ALU.add))
                    c.wait(m)
                    V.scalar_tensor_tensor(h_lo[:, k], hf[:, k], shift(k), h_hi[:, k].bitcast(F32),
                                           ALU.add, ALU.subtract).then_inc(h_ready, 1)

                for k in range(KT):
                    marks[k] = c.done(V.scalar_tensor_tensor(hf[:, k], xT[:, k], gain(k), rstd[:], ALU.mult, ALU.mult))
                    if k >= 1:
                        parts(k - 1)
                parts(KT - 1)

            def ada_products(l, a, slot, turn):
                e = l * ADA + a
                c = Chain(dve, chain_ada, e * 7)
                dve.wait_ge(ada_landed[slot], l * (ADA * 8) + turn * 16 + 16)
                c.link(V.tensor_scalar(ada_acc[:, slot], ada[:, slot, 0], cact[:, 0:1], None, ALU.mult))
                for k in range(1, KT):
                    ins = V.scalar_tensor_tensor(ada_acc[:, slot], ada[:, slot, k], cact[:, k:k + 1], ada_acc[:, slot],
                                                 ALU.mult, ALU.add)
                    if k < KT - 1:
                        c.link(ins)
                    else:
                        ins.then_inc(ada_sum, 1)

            def ada_columns(l, a, slot):
                e = l * ADA + a
                dve.wait_ge(ada_col, e + 1)
                V.tensor_tensor(modT[:, ds(e * 2, 2)], mx[:, 3, 2 * slot:2 * slot + 2],
                                vecT[:, ds(e * 2 + V_BADA, 2)], ALU.add).then_inc(ada_out, 1)

            boot = Chain(dve, boot_v, 0)
            V.memset(ones4[:], 1.0)
            for b in range(4):
                dve.wait_ge(boot_t, b + 1)
                V.tensor_copy(xT[:, 2 * b:2 * b + 2].rearrange("p k t -> p (k t)"), mx[:, b]).then_inc(acc_free, 2)
            dve.wait_ge(boot_t, 5)
            boot.link(V.tensor_copy(vecT[:], acc[:, 0, 0:VECS]))
            boot.link(V.tensor_scalar(vecT[:, 0:V_C], vecT[:, 0:V_C], float(D) ** 0.5, None, ALU.mult))
            boot.link(V.tensor_scalar(vecT[:, V_MLN:VECS], vecT[:, V_MLN:VECS], float(HD) ** 0.5, None, ALU.mult))
            dve.wait_ge(boot_t, 6)
            boot.link(V.tensor_copy(sink[:], acc[:, 1, 0:12]))
            dve.wait_ge(boot_a, 1)
            dve.wait_ge(s_small, 48)

            with dve.Fori(0, LAYERS) as l:
                c = Chain(dve, chain_a, l * CHAIN_A)
                q0 = l * A_QUADS
                c.done(V.tensor_copy(lv[:, 0:8], vecT[:, ds(l * 8 + V_LN1, 8)]))
                V.tensor_copy(lv[:, 8:16], vecT[:, ds(l * 8 + V_LN2, 8)]).then_inc(g_ready, 1)
                for at, v, n in ((16, V_CONVB, 4), (20, V_CONVW, 16), (36, V_MLN, 2)):
                    c.done(V.tensor_copy(lv[:, at:at + n], vecT[:, ds(l * n + v, n)]))
                for n in range(4):
                    c.done(V.tensor_copy(lv[:, 38 + n:39 + n], vecT[:, ds(l + V_HN + 2 * n, 1)]))
                c.done(V.tensor_copy(lsink[:], sink[:, ds(l * 6, 6)]))
                for n in range(2):
                    c.done(V.tensor_copy(lgate[:, n:n + 1], gate_b[:, ds(l + 2 * n, 1)]))
                c.link(V.tensor_scalar(lnegsink[:], sink[:, ds(l * 6, 6)], -1.0, None, ALU.mult))
                norm_scaled(l * 2, lambda k: lv[:, k:k + 1])

                u0 = l * A_UNITS + KT

                def to_sbuf(*slabs):
                    for i in slabs:
                        dve.wait_ge(slab_used, (q0 + i // 4) * 4 + i % 4 + 1 + SLOTS)
                        if i < 2:
                            V.tensor_tensor((gi, gf)[i][:], acc[0:4, i, 0:S], rstd[0:4], ALU.mult).then_inc(acc_free, 1)
                        else:
                            V.tensor_tensor(proj[:, A_ORDER[i]], acc[:, i % 4, 0:S], rstd[:], ALU.mult).then_inc(acc_free, 1)

                def convolve(j):
                    for k in range(4):
                        src = proj[:, C_XQK + k]
                        w = lambda tap: lv[:, 20 + tap * 4 + k:21 + tap * 4 + k]
                        if j == 0:
                            marks[k] = c.done(V.tensor_scalar(cv[:, k], src, w(3), lv[:, 16 + k:17 + k], ALU.mult, ALU.add))
                        else:
                            c.wait(marks[k])
                            ins = V.scalar_tensor_tensor(cv[:, k, j:], src[:, 0:S - j], w(3 - j), cv[:, k, j:],
                                                         ALU.mult, ALU.add)
                            if j < 3 or k < 3:
                                marks[k] = c.done(ins)
                            else:
                                ins.then_inc(cv_ready, 1)
                                dve.wait_ge(cv_ready, l + 1)

                groups = QK_GROUPS

                def gain_of(chunk):
                    n = 0 if chunk < C_MK else 1 if chunk < C_MV else 2 if chunk < C_SK else 3
                    return lv[:, 38 + n:39 + n]

                def head_squares(g):
                    dve.wait_ge(qk_ss, l * 5 + g + 1)
                    V.tensor_scalar(rv[:, g % 2], mx[:, 0], HD * EPS, None, ALU.add).then_inc(qk_r, 1)
                    dve.wait_ge(qk_r, l * 5 + g + 1)

                def head_norm(g):
                    dve.wait_ge(qk_s, l * 5 + g + 1)
                    refine(c, rr[:, g % 2], rv[:, g % 2], r_tmp[:])
                    for i in range(2):
                        ch = groups[g] + i
                        ins = V.scalar_tensor_tensor(proj[:, ch], proj[:, ch], gain_of(ch), rr[:, g % 2, i * S:(i + 1) * S],
                                                     ALU.mult, ALU.mult)
                    ins.then_inc(qk_n, 1)
                    dve.wait_ge(qk_n, l * 5 + g + 1)

                def rope(g):
                    pair = proj[:, groups[g]:groups[g] + 2]
                    dve.wait_ge(qk_n, l * 5 + g + 1)
                    dve.wait_ge(qk_rot, l * 5 + g + 1)
                    c.done(V.tensor_tensor(rot[:].rearrange("p (c t) -> p c t", c=2),
                                           mx[:, 1 + g % 2].rearrange("p (c t) -> p c t", c=2), sin2, ALU.mult))
                    c.link(V.tensor_tensor(pair, pair, cos2, ALU.mult))
                    V.tensor_tensor(pair, pair, rot[:].rearrange("p (c t) -> p c t", c=2), ALU.add).then_inc(qk_rope, 1)
                    dve.wait_ge(qk_rope, l * 5 + g + 1)

                def arguments(h):
                    i = h % 2
                    dve.wait_ge(f_bcsb, l * 3 + h // 2 + 1)
                    if h >= 2:
                        dve.wait_ge(ml_w, l * 4 + h - 1)
                    V.scalar_tensor_tensor(marg[:, i, 0:S], mbc[:, h], nucol[:, h:h + 1], con[:, K_MT:K_MT + S],
                                           ALU.add, ALU.add)
                    V.scalar_tensor_tensor(marg[:, i, S:384], mbc[:, h, P:S], nucol[:, 4 + h:5 + h], con[:, K_MT:K_MT + P],
                                           ALU.add, ALU.add).then_inc(ml_arg, 1)
                    dve.wait_ge(ml_arg, l * 4 + h + 1)

                def weigh(h):
                    dve.wait_ge(ml_s, l * 4 + h + 1)
                    dve.wait_ge(ml_w, l * 4 + h + 1)
                    V.scalar_tensor_tensor(mw[:, h % 2], mx[:, h % 2, 0:384], HD ** -0.5, mw[:, h % 2],
                                           ALU.mult, ALU.mult).then_inc(ml_p, 1)
                    dve.wait_ge(ml_p, l * 4 + h + 1)

                dve.wait_ge(chain_n, l * 6 + 3)
                to_sbuf(0, 1)
                dve.wait_ge(acc_free, u0 + 2)
                c.done(V.tensor_scalar(gi[:], gi[:], lgate[:, 0:1], None, ALU.add))
                c.link(V.tensor_scalar(gf[:], gf[:], lgate[:, 1:2], None, ALU.add))
                V.scalar_tensor_tensor(g_a[:], gf[:], -1.0, gf[:], ALU.mult, ALU.min).then_inc(f_abs, 1)
                dve.wait_ge(f_abs, l + 1)
                to_sbuf(2)
                dve.wait_ge(f_ln, l + 1)
                c.link(V.scalar_tensor_tensor(gf[:], gf[:], 0.0, g_a[:], ALU.min, ALU.subtract))
                c.link(V.tensor_tensor_scan(g_F[:], ones4[:], gf[:], 0.0, ALU.mult, ALU.add))
                c.link(V.tensor_tensor(g_u[:], gi[:], g_F[:], ALU.subtract))
                V.tensor_tensor_scan(g_M[:], ones4[:], g_u[:], 0.0, ALU.mult, ALU.max).then_inc(f_M, 1)
                dve.wait_ge(f_M, l + 1)
                V.tensor_tensor(g_G[:], g_F[:], g_M[:], ALU.add).then_inc(f_G, 1)
                dve.wait_ge(f_G, l + 1)
                to_sbuf(3, 4, 5)
                dve.wait_ge(acc_free, u0 + 6)
                marks = {}
                convolve(0)
                convolve(1)
                to_sbuf(6)
                convolve(2)
                to_sbuf(7)
                convolve(3)
                dve.wait_ge(f_uc, l + 1)
                V.tensor_scalar(nucol[:], mx[:, 3, 0:8], -1.0, None, ALU.mult).then_inc(f_ucsb, 1)
                dve.wait_ge(f_ucsb, l + 1)
                arguments(0)
                arguments(1)
                to_sbuf(8, 9)
                weigh(0)
                to_sbuf(10)
                arguments(2)
                weigh(1)
                to_sbuf(11)
                arguments(3)
                weigh(2)
                weigh(3)
                to_sbuf(12)
                dve.wait_ge(ml_nd, l * 4 + 4)
                dve.wait_ge(f_bcsb, l * 3 + 3)
                c.link(V.scalar_tensor_tensor(r_tmp[:], mx[:, 3], -1.0, ebc, ALU.mult, ALU.max))
                c.link(V.tensor_tensor(r_tmp[:], mx[:, 3], r_tmp[:], ALU.max))
                to_sbuf(13)
                c.link(V.reciprocal(r_tmp[:], r_tmp[:]))
                to_sbuf(14)
                c.link(V.tensor_tensor(mh, mx[:, 2], r_tmp[:], ALU.mult))
                dve.wait_ge(ml_xo, l + 1)
                V.tensor_tensor(mh, mh, proj[:, C_XO:C_XO + 2].rearrange("p c t -> p (c t)"),
                                ALU.mult).then_inc(ml_h, 1)
                dve.wait_ge(ml_h, l + 1)
                to_sbuf(15)
                dve.wait_ge(ml_ss, l + 1)
                V.tensor_scalar(rv[:, 0], mx[:, 0], HD * EPS, None, ALU.add).then_inc(ml_v, 1)
                dve.wait_ge(ml_v, l + 1)
                to_sbuf(16)
                dve.wait_ge(ml_rs, l + 1)
                refine(c, rr[:, 0], rv[:, 0], r_tmp[:])
                for k in range(2):
                    c.link(V.scalar_tensor_tensor(mh[:, k * S:(k + 1) * S], mh[:, k * S:(k + 1) * S], lv[:, 36 + k:37 + k],
                                                  rr[:, 0, k * S:(k + 1) * S], ALU.mult, ALU.mult))
                mh2 = mh.rearrange("p (c t) -> p c t", c=2)
                c.link(V.tensor_copy(y_hi[:, 3:5], mh2))
                V.tensor_tensor(y_lo[:, 3:5], mh2, y_hi[:, 3:5].bitcast(F32), ALU.subtract).then_inc(ml_y, 1)
                dve.wait_ge(ml_y, l + 1)
                head_squares(0)
                to_sbuf(17)
                head_squares(1)
                head_norm(0)
                to_sbuf(18, 19)
                head_squares(2)
                head_norm(1)
                rope(0)
                to_sbuf(20, 21)
                head_squares(3)
                head_norm(2)
                rope(1)
                to_sbuf(22, 23)
                head_squares(4)
                head_norm(3)
                rope(2)
                head_norm(4)
                rope(3)
                rope(4)

                def maxima(h):
                    i = h % 2
                    mask = K_MCA if h < 6 else K_MSW
                    dve.wait_ge(at_s, l * 12 + h + 1)
                    if h >= 2:
                        dve.wait_ge(at_e, l * 12 + h - 1)
                    V.tensor_tensor(sm[:, i], mx[:, i, 0:384], con[:, mask:mask + 384], ALU.add).then_inc(at_m, 1)
                    dve.wait_ge(at_m, l * 12 + h + 1)
                    c.done(V.tensor_reduce(st_mx[:, i, 0:1], sm[:, i, 0:P], AX, ALU.max))
                    c.link(V.tensor_reduce(st_mx[:, i, 1:2], sm[:, i, P:384], AX, ALU.max))
                    if h >= 6:
                        ins = V.tensor_scalar(st_nb[:, i], st_mx[:, i], -HD ** -0.5, lnegsink[:, h - 6:h - 5], ALU.mult, ALU.min)
                    else:
                        ins = V.tensor_scalar(st_nb[:, i], st_mx[:, i], -HD ** -0.5, None, ALU.mult)
                    ins.then_inc(at_nb, 1)
                    dve.wait_ge(at_nb, l * 12 + h + 1)

                def probabilities(h):
                    i = h % 2
                    dve.wait_ge(at_e, l * 12 + h + 1)
                    c.link(V.tensor_tensor(st_rec[:, i], st_den[:, i], st_es[:, i], ALU.add))
                    c.link(V.reciprocal(st_rec[:, i], st_rec[:, i]))
                    V.tensor_scalar(pr[:, i, 0:P], pr[:, i, 0:P], st_rec[:, i, 0:1], None, ALU.mult)
                    V.tensor_scalar(pr[:, i, P:384], pr[:, i, P:384], st_rec[:, i, 1:2], None, ALU.mult).then_inc(at_p, 1)
                    dve.wait_ge(at_p, l * 12 + h + 1)

                def outputs(h):
                    k = h // 2 if h < 6 else 5 + (h - 6) // 2
                    b = h % 2 * HD
                    dve.wait_ge(at_o, l * 12 + h + 1)
                    o = mx[b:b + HD, 3, 0:S]
                    c.link(V.tensor_copy(y_hi[b:b + HD, k], o))
                    V.tensor_tensor(y_lo[b:b + HD, k], o, y_hi[b:b + HD, k].bitcast(F32), ALU.subtract).then_inc(at_y, 1)
                    dve.wait_ge(at_y, l * 12 + h + 1)

                maxima(0)
                maxima(1)
                for h in range(12):
                    probabilities(h)
                    if h + 2 < 12:
                        maxima(h + 2)
                    if h >= 1:
                        outputs(h - 1)
                outputs(11)
                V.memset(spare[:], 0.0).then_inc(chain_a, CHAIN_A - c.n)
                assert c.n < CHAIN_A

                dve.wait_ge(slab_used, (q0 + 7) * 4 + 4 + SLOTS)
                for k in range(KT):
                    V.tensor_tensor(xT[:, k], acc[:, k // 2, k % 2 * S:(k % 2 + 1) * S], xT[:, k], ALU.add).then_inc(acc_free, 1)
                norm_scaled(l * 2 + 1, lambda k: lv[:, 8 + k:9 + k])
                with dve.Fori(0, 4) as it:
                    for half in range(2):
                        a = it * 2 + half

                        def low(j):
                            unit = it * 8 + half * 4 + j
                            dve.wait_ge(u_hi_ready, l * 32 + unit + 1)
                            dve.wait_ge(chain_up, l * 32 + unit + 1)
                            V.tensor_tensor(u_lo[:, ds(unit, 1)], tmp4[:, 2 + j % 2:3 + j % 2], u_hi[:, ds(unit, 1)].bitcast(F32),
                                            ALU.subtract).then_inc(u_ready, 1)

                        ada_products(l, a, half, it)
                        for j in range(4):
                            i = j % 2
                            unit = it * 8 + half * 4 + j
                            dve.wait_ge(slab_used, (q0 + 8) * 4 + unit + 1 + SLOTS)
                            if j == 0:
                                dve.wait_ge(chain_n, l * 6 + 6)
                            V.scalar_tensor_tensor(tmp4[:, i], acc[:, j, 0:S], 0.0, rstd[:], ALU.max, ALU.mult).then_inc(acc_free, 1)
                            if j >= 1:
                                low(j - 1)
                            dve.wait_ge(acc_free, u0 + 32 + unit + 1)
                            V.tensor_tensor(tmp4[:, 2 + i], tmp4[:, i], tmp4[:, i], ALU.mult).then_inc(chain_up, 1)
                        low(3)
                        ada_columns(l, a, half)
                with dve.Fori(0, 2) as it:
                    for n in range(4):
                        for r in range(2):
                            ada_products(l, it * 8 + 8 + 2 * n + r, r, it * 4 + 4 + n)
                            if r == 0:
                                ada_columns(l, it * 8 + 8 + 2 * n, 0)
                        k = ds(it * 4 + n, 1)
                        dve.wait_ge(slab_used, (q0 + 16 + it * 4 + n) * 4 + 4 + SLOTS)
                        V.tensor_tensor(xT[:, k], acc[:, n, 0:S].unsqueeze(1), xT[:, k], ALU.add).then_inc(acc_free, 1)
                        ada_columns(l, it * 8 + 9 + 2 * n, 1)

            dve.wait_ge(s_con2, 16)
            dve.wait_ge(s_grp, 16)
            dve.wait_ge(ada_out, LAYERS * ADA)
            with dve.Fori(0, LAYERS) as l:
                c = Chain(dve, chain_b, l * CHAIN_B)
                q0 = l * B_QUADS + LAYERS * A_QUADS
                u0 = l * B_UNITS + LAYERS * A_UNITS + KT
                dve.wait_ge(acc_free, u0)
                c.done(V.tensor_copy(lgrp[:], wgrp[:, ds(l * 4, 4)]))
                c.done(V.tensor_copy(lv[:, 0:4], vecT[:, ds(l * 4 + V_PSC, 4)]))
                c.link(V.tensor_copy(lm[:], modT[:, ds(l * MOD, MOD)]))
                c.done(V.scalar_tensor_tensor(lv[:, 8:16], lm[:, 8:16], 1.0, vecT[:, ds(l * 8 + V_N1, 8)], ALU.add, ALU.mult))
                c.link(V.scalar_tensor_tensor(lv[:, 16:24], lm[:, 32:40], 1.0, vecT[:, ds(l * 8 + V_N2, 8)], ALU.add, ALU.mult))
                norm(l * 2 + 4, lambda k: lv[:, 8 + k:9 + k], lambda k: lm[:, k:k + 1])
                with dve.Fori(0, 4) as it:
                    for j in range(4):
                        dve.wait_ge(slab_used, (q0 + it) * 4 + j + 1 + SLOTS)
                        V.tensor_copy(projb[:, ds(it * 4 + j, 1)], acc[:, j, 0:S].unsqueeze(1)).then_inc(acc_free, 1)

                def to_sbuf(*chunks):
                    for i in chunks:
                        dve.wait_ge(slab_used, (q0 + i // 4) * 4 + i % 4 + 1 + SLOTS)
                        V.tensor_copy(projb[:, i], acc[:, i % 4, 0:S]).then_inc(acc_free, 1)

                dve.wait_ge(acc_free, u0 + 16)
                def rope2(g):
                    pair = projb[:, 2 * g:2 * g + 2]
                    r3 = rotb[:].rearrange("p (c t) -> p c t", c=2)
                    dve.wait_ge(b_rot, l * 4 + g + 1)
                    c.done(V.tensor_tensor(r3, mx[:, g % 2].rearrange("p (c t) -> p c t", c=2), sin2, ALU.mult))
                    c.link(V.tensor_tensor(pair, pair, cos2, ALU.mult))
                    V.tensor_tensor(pair, pair, r3, ALU.add).then_inc(b_rope, 1)
                    dve.wait_ge(b_rope, l * 4 + g + 1)

                def decayed(h):
                    i = h % 2
                    dec = con[:, K_DEC + h * S:K_DEC + (h + 1) * S]
                    dve.wait_ge(b_s, l * 8 + h + 1)
                    if h >= 2:
                        dve.wait_ge(b_ret, l * 4 + h // 2)
                    V.tensor_tensor(pb[:, i, 0:S], mx[:, i, 0:S], dec, ALU.mult)
                    V.tensor_tensor(pb[:, i, S:384], mx[:, i, S:384], dec[:, 0:P], ALU.mult).then_inc(b_p, 1)
                    dve.wait_ge(b_p, l * 8 + h + 1)

                def mean_squares(q):
                    dve.wait_ge(b_ss, l * 4 + q + 1)
                    V.tensor_scalar(bv[:], mx[:, 3], 1.0 / P, EPS, ALU.mult, ALU.add).then_inc(b_r, 1)
                    dve.wait_ge(b_r, l * 4 + q + 1)

                def gated(q):
                    g2 = projb[:, B_G + 2 * q:B_G + 2 * q + 2].rearrange("p c t -> p (c t)")
                    dve.wait_ge(b_rs, l * 4 + q + 1)
                    refine(c, rb[:], bv[:], b_tmp[:])
                    c.link(V.tensor_tensor(rb[:], mx[:, 2], rb[:], ALU.mult))
                    dve.wait_ge(b_gx, l + 1)
                    c.link(V.tensor_tensor(rb[:], rb[:], g2, ALU.mult))
                    r3 = rb[:].rearrange("p (c t) -> p c t", c=2)
                    c.link(V.tensor_copy(y_hi[:, 2 * q:2 * q + 2], r3))
                    V.tensor_tensor(y_lo[:, 2 * q:2 * q + 2], r3, y_hi[:, 2 * q:2 * q + 2].bitcast(F32),
                                    ALU.subtract).then_inc(b_y, 1)
                    dve.wait_ge(b_y, l * 4 + q + 1)

                def pooled(g):
                    src = projb[:, B_PIN + g]
                    c.link(V.tensor_copy(pad[:, 0, 16:], src))
                    for n in range(g + 1):
                        a, b = n % 2, 1 - n % 2
                        step = 1 << n
                        c.link(V.tensor_tensor(pad[:, b, 16:], pad[:, a, 16:], pad[:, a, 16 - step:16 + S - step], ALU.add))
                    sums = pad[:, (g + 1) % 2, 16:]
                    cnt = con[:, K_CNT + 16 * g:K_CNT + 16 * (g + 1)]
                    c.done(V.tensor_tensor(b_tmp[:, 0:16], sums[:, 0:16], cnt, ALU.mult))
                    c.link(V.scalar_tensor_tensor(src[:, 16:], sums[:, 16:], 1.0 / (2 << g), src[:, 16:], ALU.mult, ALU.subtract))
                    V.tensor_tensor(src[:, 0:16], b_tmp[:, 0:16], src[:, 0:16], ALU.subtract).then_inc(b_pool, 1)
                    dve.wait_ge(b_pool, l * 4 + g + 1)

                c.link(V.memset(pad[:], 0.0))
                rope2(0)
                rope2(1)
                to_sbuf(16)
                rope2(2)
                to_sbuf(17)
                rope2(3)
                to_sbuf(18)
                decayed(0)
                decayed(1)
                to_sbuf(19, 20)
                for q in range(4):
                    mean_squares(q)
                    to_sbuf(21 + 4 * q, 22 + 4 * q)
                    if q + 1 < 4:
                        decayed(2 * q + 2)
                        decayed(2 * q + 3)
                    to_sbuf(23 + 4 * q)
                    gated(q)
                    to_sbuf(24 + 4 * q)
                    if q >= 2:
                        if q == 2:
                            dve.wait_ge(acc_free, u0 + B_PIN + 4)
                        pooled(2 * q - 4)
                        pooled(2 * q - 3)
                to_sbuf(*range(37, 44))
                for g in range(4):
                    dve.wait_ge(b_grp, l * 4 + g + 1)
                    c.link(V.tensor_scalar(rb[:, 0:S], mx[:, g, 0:S], lv[:, g:g + 1], None, ALU.mult))
                    c.link(V.tensor_copy(h_hi[:, g], rb[:, 0:S]))
                    V.tensor_tensor(h_lo[:, g], rb[:, 0:S], h_hi[:, g].bitcast(F32), ALU.subtract).then_inc(b_z, 1)
                    dve.wait_ge(b_z, l * 4 + g + 1)
                V.memset(spare[:], 0.0).then_inc(chain_b, CHAIN_B - c.n)
                assert c.n < CHAIN_B

                with dve.Fori(0, 2) as it:
                    for j in range(4):
                        k = ds(it * 4 + j + B_ARET, 1)
                        dve.wait_ge(b_ax, l + 1)
                        dve.wait_ge(slab_used, (q0 + 11 + it) * 4 + j + 1 + SLOTS)
                        V.tensor_tensor(projb[:, k], acc[:, j, 0:S].unsqueeze(1), projb[:, k], ALU.mult).then_inc(acc_free, 1)
                for j in range(4):
                    e = Chain(dve, chain_pool, (l * 4 + j) * 2)
                    ap2 = projb[:, B_APOOL + 2 * j:B_APOOL + 2 * j + 2]
                    ar2 = projb[:, B_ARET + 2 * j:B_ARET + 2 * j + 2]
                    dve.wait_ge(slab_used, (q0 + 13) * 4 + j + 1 + SLOTS)
                    V.tensor_tensor(ap2, acc[:, j].rearrange("p (c t) -> p c t", c=2), ap2, ALU.mult).then_inc(acc_free, 1)
                    dve.wait_ge(acc_free, u0 + B_PROJ + B_RET + j + 1)
                    e.link(V.tensor_tensor(ap2, ap2, ar2, ALU.add))
                    e.link(V.tensor_copy(y_hi[:, 2 * j:2 * j + 2], ap2))
                    V.tensor_tensor(y_lo[:, 2 * j:2 * j + 2], ap2, y_hi[:, 2 * j:2 * j + 2].bitcast(F32),
                                    ALU.subtract).then_inc(b_mrg, 1)
                    dve.wait_ge(b_mrg, l * 4 + j + 1)
                for j in range(8):
                    dve.wait_ge(slab_used, (q0 + 14) * 4 + j + 1 + SLOTS)
                    V.scalar_tensor_tensor(xT[:, j], acc[:, j % 4, 0:S], lm[:, 16 + j:17 + j], xT[:, j], ALU.mult,
                                           ALU.add).then_inc(acc_free, 1)
                norm(l * 2 + 5, lambda k: lv[:, 16 + k:17 + k], lambda k: lm[:, 24 + k:25 + k])
                with dve.Fori(0, 11) as it:
                    for i in range(2):
                        unit = it * 2 + i
                        e = Chain(dve, chain_ffn, l * 22 + unit)
                        to = ds(unit, 1)
                        dve.wait_ge(g_exp, l * 22 + unit + 1)
                        dve.wait_ge(slab_used, (q0 + 16 + it) * 4 + 2 * i + 2 + SLOTS)
                        V.tensor_tensor(tmp4[:, 2 + i], acc[:, 2 * i + 1, 0:S], tmp4[:, i], ALU.mult).then_inc(acc_free, 2)
                        dve.wait_ge(acc_free, u0 + 64 + unit * 2 + 2)
                        e.link(V.tensor_copy(u_hi[:, to], tmp4[:, 2 + i:3 + i]))
                        V.tensor_tensor(u_lo[:, to], tmp4[:, 2 + i:3 + i], u_hi[:, to].bitcast(F32),
                                        ALU.subtract).then_inc(g_used, 1)
                for n in range(8):
                    dve.wait_ge(slab_used, (q0 + 27 + n) * 4 + 4 + SLOTS)
                    V.scalar_tensor_tensor(xT[:, n], acc[:, n % 4, 0:S], lm[:, 40 + n:41 + n], xT[:, n], ALU.mult,
                                           ALU.add).then_inc(acc_free, 1)

            norm_rstd(Chain(dve, chain_n, 12 + 4 * 19), 8)
            for k in range(KT):
                V.scalar_tensor_tensor(hf[:, k], xT[:, k], vecT[:, V_FIN + k:V_FIN + k + 1], rstd[:], ALU.mult,
                                       ALU.mult).then_inc(fin_h, 1)
            for b in range(4):
                dve.wait_ge(fin_t, b + 1)
                V.tensor_copy(raw[:, b // 2, b % 2 * 4:(b % 2 + 1) * 4].rearrange("p k n -> p (k n)"), acc[:, b]).then_inc(fin_sb, 1)

        @block.tensor
        def _(pe):
            mm = nc.tensor.matmul

            def slab(Q, j, rhs_hi, rhs_lo, outp, first=True, last=True, kts=KT, lhs=None, before=None):
                pe.wait_ge(lo_ready, Q * 4 + j + 1 + SLOTS)
                for k in range(kts):
                    if before:
                        before(k)
                    wh, wl = (w_hi[:, j, k], w_lo[:, j, k]) if lhs is None else lhs(k)
                    mm(outp, wh, rhs_hi(k), start=first and k == 0, stop=False)
                    mm(outp, wh, rhs_lo(k), start=False, stop=False)
                    ins = mm(outp, wl, rhs_hi(k), start=False, stop=last and k == kts - 1)
                return ins

            def norm_sums(v):
                for kt in range(KT):
                    pe.wait_ge(n_sq, v * KT + kt + 1)
                    mm(mx[:, 0, 0:S], one, tmp4[:, kt % 4], start=kt == 0, stop=kt == KT - 1).then_inc(n_ss, 1)

            def dense(q, n, rhs, unit0, ready):
                with pe.Fori(0, n) as it:
                    pe.wait_ge(*ready)
                    for j in range(4):
                        pe.wait_ge(acc_free, unit0 + it * 4 + j + 1)
                        slab(q + it, j, lambda k: rhs[0][:, k], lambda k: rhs[1][:, k], acc[:, j, 0:S]).then_inc(slab_used, 1)

            def ada_partitions(l, a, slot):
                pe.wait_ge(ada_sum, l * ADA + a + 1 + 2)
                for half in range(2):
                    ins = mm(mx[:, 3, 2 * slot + half:2 * slot + half + 1], ada_acc[:, slot, half * P:(half + 1) * P],
                             one[:, 0:1], start=True, stop=True)
                ins.then_inc(ada_col, 1)

            pe.wait_ge(s_con, 16)
            pe.wait_ge(s_x, 16)
            for b in range(4):
                for k in range(2):
                    for t in range(2):
                        kt = 2 * b + k
                        ins = nc.tensor.transpose(mx[:, b, (2 * k + t) * P:(2 * k + t + 1) * P],
                                                  xtok[:, t, kt * P:(kt + 1) * P], ident)
                ins.then_inc(boot_t, 1)
            pe.wait_ge(s_rows, 19 * 16)
            nc.tensor.transpose(acc[:, 0, 0:P], rows[:, 0], ident)
            nc.tensor.transpose(acc[:, 0, P:VECS], rows[0:VECS - P, 1], con[0:VECS - P, K_ID:K_ID + VECS - P]).then_inc(boot_t, 1)
            pe.wait_ge(s_small, 48)
            mm(acc[:, 1, 0:12], one[0:1, :], sinkrow[:], start=True, stop=True).then_inc(boot_t, 1)
            pe.wait_ge(boot_v, 4)

            with pe.Fori(0, LAYERS) as l:
                q0 = l * A_QUADS
                u0 = l * A_UNITS + KT - SLOTS
                norm_sums(l * 2)
                def project(*slabs):
                    for i in slabs:
                        pe.wait_ge(acc_free, u0 + i + 1)
                        slab(q0 + i // 4, i % 4, lambda k: h_hi[:, k], lambda k: h_lo[:, k], acc[:, i % 4, 0:S],
                             before=(lambda k: pe.wait_ge(h_ready, l * 16 + k + 1)) if i == 0 else None).then_inc(slab_used, 1)

                def values(b):
                    pe.wait_ge(acc_free, u0 + SLOTS + (10, 18, 24)[b])
                    if b == 0:
                        pe.wait_ge(f_bcsb, l * 3 + 2)
                    if b == 1:
                        pe.wait_ge(ml_y, l + 1)
                    if b == 2:
                        pe.wait_ge(v_sb, l * 3 + 2)
                    for n, ch in enumerate(V_PAIRS[b]):
                        for t in range(2):
                            ins = nc.tensor.transpose(mx[:, 3 if b else 2, (2 * n + t) * P:(2 * n + t + 1) * P],
                                                      proj[:, ch, t * P:(t + 1) * P], ident)
                    ins.then_inc(v_t, 1)

                groups = QK_GROUPS

                def sums(g):
                    pe.wait_ge(qk_sq, l * 5 + g + 1)
                    if g >= 1:
                        pe.wait_ge(qk_r, l * 5 + g)
                    else:
                        pe.wait_ge(ml_v, l + 1)
                    mm(mx[:, 0], blk, sqq[:, g % 2], start=True, stop=True).then_inc(qk_ss, 1)

                def partners(g):
                    pe.wait_ge(qk_n, l * 5 + g + 1)
                    if g >= 2:
                        pe.wait_ge(qk_rope, l * 5 + g - 1)
                    mm(mx[:, 1 + g % 2], rotm, proj[:, groups[g]:groups[g] + 2].rearrange("p c t -> p (c t)"),
                       start=True, stop=True).then_inc(qk_rot, 1)

                def ml_scores(h):
                    k, b = h // 2, h % 2 * HD
                    if h == 0:
                        pe.wait_ge(cv_silu, l + 1)
                        pe.wait_ge(f_bcsb, l * 3 + 3)
                    if h >= 2:
                        pe.wait_ge(ml_p, l * 4 + h - 1)
                    for a, t, n in ((0, 0, S), (S, P, P)):
                        ins = mm(mx[:, h % 2, a:a + n], cv[b:b + HD, 2 + k, t:t + P], cv[b:b + HD, k, t:t + n],
                                 start=True, stop=True)
                    ins.then_inc(ml_s, 1)

                def ml_outputs(h):
                    k, b = h // 2, h % 2 * HD
                    pe.wait_ge(ml_p, l * 4 + h + 1)
                    if h == 0:
                        pe.wait_ge(f_ucsb, l + 1)
                        pe.wait_ge(v_sb, l * 3 + 1)
                    for bank in (2, 3):
                        for t, (a, n) in enumerate(((0, S), (S, P))):
                            lhs = vtok[:, 0, 2 * k + t, b:b + HD] if bank == 2 else one[:, 0:HD]
                            ins = mm(mx[b:b + HD, bank, k * S + t * P:(k + 1) * S], lhs, mw[:, h % 2, a:a + n],
                                     start=t == 0, stop=t == 1)
                    ins.then_inc(ml_nd, 1)

                project(0, 1, 2, 3, 4, 5)
                pe.wait_ge(f_M, l + 1)
                for n in range(2):
                    for i in range(2):
                        h = 2 * n + i
                        ins = mm(mx[:, 1 + n, i * S:(i + 1) * S], con[0:4, K_SEL + h * P:K_SEL + (h + 1) * P], g_M[:],
                                 start=True, stop=True)
                    ins.then_inc(f_bc, 1)
                project(6)
                for t in range(2):
                    ins = mm(mx[:, 3, 4 * t:4 * t + 4], g_u[:, t * P:(t + 1) * P], con[0:4, K_ID:K_ID + 4], start=True, stop=True)
                ins.then_inc(f_uc, 1)
                pe.wait_ge(f_E, l + 1)
                for n in range(2):
                    ins = mm(mx[:, 0, n * S:(n + 1) * S], con[0:4, K_PAIR + n * P:K_PAIR + (n + 1) * P], g_E[:],
                             start=True, stop=True)
                ins.then_inc(f_bc, 1)
                project(7, 8)
                ml_scores(0)
                project(9)
                ml_scores(1)
                values(0)
                project(10)
                ml_outputs(0)
                project(11)
                ml_scores(2)
                ml_outputs(1)
                ml_scores(3)
                project(12)
                ml_outputs(2)
                ml_outputs(3)
                project(13, 14, 15)
                pe.wait_ge(ml_sq, l + 1)
                mm(mx[:, 0], blk, sqq[:, 0], start=True, stop=True).then_inc(ml_ss, 1)
                project(16)
                sums(0)
                project(17)
                sums(1)
                project(18)
                partners(0)
                project(19)
                values(1)
                sums(2)
                project(20)
                partners(1)
                project(21)
                sums(3)
                project(22)
                partners(2)
                project(23)
                sums(4)
                partners(3)
                values(2)
                partners(4)
                pe.wait_ge(qk_rope, l * 5 + 5)
                pe.wait_ge(v_sb, l * 3 + 3)
                mm(mx[:, 3, 0:S], swpm, proj[:, C_SK], start=True, stop=True).then_inc(swp_t, 1)

                def out_slab(w):
                    k = W_ORDER[w]
                    pe.wait_ge(lo_ready, (q0 + 6) * 4 + w + 1 + SLOTS)
                    if w == 0:
                        pe.wait_ge(ml_y, l + 1)
                        pe.wait_ge(acc_free, u0 + A_PROJ + SLOTS)
                    if w >= 2:
                        pe.wait_ge(at_y, l * 12 + 2 * (w - 1))
                    for n in range(KT):
                        o = acc[:, n // 2, n % 2 * S:(n % 2 + 1) * S]
                        mm(o, w_hi[:, w % 4, n], y_hi[:, k], start=w == 0 and n % 2 == 0, stop=False)
                        mm(o, w_hi[:, w % 4, n], y_lo[:, k], start=False, stop=False)
                        ins = mm(o, w_lo[:, w % 4, n], y_hi[:, k], start=False, stop=w == KT - 1 and n % 2 == 1)
                    ins.then_inc(slab_used, 1)

                def at_scores(h):
                    i, b = h % 2, h % 2 * HD
                    if h == 6:
                        pe.wait_ge(swp_sb, l + 1)
                    if h >= 2:
                        pe.wait_ge(at_m, l * 12 + h - 1)
                    if h < 6:
                        q, key = proj[b:b + HD, C_MQ + h // 2], proj[b:b + HD, C_MK + h // 2]
                    else:
                        g = h - 6
                        q = proj[b:b + HD, C_SQ + g // 2]
                        key = proj[b:b + HD, C_SK] if g // 3 * HD == b else skswap[b:b + HD]
                    mm(mx[:, i, 0:P], q[:, 0:P], key[:, 0:P], start=True, stop=True)
                    mm(mx[:, i, P:384], q[:, P:S], key, start=True, stop=True).then_inc(at_s, 1)

                at_scores(0)
                at_scores(1)
                out_slab(0)
                for h in range(12):
                    i, b = h % 2, h % 2 * HD
                    if h + 2 < 12:
                        at_scores(h + 2)
                    pe.wait_ge(at_p, l * 12 + h + 1)
                    if h >= 1:
                        pe.wait_ge(at_pt, l * 12 + h)
                    else:
                        pe.wait_ge(swp_sb, l + 1)
                    for n, a in enumerate((0, P, 2 * P)):
                        ins = nc.tensor.transpose(mx[:, 2, a:a + P], pr[:, i, a:a + P], ident)
                    ins.then_inc(at_t, 1)
                    if h % 2:
                        out_slab((h + 1) // 2)
                    pe.wait_ge(at_pt, l * 12 + h + 1)
                    if h >= 2:
                        pe.wait_ge(at_y, l * 12 + h - 1)
                    if h < 6:
                        v = lambda t: vtok[:, 1 + h // 4, 2 * (h // 2 % 2) + t, b:b + HD]
                    else:
                        v = lambda t: vtok[:, 2, 2 + t, (h - 6) // 3 * HD:(h - 6) // 3 * HD + HD]
                    mm(mx[b:b + HD, 3, 0:S], v(0), pT[:, i, 0:S], start=True, stop=False)
                    mm(mx[b:b + HD, 3, P:S], v(1), pT[:, i, S:384], start=False, stop=True).then_inc(at_o, 1)

                out_slab(7)
                norm_sums(l * 2 + 1)
                with pe.Fori(0, 4) as it:
                    pe.wait_ge(h_ready, l * 16 + 2 * KT)
                    for half in range(2):
                        for j in range(4):
                            pe.wait_ge(acc_free, u0 + 32 + it * 8 + half * 4 + j + 1)
                            slab(q0 + 8 + it * 2 + half, j, lambda k: h_hi[:, k], lambda k: h_lo[:, k],
                                 acc[:, j, 0:S]).then_inc(slab_used, 1)
                        ada_partitions(l, it * 2 + half, half)
                with pe.Fori(0, 2) as it:
                    pe.wait_ge(u_ready, l * 32 + 32)
                    for n in range(4):
                        pe.wait_ge(acc_free, u0 + 64 + it * 4 + n + 1)
                        for j in range(4):
                            slab(q0 + 16 + it * 4 + n, j, lambda k: u_hi[:, j * KT + k], lambda k: u_lo[:, j * KT + k],
                                 acc[:, n, 0:S], j == 0, j == 3).then_inc(slab_used, 1)
                            if j % 2:
                                ada_partitions(l, it * 8 + 8 + 2 * n + j // 2, j // 2)

            with pe.Fori(0, LAYERS) as l:
                q0 = l * B_QUADS + LAYERS * A_QUADS
                u0 = l * B_UNITS + LAYERS * A_UNITS + KT - SLOTS
                norm_sums(l * 2 + 4)
                dense(q0, 4, (h_hi, h_lo), u0, (h_ready, l * 16 + 32 + KT))

                def project(*chunks):
                    for i in chunks:
                        pe.wait_ge(acc_free, u0 + i + 1)
                        slab(q0 + i // 4, i % 4, lambda k: h_hi[:, k], lambda k: h_lo[:, k], acc[:, i % 4, 0:S]).then_inc(slab_used, 1)

                def partners2(g):
                    if g >= 2:
                        pe.wait_ge(b_rope, l * 4 + g - 1)
                    mm(mx[:, g % 2], rotm, projb[:, 2 * g:2 * g + 2].rearrange("p c t -> p (c t)"),
                       start=True, stop=True).then_inc(b_rot, 1)

                def values2(g):
                    if g >= 2:
                        pe.wait_ge(b_vsb, l * 4 + g - 1)
                    for n in range(2):
                        for t in range(2):
                            ins = nc.tensor.transpose(mx[:, 2 + g % 2, (2 * n + t) * P:(2 * n + t + 1) * P],
                                                      projb[:, B_V + 2 * g + n, t * P:(t + 1) * P], ident)
                    ins.then_inc(b_vt, 1)

                def ret_scores(h):
                    k, b = h // 2, h % 2 * HD
                    if h >= 2:
                        pe.wait_ge(b_p, l * 8 + h - 1)
                    for a, t, n in ((0, 0, S), (S, P, P)):
                        ins = mm(mx[:, h % 2, a:a + n], projb[b:b + HD, B_K + k, t:t + P], projb[b:b + HD, B_Q + k, t:t + n],
                                 start=True, stop=True)
                    ins.then_inc(b_s, 1)

                def ret_outputs(q):
                    if q >= 1:
                        pe.wait_ge(b_y, l * 4 + q)
                    for i in range(2):
                        h = 2 * q + i
                        pe.wait_ge(b_p, l * 8 + h + 1)
                        for t, (a, n) in enumerate(((0, S), (S, P))):
                            ins = mm(mx[:, 2, i * S + t * P:(i + 1) * S], vtokb[:, h // 2, 2 * (h % 2) + t], pb[:, i, a:a + n],
                                     start=t == 0, stop=t == 1)
                    ins.then_inc(b_ret, 1)

                def grouped(g):
                    pe.wait_ge(b_pool, l * 4 + g + 1)
                    mm(mx[:, g, 0:S], lgrp[:, g], projb[:, B_PIN + g], start=True, stop=True).then_inc(b_grp, 1)

                pe.wait_ge(acc_free, u0 + SLOTS + 8)
                partners2(0)
                partners2(1)
                project(16)
                pe.wait_ge(acc_free, u0 + SLOTS + 16)
                values2(0)
                values2(1)
                project(17)
                partners2(2)
                project(18)
                partners2(3)
                project(19)
                values2(2)
                values2(3)
                project(20)
                pe.wait_ge(b_rope, l * 4 + 4)
                ret_scores(0)
                ret_scores(1)
                project(21, 22)
                pe.wait_ge(b_vsb, l * 4 + 4)
                for q in range(4):
                    ret_outputs(q)
                    project(23 + 4 * q)
                    if q + 1 < 4:
                        ret_scores(2 * q + 2)
                        ret_scores(2 * q + 3)
                    pe.wait_ge(b_sq, l * 4 + q + 1)
                    mm(mx[:, 3], one, sqb[:], start=True, stop=True).then_inc(b_ss, 1)
                    project(24 + 4 * q, 25 + 4 * q, 26 + 4 * q)
                project(39, 40)
                grouped(0)
                grouped(1)
                project(41, 42)
                grouped(2)
                grouped(3)
                project(43)
                dense(q0 + 11, 2, (y_hi, y_lo), u0 + 44, (b_y, l * 4 + 4))
                pe.wait_ge(b_z, l * 4 + 4)
                for j in range(4):
                    pe.wait_ge(acc_free, u0 + 52 + j + 1)
                    flat = [w[:, j].rearrange("p k n -> p (k n)") for w in (w_hi, w_lo)]
                    for n in range(2):
                        ins = slab(q0 + 13, j, lambda k: h_hi[:, k], lambda k: h_lo[:, k], acc[:, j, n * S:(n + 1) * S], kts=4,
                                   lhs=lambda k: [f[:, k * 256 + n * P:k * 256 + (n + 1) * P] for f in flat])
                    ins.then_inc(slab_used, 1)
                dense(q0 + 14, 2, (y_hi, y_lo), u0 + 56, (b_mrg, l * 4 + 4))
                norm_sums(l * 2 + 5)
                dense(q0 + 16, 11, (h_hi, h_lo), u0 + 64, (h_ready, l * 16 + 32 + 2 * KT))
                with pe.Fori(0, 2) as it:
                    pe.wait_ge(g_used, l * 22 + 22 + 2)
                    for n in range(4):
                        pe.wait_ge(acc_free, u0 + 108 + it * 4 + n + 1)
                        for j in range(4):
                            slab(q0 + 27 + it * 4 + n, j, lambda k: u_hi[:, FFO_AT[j] + k], lambda k: u_lo[:, FFO_AT[j] + k],
                                 acc[:, n, 0:S], j == 0, j == 3, kts=FFO_PARTS[j]).then_inc(slab_used, 1)

            norm_sums(8)
            pe.wait_ge(acc_free, LAYERS * (A_UNITS + B_UNITS) + KT)
            pe.wait_ge(fin_h, KT)
            for b in range(4):
                for n in range(4):
                    kt, t = 4 * (b % 2) + n, b // 2
                    ins = nc.tensor.transpose(acc[:, b, n * P:(n + 1) * P], hf[:, kt, t * P:(t + 1) * P], ident)
                ins.then_inc(fin_t, 1)


_INS = ["x", "ln1", "w_in", "conv_w", "conv_b", "igate_b", "fgate_b", "mlstm_norm", "moba_q_norm", "moba_k_norm",
        "swa_q_norm", "swa_k_norm", "swa_sinks", "w_out", "ln2", "w_up", "w_down", "c_2", "w_ada_2", "b_ada_2",
        "norm1_2", "w_in_2", "w_ret_o_2", "w_pool_grp_2", "pool_scale_2", "w_pool_o_2", "w_out_2", "norm2_2",
        "w_ffn_in_2", "w_ffn_out_2", "final_norm_2"]


def kernel(**inputs):
    import numpy as np
    import concourse.bacc as bacc
    from concourse.bass_utils import run_bass_kernel_spmd

    nc = bacc.Bacc("TRN2", target_bir_lowering=False, num_devices=1)
    arrays = {"consts": shape_constants()}
    for name in _INS:
        arrays["in_" + name] = np.ascontiguousarray(inputs[name])
    args = [nc.dram_tensor(n, a.shape, mybir.dt.from_np(a.dtype), kind="ExternalInput").ap() for n, a in arrays.items()]
    result = nc.dram_tensor("out_0", (1, S, D), F32, kind="ExternalOutput").ap()
    program(nc, *args, result)
    r = run_bass_kernel_spmd(nc, [arrays], core_ids=[0])
    return r.results[0]["out_0"]
```

```python
from contextlib import ExitStack

import concourse.bass as bass
from concourse import mybir

F32 = mybir.dt.float32
F32R = mybir.dt.float32r
ACT = mybir.ActivationFunctionType
ALU = mybir.AluOpType
AX = mybir.AxisListType.X
ds = bass.ds

P = 128
D = 1024
S = 256
KT = D // P
LAYERS = 2
SLOTS = 4
EPS = 1e-6
HD = 64
BIG = 1e30

A_PROJ, A_OUT, A_UP, A_DOWN = 24, 8, 32, 32
A_QUADS = (A_PROJ + A_OUT + A_UP + A_DOWN) // 4
A_UNITS = A_PROJ + A_OUT + A_UP + A_DOWN // 4
C_MQ, C_MK, C_MV, C_SQ, C_SK, C_SV, C_XQK, C_XV, C_XO, C_GATES = 0, 3, 6, 9, 12, 13, 14, 18, 20, 22
A_ORDER = (22, 22, 14, 15, 16, 17, 20, 21, 18, 19, *range(14))
W_ORDER = (3, 4, 0, 1, 2, 5, 6, 7)
QK_GROUPS = (0, 2, 4, 9, 11)
V_PAIRS = ((C_XV, C_XV + 1), (C_MV, C_MV + 1), (C_MV + 2, C_SV))
FF2 = 2816
B_PROJ, B_RET, B_POOL, B_OUT, B_FFN, B_FFO = 44, 8, 4, 8, 44, 32
B_QUADS = (B_PROJ + B_RET + B_POOL + B_OUT + B_FFN + B_FFO) // 4
B_UNITS = B_PROJ + B_RET + B_POOL + B_OUT + B_FFN + B_FFO // 4
B_Q, B_K, B_V, B_G, B_PIN, B_ARET, B_APOOL = 0, 4, 8, 16, 24, 28, 36
FFO_PARTS = (6, 6, 5, 5)
FFO_AT = (0, 6, 12, 17)
MOD = 6 * KT
ADA = MOD // 2

V_LN1, V_LN2, V_N1, V_N2, V_FIN, V_C, V_CONVB, V_PSC, V_CONVW = 0, 16, 32, 48, 64, 72, 80, 88, 96
V_BADA, V_MLN, V_HN = 128, 224, 228
VECS = 236
CHAIN_A, CHAIN_B = 256, 128
K_ID, K_ONE, K_BLK, K_ROT, K_SWP, K_COS, K_SIN = 0, 128, 256, 384, 512, 640, 896
K_MCA, K_MSW, K_MT, K_SEL, K_PAIR = 1152, 1536, 1920, 2176, 2688
K_DEC, K_CNT = 2944, 4992
NCONST = 5056


def shape_constants():
    import numpy as np

    f = np.float32
    c = np.zeros((P, NCONST), f)
    p = np.arange(P)
    t = np.arange(S)
    c[:, K_ID:K_ID + P] = np.eye(P, dtype=f)
    c[:, K_ONE:K_ONE + P] = 1.0
    c[:, K_BLK:K_BLK + P] = (p[:, None] // HD == p[None, :] // HD)
    for m in range(P):
        low = m % HD < HD // 2
        c[m + HD // 2 if low else m - HD // 2, K_ROT + m] = -1.0 if low else 1.0
        c[(m + HD) % P, K_SWP + m] = 1.0
    inv = f(10000.0) ** (-np.arange(0, HD, 2, dtype=f) / f(HD))
    ang = t.astype(f)[None, :] * inv[p % (HD // 2)][:, None]
    c[:, K_COS:K_COS + S] = np.cos(ang)
    c[:, K_SIN:K_SIN + S] = np.sin(ang)
    q1 = p[:, None] + P
    c[:, K_MCA:K_MCA + P] = np.where(p[None, :] <= p[:, None], 0.0, -BIG)
    c[:, K_MCA + P:K_MCA + 3 * P] = np.where(t[None, :] <= q1, 0.0, -BIG)
    c[:, K_MSW:K_MSW + P] = c[:, K_MCA:K_MCA + P]
    c[:, K_MSW + P:K_MSW + 3 * P] = np.where((t[None, :] <= q1) & (q1 - t[None, :] < P), 0.0, -BIG)
    c[:, K_MT:K_MT + S] = np.where(t[None, :] >= p[:, None], 0.0, BIG)
    for h in range(4):
        c[h, K_SEL + h * P:K_SEL + (h + 1) * P] = 1.0
        c[h, K_PAIR + h * HD:K_PAIR + (h + 1) * HD] = 1.0
    for h in range(8):
        g = np.log1p(-(f(2.0) ** (f(-5.0) - f(h))))
        d = (t[None, :] - p[:, None]).astype(f)
        c[:, K_DEC + h * S:K_DEC + (h + 1) * S] = np.where(d >= 0, np.exp(g * np.maximum(d, 0)), 0.0) * f(0.125)
    for g, w in enumerate((2, 4, 8, 16)):
        c[:, K_CNT + g * 16:K_CNT + (g + 1) * 16] = f(1.0) / np.minimum(t[:16] + 1, w).astype(f)
    return c


class Chain:

    def __init__(self, eng, sem, base):
        self.eng, self.sem, self.base, self.n = eng, sem, base, 0

    def done(self, ins):
        ins.then_inc(self.sem, 1)
        self.n += 1
        return self.n

    def wait(self, mark):
        self.eng.wait_ge(self.sem, self.base + mark)

    def link(self, ins):
        self.wait(self.done(ins))


def program(nc, consts, x, ln1, w_in, conv_w, conv_b, igate_b, fgate_b, mlstm_norm, moba_q_norm, moba_k_norm,
            swa_q_norm, swa_k_norm, swa_sinks, w_out, ln2, w_up, w_down, c_2, w_ada_2, b_ada_2, norm1_2, w_in_2,
            w_ret_o_2, w_pool_grp_2, pool_scale_2, w_pool_o_2, w_out_2, norm2_2, w_ffn_in_2, w_ffn_out_2,
            final_norm_2, out):
    ctx = ExitStack()
    with ctx:
        def sb(name, shape, dt=F32, stack=ctx):
            return stack.enter_context(nc.sbuf_tensor(name, shape, dt))

        def sem(name):
            return ctx.enter_context(nc.semaphore(name))

        raw = sb("raw", [P, SLOTS, KT, P])
        w_hi = sb("w_hi", [P, SLOTS, KT, P], F32R)
        w_lo = sb("w_lo", [P, SLOTS, KT, P], F32R)
        con = sb("con", [P, NCONST])
        xT = sb("xT", [P, KT, S])
        h_hi = sb("h_hi", [P, KT, S + 2], F32R)
        h_lo = sb("h_lo", [P, KT, S + 2], F32R)
        y_hi = sb("y_hi", [P, KT, S], F32R)
        y_lo = sb("y_lo", [P, KT, S], F32R)
        tmp4 = sb("tmp4", [P, 4, S])
        vecT = sb("vecT", [P, VECS])
        modT = sb("modT", [P, (LAYERS + 1) * MOD])
        shift_w = sb("shift_w", [P, SLOTS])
        nx_a = sb("nx_a", [P, KT])
        nx = sb("nx", [P, 2 * KT])
        lv = sb("lv", [P, 64])
        lm = sb("lm", [P, MOD])
        gate_b = sb("gate_b", [4, 4])
        lgate = sb("lgate", [4, 2])
        ones4 = sb("ones4", [4, S])
        sinkrow = sb("sinkrow", [1, 12])
        sink = sb("sink", [P, 12])
        lsink = sb("lsink", [P, 6])
        lnegsink = sb("lnegsink", [P, 6])
        cact = sb("cact", [P, KT])
        head_eps = sb("head_eps", [P, 1])
        rstd = sb("rstd", [P, S])
        var = sb("var", [P, S])
        rs_tmp = sb("rs_tmp", [P, S])
        ssq = sb("ssq", [P, S])
        spare = sb("spare", [P, 2])
        wgrp = sb("wgrp", [P, LAYERS * 4, P])
        with ExitStack() as first:
            ada = sb("ada", [P, 2, KT, 256], F32, first)
            ada_acc = sb("ada_acc", [P, 2, 256], F32, first)
        with ExitStack() as second:
            rotb = sb("rotb", [P, 512], F32, second)
            pb = sb("pb", [P, 2, 384], F32, second)
            sqb = sb("sqb", [P, 512], F32, second)
            rb = sb("rb", [P, 512], F32, second)
            bv = sb("bv", [P, 512], F32, second)
            b_tmp = sb("b_tmp", [P, 512], F32, second)
            pad = sb("pad", [P, 2, 16 + S], F32, second)
            lgrp = sb("lgrp", [P, 4, P], F32, second)
        with ExitStack() as third:
            hf = sb("hf", [P, KT, S], F32, third)
        sb("reserve_turns", [P, 4608])
        with ExitStack() as mlp:
            u_hi = sb("u_hi", [P, 32, S], F32R, mlp)
            u_lo = sb("u_lo", [P, 32, S], F32R, mlp)
        with ExitStack() as ends:
            xtok = sb("xtok", [P, 2, D], F32, ends)
            rows = sb("rows", [P, 2, P], F32, ends)
        with ExitStack() as mix_a:
            proj = sb("proj", [P, 22, S], F32, mix_a)
            gi = sb("gi", [4, S], F32, mix_a)
            gf = sb("gf", [4, S], F32, mix_a)
            g_a = sb("g_a", [4, S], F32, mix_a)
            g_e = sb("g_e", [4, S], F32, mix_a)
            g_F = sb("g_F", [4, S], F32, mix_a)
            g_u = sb("g_u", [4, S], F32, mix_a)
            g_M = sb("g_M", [4, S], F32, mix_a)
            g_G = sb("g_G", [4, S], F32, mix_a)
            g_E = sb("g_E", [4, S], F32, mix_a)
            vtok = sb("vtok", [P, 3, 4, P], F32, mix_a)
            skswap = sb("skswap", [P, S], F32, mix_a)
            rv = sb("rv", [P, 2, 512], F32, mix_a)
            rr = sb("rr", [P, 2, 512], F32, mix_a)
            r_tmp = sb("r_tmp", [P, 512], F32, mix_a)
            st_mx = sb("st_mx", [P, 2, 2], F32, mix_a)
            st_nb = sb("st_nb", [P, 2, 2], F32, mix_a)
            st_den = sb("st_den", [P, 2, 2], F32, mix_a)
            st_es = sb("st_es", [P, 2, 2], F32, mix_a)
            st_rec = sb("st_rec", [P, 2, 2], F32, mix_a)
            nucol = sb("nucol", [P, 8], F32, mix_a)
            cv = sb("cv", [P, 4, S], F32, mix_a)
            sqq = sb("sqq", [P, 2, 512], F32, mix_a)
            mbc = sb("mbc", [P, 4, S], F32, mix_a)
            marg = sb("marg", [P, 2, 384], F32, mix_a)
            mw = sb("mw", [P, 2, 384], F32, mix_a)
        with ExitStack() as mix_b:
            projb = sb("projb", [P, 44, S], F32, mix_b)
            vtokb = sb("vtokb", [P, 4, 4, P], F32, mix_b)
        sm, pr = marg, mw
        pT = sqq[:, :, 0:384]
        rot = r_tmp
        seed2 = [t[:].rearrange("p a b -> p (a b)")[:, 0:512] for t in (marg, mw)]
        ebc, mh = rv[:, 1], rr[:, 1]

        one = con[:, K_ONE:K_ONE + P]
        ident = con[:, K_ID:K_ID + P]
        blk = con[:, K_BLK:K_BLK + P]
        rotm = con[:, K_ROT:K_ROT + P]
        swpm = con[:, K_SWP:K_SWP + P]
        cos = con[:, K_COS:K_COS + S]
        sin = con[:, K_SIN:K_SIN + S]
        cos2 = cos.unsqueeze(1).to_broadcast([P, 2, S])
        sin2 = sin.unsqueeze(1).to_broadcast([P, 2, S])

        acc = ctx.enter_context(nc.psum_tensor("acc", [P, SLOTS, 512], F32))
        mx = ctx.enter_context(nc.psum_tensor("mx", [P, 4, 512], F32))

        landed = [sem(f"landed{j}") for j in range(SLOTS)]
        hi_ready = sem("hi_ready")
        lo_ready = sem("lo_ready")
        slab_used = sem("slab_used")
        acc_free = sem("acc_free")
        ada_landed = [sem(f"ada_landed{j}") for j in range(2)]
        ada_sum = sem("ada_sum")
        ada_col = sem("ada_col")
        ada_out = sem("ada_out")
        s_con = sem("s_con")
        s_con2 = sem("s_con2")
        s_x = sem("s_x")
        s_rows = sem("s_rows")
        s_rows2 = sem("s_rows2")
        s_small = sem("s_small")
        s_grp = sem("s_grp")
        boot_t = sem("boot_t")
        boot_v = sem("boot_v")
        c_silu = sem("c_silu")
        g_ready = sem("g_ready")
        nxa_ready = sem("nxa_ready")
        nx_ready = sem("nx_ready")
        chain_ev = sem("chain_ev")
        chain_nx = sem("chain_nx")
        g_scaled = sem("g_scaled")
        n_acc = sem("n_acc")
        n_hi = sem("n_hi")
        u_hi_ready = sem("u_hi_ready")
        n_sq = sem("n_sq")
        n_var = sem("n_var"); n_ln = sem("n_ln"); n_rs = sem("n_rs")
        n_ss = sem("n_ss")
        h_ready = sem("h_ready")
        chain_n = sem("chain_n")
        chain_a = sem("chain_a")
        chain_b = sem("chain_b")
        chain_up = sem("chain_up")
        chain_ffn = sem("chain_ffn")
        chain_pool = sem("chain_pool")
        chain_ada = sem("chain_ada")
        v_t = sem("v_t"); v_sb = sem("v_sb")
        qk_sq = sem("qk_sq"); qk_ss = sem("qk_ss"); qk_r = sem("qk_r"); qk_ln = sem("qk_ln"); qk_s = sem("qk_s"); qk_e = sem("qk_e"); qk_n = sem("qk_n")
        qk_rot = sem("qk_rot"); qk_rope = sem("qk_rope")
        swp_t = sem("swp_t"); swp_sb = sem("swp_sb")
        cv_ready = sem("cv_ready"); cv_silu = sem("cv_silu")
        f_abs = sem("f_abs"); f_ln = sem("f_ln"); f_M = sem("f_M"); f_G = sem("f_G"); f_E = sem("f_E")
        f_bc = sem("f_bc"); f_bcsb = sem("f_bcsb"); f_uc = sem("f_uc"); f_ucsb = sem("f_ucsb")
        f_exp = sem("f_exp"); ml_v = sem("ml_v"); ml_ln = sem("ml_ln"); ml_rs = sem("ml_rs")
        ml_s = sem("ml_s"); ml_arg = sem("ml_arg"); ml_w = sem("ml_w"); ml_p = sem("ml_p"); ml_nd = sem("ml_nd")
        ml_xo = sem("ml_xo"); ml_h = sem("ml_h"); ml_sq = sem("ml_sq"); ml_ss = sem("ml_ss"); ml_y = sem("ml_y")
        at_s = sem("at_s"); at_m = sem("at_m"); at_nb = sem("at_nb"); at_e = sem("at_e"); at_p = sem("at_p")
        at_t = sem("at_t"); at_pt = sem("at_pt"); at_o = sem("at_o"); at_y = sem("at_y"); at_hi = sem("at_hi")
        b_ln = sem("b_ln"); b_rs = sem("b_rs")
        g_used = sem("g_used")
        u_ready = sem("u_ready")
        b_rot = sem("b_rot"); b_rope = sem("b_rope"); b_vt = sem("b_vt"); b_vsb = sem("b_vsb")
        b_s = sem("b_s"); b_p = sem("b_p"); b_ret = sem("b_ret"); b_sq = sem("b_sq"); b_ss = sem("b_ss")
        b_r = sem("b_r"); b_y = sem("b_y"); b_gx = sem("b_gx"); b_ax = sem("b_ax")
        b_pool = sem("b_pool"); b_grp = sem("b_grp"); b_z = sem("b_z"); b_mrg = sem("b_mrg")
        g_exp = sem("g_exp")
        fin_h = sem("fin_h"); fin_t = sem("fin_t"); fin_sb = sem("fin_sb"); s_out = sem("s_out")

        with_k = lambda w: w.rearrange("l (k p) n -> p (l k) n", p=P)
        win_v, wout_v, wup_v, wdown_v = map(with_k, (w_in, w_out, w_up, w_down))
        ada_v, win2_v, ret_v, pool_v, wout2_v, ffn_v, ffo_v = map(
            with_k, (w_ada_2, w_in_2, w_ret_o_2, w_pool_o_2, w_out_2, w_ffn_in_2, w_ffn_out_2))

        block = ctx.enter_context(nc.Block())

        @block.sync
        def _(sp):
            def load(Q, j, dst, src):
                sp.wait_ge(lo_ready, Q * 4 + j + 1)
                sp.dma_start(dst, src).then_inc(landed[j], 16)

            def load_ada(l, a, slot):
                sp.wait_ge(ada_sum, l * ADA + a + 1)
                sp.dma_start(ada[:, slot], ada_v[:, ds(l * KT, KT), ds(a * 256, 256)]).then_inc(ada_landed[slot], 16)

            sp.dma_start(con[:, 0:K_BLK], consts[:, 0:K_BLK]).then_inc(s_con, 16)
            sp.dma_start(xtok[:], x[0].rearrange("(t p) d -> p t d", p=P)).then_inc(s_x, 16)
            r = 0
            for v, n in ((ln1, 16), (ln2, 16), (norm1_2, 16), (norm2_2, 16)):
                sp.dma_start(rows[r:r + n, 0, :], v.rearrange("l (k p) -> (l k) p", p=P)).then_inc(s_rows, 16)
                r += n
            sp.dma_start(rows[64:72, 0, :], final_norm_2.rearrange("(k p) -> k p", p=P)).then_inc(s_rows, 16)
            sp.dma_start(rows[72:80, 0, :], c_2[0].rearrange("(k p) -> k p", p=P)).then_inc(s_rows, 16)
            sp.dma_start(rows[80:88, 0, :], conv_b.rearrange("l (k p) -> (l k) p", p=P)).then_inc(s_rows, 16)
            sp.dma_start(rows[88:96, 0, :], pool_scale_2.rearrange("l (k p) -> (l k) p", p=P)).then_inc(s_rows, 16)
            sp.dma_start(rows[96:128, 0, :], conv_w.rearrange("l j (k p) -> (l j k) p", p=P)).then_inc(s_rows, 16)

            with sp.Fori(0, LAYERS) as l:
                q0 = l * A_QUADS
                for j in range(2):
                    load(q0, j, raw[:, j, :, 0:4],
                         win_v[:, ds(l * KT, KT), C_GATES * P + 4 * j:C_GATES * P + 4 * j + 4])
                for j in (2, 3):
                    load(q0, j, raw[:, j], win_v[:, ds(l * KT, KT), A_ORDER[j] * P:(A_ORDER[j] + 1) * P])
                with sp.Fori(0, 2) as it:
                    for j in range(4):
                        at, step = A_ORDER[4 + j] * P, (A_ORDER[8 + j] - A_ORDER[4 + j]) * P
                        load(q0 + 1 + it, j, raw[:, j], win_v[:, ds(l * KT, KT), ds(it * step + at, P)])
                with sp.Fori(0, 3) as it:
                    for j in range(4):
                        load(q0 + 3 + it, j, raw[:, j], win_v[:, ds(l * KT, KT), ds(it * 512 + (2 + j) * P, P)])
                with sp.Fori(0, 2) as it:
                    for j in range(4):
                        at, step = W_ORDER[j], W_ORDER[4 + j] - W_ORDER[j]
                        load(q0 + 6 + it, j, raw[:, j].rearrange("p k n -> p (k n)").unsqueeze(1),
                             wout_v[:, ds(l * KT + it * step + at, 1), :])
                with sp.Fori(0, A_UP // 8) as it:
                    for half in range(2):
                        for j in range(4):
                            load(q0 + 8 + it * 2 + half, j, raw[:, j],
                                 wup_v[:, ds(l * KT, KT), ds(it * 1024 + half * 512 + j * P, P)])
                        load_ada(l, it * 2 + half, half)
                with sp.Fori(0, KT // 4) as it:
                    for n in range(4):
                        for j in range(4):
                            load(q0 + 16 + it * 4 + n, j, raw[:, j],
                                 wdown_v[:, ds(l * 32 + j * KT, KT), ds(it * 512 + n * P, P)])
                        for r in range(2):
                            load_ada(l, it * 8 + 8 + 2 * n + r, r)

            with sp.Fori(0, LAYERS) as l:
                q0 = l * B_QUADS + LAYERS * A_QUADS
                for v, q, n in ((win2_v, 0, 11), (ret_v, 11, 2)):
                    with sp.Fori(0, n) as it:
                        for j in range(4):
                            load(q0 + q + it, j, raw[:, j], v[:, ds(l * KT, KT), ds(it * 512 + j * P, P)])
                for j in range(4):
                    load(q0 + 13, j, raw[:, j].rearrange("p k n -> p (k n)").rearrange("p (k n) -> p k n", k=4),
                         pool_v[:, ds(l * 4, 4), j * 256:(j + 1) * 256])
                with sp.Fori(0, 2) as it:
                    for j in range(4):
                        load(q0 + 14 + it, j, raw[:, j], wout2_v[:, ds(l * KT, KT), ds(it * 512 + j * P, P)])
                with sp.Fori(0, 11) as it:
                    for j in range(4):
                        load(q0 + 16 + it, j, raw[:, j],
                             ffn_v[:, ds(l * KT, KT), ds(it * 256 + (j // 2) * P + (j % 2) * FF2, P)])
                with sp.Fori(0, 2) as it:
                    for n in range(4):
                        for j in range(4):
                            k = FFO_PARTS[j]
                            load(q0 + 27 + it * 4 + n, j, raw[:, j, 0:k, :],
                                 ffo_v[:, ds(l * 22 + FFO_AT[j], k), ds(it * 512 + n * P, P)])

            for t in range(2):
                sp.wait_ge(fin_sb, 2 * t + 2)
                sp.dma_start(out[0, t * P:(t + 1) * P, :], raw[:, t].rearrange("p k n -> p (k n)")).then_inc(s_out, 16)
            sp.wait_ge(s_out, 32)

        @block.gpsimd
        def _(pool):
            nc.gpsimd.memset(raw[:, 0:2], 0.0).then_inc(lo_ready, SLOTS)
            nc.gpsimd.memset(ada_acc[:, 0, 2:4], 0.0).then_inc(slab_used, SLOTS)
            nc.gpsimd.memset(ada_acc[:, 0, 6:8], 0.0).then_inc(ada_sum, 2)
            nc.gpsimd.memset(ada_acc[:, 0, 8:10], 0.0).then_inc(g_used, 2)
            pool.dma_start(gate_b[:, 0:2], igate_b.rearrange("l h -> h l"), allow_slow_non_contiguous=True).then_inc(s_small, 16)
            pool.dma_start(gate_b[:, 2:4], fgate_b.rearrange("l h -> h l"), allow_slow_non_contiguous=True).then_inc(s_small, 16)
            pool.dma_start(sinkrow[:], swa_sinks.rearrange("l h -> (l h)").rearrange("(a n) -> a n", a=1)).then_inc(s_small, 16)
            pool.dma_start(wgrp[:], w_pool_grp_2.rearrange("l g i o -> i (l g) o")).then_inc(s_grp, 16)
            pool.dma_start(con[:, K_DEC:], consts[:, K_DEC:]).then_inc(s_con2, 16)

            def low(Q, kts=(KT,) * 4):
                for j, k in enumerate(kts):
                    pool.wait_ge(hi_ready, Q * 4 + j + 1)
                    nc.gpsimd.tensor_tensor(w_lo[:, j, 0:k], raw[:, j, 0:k], w_hi[:, j, 0:k].bitcast(F32),
                                            ALU.subtract).then_inc(lo_ready, 1)

            with pool.Fori(0, LAYERS * A_QUADS) as Q:
                low(Q)
            with pool.Fori(0, LAYERS) as l:
                with pool.Fori(0, 27) as q:
                    low(l * B_QUADS + q + LAYERS * A_QUADS)
                with pool.Fori(27, B_QUADS) as q:
                    low(l * B_QUADS + q + LAYERS * A_QUADS, FFO_PARTS)

        @block.scalar
        def _(act):
            def split(Q, js=(0, 1, 2, 3), kts=(KT,) * 4):
                for j in js:
                    act.wait_ge(landed[j], Q * 16 + 16)
                    act.wait_ge(slab_used, Q * 4 + j + 1)
                    nc.scalar.activation(w_hi[:, j, 0:kts[j]], raw[:, j, 0:kts[j]], ACT.Copy).then_inc(hi_ready, 1)

            def final_norm(v, x0):
                for kt in range(KT):
                    act.wait_ge(acc_free, x0 + kt + 1)
                    nc.scalar.activation(hf[:, kt], xT[:, kt], ACT.Copy, scale=vecT[:, V_FIN + kt:V_FIN + kt + 1]).then_inc(fin_h, 1)
                    if kt >= 4:
                        act.wait_ge(n_acc, v * KT + kt - 3)
                    nc.scalar.activation(tmp4[:, kt % 4], xT[:, kt], ACT.Square).then_inc(n_sq, 1)
                act.wait_ge(n_var, v + 1)
                rsqrt_seed(rstd[:, 0:2], var[:, 0:2], n_ln, n_rs, v)

            def norm_scaled(v, x0, ready, gain, early, late):
                def hi(kt):
                    act.wait_ge(acc_free, x0 + kt + 1)
                    if kt == 0:
                        act.wait_ge(*ready)
                    nc.scalar.activation(h_hi[:, kt, 0:S], xT[:, kt], ACT.Copy, scale=gain(kt)).then_inc(n_hi, 1)

                def square(kt):
                    if kt >= 4:
                        act.wait_ge(n_acc, v * KT + kt - 3)
                    nc.scalar.activation(tmp4[:, kt % 4], xT[:, kt], ACT.Square).then_inc(n_sq, 1)

                for kt in range(4):
                    hi(kt)
                    square(kt)
                for kt in range(4, KT):
                    early(kt - 4)
                    hi(kt)
                for kt in range(4, KT):
                    square(kt)
                late()
                act.wait_ge(n_var, v + 1)
                rsqrt_seed(rstd[:], var[:], n_ln, n_rs, v)

            def rsqrt_seed(r, x, ln_done, done, n):
                nc.scalar.activation(r, x, ACT.Ln).then_inc(ln_done, 1)
                act.wait_ge(ln_done, n + 1)
                nc.scalar.activation(r, r, ACT.Exp, scale=-0.5).then_inc(done, 1)

            LOG_EXP = "natural_log_exp_and_others"

            nc.scalar.preload_act_table_set(LOG_EXP)
            act.dma_start(rows[0:96, 1, :], b_ada_2.rearrange("l (k p) -> (l k) p", p=P)).then_inc(s_rows2, 16)
            act.dma_start(rows[96:100, 1, :], mlstm_norm.rearrange("l (k h) d -> (l k) (h d)", h=2)).then_inc(s_rows2, 16)
            for n, v in enumerate((moba_q_norm, moba_k_norm, swa_q_norm, swa_k_norm)):
                for half in range(2):
                    act.dma_start(rows[100 + 2 * n:102 + 2 * n, 1, half * HD:(half + 1) * HD], v).then_inc(s_rows2, 16)
            act.dma_start(con[:, K_BLK:K_DEC], consts[:, K_BLK:K_DEC]).then_inc(s_con, 16)

            with act.Fori(0, LAYERS) as l:
                q0 = l * A_QUADS
                u0 = l * A_UNITS + KT

                def split_one(i):
                    split(q0 + i // 4, (i % 4,))

                def values(b):
                    act.wait_ge(v_t, l * 3 + b + 1)
                    nc.scalar.activation(vtok[:, b].rearrange("p a n -> p (a n)"), mx[:, 3 if b else 2], ACT.Copy).then_inc(v_sb, 1)

                def head_square(g):
                    act.wait_ge(acc_free, u0 + (12, 14, 16, 21, 23)[g])
                    if g == 0:
                        act.wait_ge(ml_ss, l + 1)
                    if g >= 2:
                        act.wait_ge(qk_ss, l * 5 + g - 1)
                    nc.scalar.activation(sqq[:, g % 2], proj[:, QK_GROUPS[g]:QK_GROUPS[g] + 2].rearrange("p c t -> p (c t)"),
                                         ACT.Square).then_inc(qk_sq, 1)

                def head_seed(g):
                    act.wait_ge(qk_ss, l * 5 + g + 1)
                    if g >= 2:
                        act.wait_ge(qk_n, l * 5 + g - 1)
                    if g == 0:
                        act.wait_ge(ml_y, l + 1)
                    nc.scalar.activation(rv[:, g % 2], mx[:, 0], ACT.Identity, bias=head_eps[:]).then_inc(qk_r, 1)
                    act.wait_ge(qk_r, l * 5 + g + 1)
                    rsqrt_seed(rr[:, g % 2], rv[:, g % 2], qk_ln, qk_e, l * 5 + g)
                    act.wait_ge(qk_e, l * 5 + g + 1)
                    nc.scalar.activation(seed2[g % 2], rr[:, g % 2], ACT.Square).then_inc(qk_s, 1)

                def weights(h):
                    act.wait_ge(ml_arg, l * 4 + h + 1)
                    if h >= 2:
                        act.wait_ge(ml_nd, l * 4 + h - 1)
                    nc.scalar.activation(mw[:, h % 2], marg[:, h % 2], ACT.Exp, scale=-1.0).then_inc(ml_w, 1)

                norm_scaled(l * 2, l * A_UNITS, (nxa_ready, l + 1), lambda k: nx_a[:, k:k + 1], lambda n: split(q0, ((0,), (1,), (), (2,))[n]),
                            lambda: split_one(3))
                for i in range(4, 6):
                    split_one(i)
                act.wait_ge(f_abs, l + 1)
                nc.scalar.activation(g_e[:], g_a[:], ACT.Exp).then_inc(f_exp, 1)
                act.wait_ge(f_exp, l + 1)
                nc.scalar.activation(g_a[:], g_e[:], ACT.Ln, bias=1.0).then_inc(f_ln, 1)
                for i in (6, 7, 8):
                    split_one(i)
                act.wait_ge(f_G, l + 1)
                nc.scalar.activation(g_E[:], g_G[:], ACT.Exp, scale=-1.0).then_inc(f_E, 1)
                split_one(9)
                for n in range(2):
                    act.wait_ge(f_bc, l * 3 + n + 1)
                    nc.scalar.activation(mbc[:, 2 * n:2 * n + 2].rearrange("p h t -> p (h t)"), mx[:, 1 + n],
                                         ACT.Copy).then_inc(f_bcsb, 1)
                split_one(10)
                act.wait_ge(f_bc, l * 3 + 3)
                nc.scalar.activation(ebc, mx[:, 0], ACT.Copy).then_inc(f_bcsb, 1)
                split_one(11)
                act.wait_ge(cv_ready, l + 1)
                nc.scalar.activation(cact[:], vecT[:, V_C:V_C + KT], ACT.Silu).then_inc(c_silu, 1)
                nc.scalar.activation(cv[:], cv[:], ACT.Silu).then_inc(cv_silu, 1)
                act.wait_ge(acc_free, u0 + 8)
                nc.scalar.activation(proj[:, C_XO:C_XO + 2], proj[:, C_XO:C_XO + 2], ACT.Sigmoid).then_inc(ml_xo, 1)
                nc.scalar.preload_act_table_set(LOG_EXP)
                weights(0)
                split_one(12)
                values(0)
                weights(1)
                split_one(13)
                split_one(14)
                weights(2)
                split_one(15)
                weights(3)
                for i in (16, 17, 18):
                    split_one(i)
                act.wait_ge(ml_h, l + 1)
                nc.scalar.activation(sqq[:, 0], mh, ACT.Square).then_inc(ml_sq, 1)
                split_one(19)
                head_square(0)
                act.wait_ge(ml_v, l + 1)
                rsqrt_seed(rr[:, 0], rv[:, 0], ml_ln, ml_rs, l)
                split_one(20)
                head_square(1)
                head_seed(0)
                split_one(21)
                head_square(2)
                head_seed(1)
                split_one(22)
                split_one(23)
                values(1)
                head_seed(2)
                split_one(24)
                head_square(3)
                split_one(25)
                head_seed(3)
                split_one(26)
                head_square(4)
                split_one(27)
                head_seed(4)
                values(2)
                def exps(h):
                    i = h % 2
                    act.wait_ge(at_nb, l * 12 + h + 1)
                    if h >= 2:
                        act.wait_ge(at_t, l * 12 + h - 1)
                    for t, (a, b) in enumerate(((0, P), (P, 3 * P))):
                        ins = nc.scalar.activation(pr[:, i, a:b], sm[:, i, a:b], ACT.Exp, bias=st_nb[:, i, t:t + 1],
                                             scale=HD ** -0.5, accum_out=st_den[:, i, t:t + 1])
                    if h >= 6:
                        ins = nc.scalar.activation(st_es[:, i], st_nb[:, i], ACT.Exp, bias=lsink[:, h - 6:h - 5])
                    ins.then_inc(at_e, 1)

                exps(0)
                act.wait_ge(swp_t, l + 1)
                nc.scalar.activation(skswap[:], mx[:, 3, 0:S], ACT.Copy).then_inc(swp_sb, 1)

                def output_hi(h):
                    k = h // 2 if h < 6 else 5 + (h - 6) // 2
                    b = h % 2 * HD
                    act.wait_ge(at_o, l * 12 + h + 1)
                    nc.scalar.activation(y_hi[b:b + HD, k], mx[b:b + HD, 3, 0:S], ACT.Copy).then_inc(at_hi, 1)

                for h in range(12):
                    if h + 1 < 12:
                        exps(h + 1)
                    if h >= 1:
                        output_hi(h - 1)
                    act.wait_ge(at_t, l * 12 + h + 1)
                    if h >= 2:
                        act.wait_ge(at_o, l * 12 + h - 1)
                    nc.scalar.activation(pT[:, h % 2], mx[:, 2, 0:384], ACT.Copy).then_inc(at_pt, 1)
                    if h in (0, 3, 5, 7, 9, 11):
                        split_one((28, 29, 30, 31, 32, 33)[(0, 3, 5, 7, 9, 11).index(h)])
                output_hi(11)
                norm_scaled(l * 2 + 1, u0 + A_PROJ, (g_ready, l + 1), lambda k: lv[:, 8 + k:9 + k], lambda n: split(q0 + 8, ((), (), (), (2,))[n]),
                            lambda: split_one(35))
                with act.Fori(0, 8) as it:
                    for j in range(4):
                        split(q0 + 9 + it, (j,))
                        act.wait_ge(acc_free, u0 + 32 + it * 4 + j + 1)
                        nc.scalar.activation(u_hi[:, ds(it * 4 + j, 1)], tmp4[:, j % 2].unsqueeze(1), ACT.Square).then_inc(u_hi_ready, 1)
                with act.Fori(17, A_QUADS) as q:
                    split(q0 + q)

            with act.Fori(0, LAYERS) as l:
                q0 = l * B_QUADS + LAYERS * A_QUADS
                u0 = l * B_UNITS + LAYERS * A_UNITS + KT
                norm_scaled(l * 2 + 4, l * B_UNITS + LAYERS * A_UNITS, (nx_ready, l + 2), lambda k: nx[:, k:k + 1],
                            lambda n: split(q0, ((0,), (1,), (), (2,))[n]), lambda: split(q0, (3,)))
                with act.Fori(1, 5) as it:
                    split(q0 + it)

                def split_one(i):
                    split(q0 + i // 4, (i % 4,))

                def values(g):
                    act.wait_ge(b_vt, l * 4 + g + 1)
                    nc.scalar.activation(vtokb[:, g].rearrange("p a n -> p (a n)"), mx[:, 2 + g % 2], ACT.Copy).then_inc(b_vsb, 1)

                split_one(20)
                values(0)
                values(1)
                for i in (21, 22, 23):
                    split_one(i)
                values(2)
                values(3)
                for i in (24, 25):
                    split_one(i)
                for q in range(4):
                    act.wait_ge(b_ret, l * 4 + q + 1)
                    if q >= 1:
                        act.wait_ge(b_ss, l * 4 + q)
                    nc.scalar.activation(sqb[:], mx[:, 2], ACT.Square).then_inc(b_sq, 1)
                    split_one(26 + 5 * q)
                    split_one(27 + 5 * q)
                    act.wait_ge(b_r, l * 4 + q + 1)
                    rsqrt_seed(rb[:], bv[:], b_ln, b_rs, l * 4 + q)
                    if q == 0:
                        act.wait_ge(acc_free, u0 + 24)
                        swish = projb[:, B_G:B_G + 8]
                        nc.scalar.activation(swish, swish, ACT.Silu).then_inc(b_gx, 1)
                        nc.scalar.preload_act_table_set(LOG_EXP)
                    for i in range(28 + 5 * q, 31 + 5 * q):
                        split_one(i)
                for i in (46, 47):
                    split_one(i)
                act.wait_ge(acc_free, u0 + B_PROJ)
                for at in (B_ARET, B_APOOL):
                    branch = projb[:, at:at + 8]
                    nc.scalar.activation(branch, branch, ACT.Sigmoid).then_inc(b_ax, 1)
                    split(q0 + 12, (0, 1) if at == B_ARET else (2, 3))
                nc.scalar.preload_act_table_set(LOG_EXP)
                with act.Fori(13, 16) as q:
                    split(q0 + q)
                norm_scaled(l * 2 + 5, u0 + 56, (g_ready, l + LAYERS + 1), lambda k: lv[:, 16 + k:17 + k],
                            lambda n: split(q0 + 16, ((), (), (0,), (1,))[n]), lambda: split(q0 + 16, (2, 3)))
                nc.scalar.preload_act_table(ACT.Silu)
                with act.Fori(0, 11) as it:
                    for i in range(2):
                        act.wait_ge(g_scaled, l * 22 + it * 2 + i + 1)
                        nc.scalar.activation(tmp4[:, i], tmp4[:, i], ACT.Silu, bias=shift_w[:, 2 * i:2 * i + 1]).then_inc(g_exp, 1)
                        split(q0 + 17 + it, (2 * i, 2 * i + 1))
                with act.Fori(28, B_QUADS) as q:
                    split(q0 + q, kts=FFO_PARTS)
                nc.scalar.preload_act_table_set(LOG_EXP)
            final_norm(8, LAYERS * (A_UNITS + B_UNITS))

        @block.vector
        def _(dve):
            V = nc.vector

            def refine(c, r, x, t, wait=True):
                c.link(V.tensor_tensor(t, r, r, ALU.mult))
                c.link(V.scalar_tensor_tensor(t, t, -0.5, x, ALU.mult, ALU.mult))
                m = c.done(V.scalar_tensor_tensor(r, t, 1.5, r, ALU.add, ALU.mult))
                if wait:
                    c.wait(m)

            def norm_rstd(c, v, wait=True, width=S):
                for k in range(KT):
                    dve.wait_ge(n_sq, v * KT + k + 1)
                    if k:
                        dve.wait_ge(n_acc, v * KT + k)
                        V.tensor_tensor(ssq[:], ssq[:], tmp4[:, k % 4], ALU.add).then_inc(n_acc, 1)
                    else:
                        V.tensor_copy(ssq[:], tmp4[:, 0]).then_inc(n_acc, 1)
                dve.wait_ge(n_ss, v + 1)
                V.tensor_scalar(var[:, 0:width], mx[:, 0, 0:width], D * EPS, None, ALU.add).then_inc(n_var, 1)
                dve.wait_ge(n_rs, v + 1)
                refine(c, rstd[:, 0:width], var[:, 0:width], rs_tmp[:, 0:width], wait)

            def norm_scaled(v, gain, shift=None):
                c = Chain(dve, chain_n, v * 3 if shift is None else (v - 4) * 4 + 12)
                if shift is not None:
                    both = shift.unsqueeze(2).to_broadcast([P, KT, 2])
                    c.link(V.tensor_copy(h_hi[:, :, S:], both))
                    V.tensor_tensor(h_lo[:, :, S:], both, h_hi[:, :, S:].bitcast(F32), ALU.subtract)
                for k in range(KT):
                    dve.wait_ge(n_hi, v * KT + k + 1)
                    V.scalar_tensor_tensor(h_lo[:, k, 0:S], xT[:, k], gain(k), h_hi[:, k, 0:S].bitcast(F32),
                                           ALU.mult, ALU.subtract).then_inc(h_ready, 1)
                norm_rstd(c, v, wait=False)

            def ada_products(l, a, slot, turn):
                e = l * ADA + a
                c = Chain(dve, chain_ada, e * 7)
                dve.wait_ge(c_silu, l + 1)
                dve.wait_ge(ada_landed[slot], l * (ADA * 8) + turn * 16 + 16)
                c.link(V.tensor_scalar(ada_acc[:, slot], ada[:, slot, 0], cact[:, 0:1], None, ALU.mult))
                for k in range(1, KT):
                    ins = V.scalar_tensor_tensor(ada_acc[:, slot], ada[:, slot, k], cact[:, k:k + 1], ada_acc[:, slot],
                                                 ALU.mult, ALU.add)
                    if k < KT - 1:
                        c.link(ins)
                    else:
                        ins.then_inc(ada_sum, 1)

            def ada_columns(l, a, slot):
                e = l * ADA + a
                dve.wait_ge(ada_col, e + 1)
                V.tensor_tensor(modT[:, ds(e * 2, 2)], mx[:, 3, 2 * slot:2 * slot + 2],
                                vecT[:, ds(e * 2 + V_BADA, 2)], ALU.add).then_inc(ada_out, 1)

            boot = Chain(dve, boot_v, 0)
            V.memset(ones4[:], 1.0)
            V.memset(head_eps[:], HD * EPS)
            V.memset(modT[:], 0.0)
            for b in range(4):
                dve.wait_ge(boot_t, b + 1)
                V.tensor_copy(xT[:, 2 * b:2 * b + 2].rearrange("p k t -> p (k t)"), mx[:, b]).then_inc(acc_free, 2)
            dve.wait_ge(boot_t, 5)
            boot.link(V.tensor_copy(vecT[:, 0:P], acc[:, 0, 0:P]))
            boot.link(V.tensor_scalar(vecT[:, 0:V_C], vecT[:, 0:V_C], float(D) ** 0.5, None, ALU.mult))
            V.tensor_copy(nx_a[:], vecT[:, V_LN1:V_LN1 + KT]).then_inc(nxa_ready, 1)
            dve.wait_ge(boot_t, 6)
            boot.link(V.tensor_copy(vecT[:, P:VECS], acc[:, 1, 0:VECS - P]))
            boot.link(V.tensor_scalar(vecT[:, V_MLN:VECS], vecT[:, V_MLN:VECS], float(HD) ** 0.5, None, ALU.mult))
            dve.wait_ge(boot_t, 7)
            boot.link(V.tensor_copy(sink[:], acc[:, 2, 0:12]))
            dve.wait_ge(s_small, 48)
            dve.wait_ge(s_con, 32)
            dve.wait_ge(nxa_ready, 1)

            with dve.Fori(0, LAYERS) as l:
                c = Chain(dve, chain_a, l * CHAIN_A)
                q0 = l * A_QUADS
                norm_scaled(l * 2, lambda k: nx_a[:, k:k + 1])
                V.tensor_copy(lv[:, 8:16], vecT[:, ds(l * 8 + V_LN2, 8)]).then_inc(g_ready, 1)
                for at, v, n in ((16, V_CONVB, 4), (20, V_CONVW, 16), (36, V_MLN, 2)):
                    c.done(V.tensor_copy(lv[:, at:at + n], vecT[:, ds(l * n + v, n)]))
                for n in range(4):
                    c.done(V.tensor_copy(lv[:, 38 + n:39 + n], vecT[:, ds(l + V_HN + 2 * n, 1)]))
                c.done(V.tensor_copy(lsink[:], sink[:, ds(l * 6, 6)]))
                for n in range(2):
                    c.done(V.tensor_copy(lgate[:, n:n + 1], gate_b[:, ds(l + 2 * n, 1)]))
                c.link(V.tensor_scalar(lnegsink[:], sink[:, ds(l * 6, 6)], -1.0, None, ALU.mult))

                u0 = l * A_UNITS + KT

                def to_sbuf(*slabs):
                    for i in slabs:
                        dve.wait_ge(slab_used, (q0 + i // 4) * 4 + i % 4 + 1 + SLOTS)
                        if i < 2:
                            V.tensor_tensor((gi, gf)[i][:], acc[0:4, i, 0:S], rstd[0:4], ALU.mult).then_inc(acc_free, 1)
                        else:
                            V.tensor_tensor(proj[:, A_ORDER[i]], acc[:, i % 4, 0:S], rstd[:], ALU.mult).then_inc(acc_free, 1)

                def convolve(j):
                    for k in range(4):
                        src = proj[:, C_XQK + k]
                        w = lambda tap: lv[:, 20 + tap * 4 + k:21 + tap * 4 + k]
                        if j == 0:
                            marks[k] = c.done(V.tensor_scalar(cv[:, k], src, w(3), lv[:, 16 + k:17 + k], ALU.mult, ALU.add))
                        else:
                            c.wait(marks[k])
                            ins = V.scalar_tensor_tensor(cv[:, k, j:], src[:, 0:S - j], w(3 - j), cv[:, k, j:],
                                                         ALU.mult, ALU.add)
                            if j < 3 or k < 3:
                                marks[k] = c.done(ins)
                            else:
                                ins.then_inc(cv_ready, 1)
                                dve.wait_ge(cv_ready, l + 1)

                groups = QK_GROUPS

                def gain_of(chunk):
                    n = 0 if chunk < C_MK else 1 if chunk < C_MV else 2 if chunk < C_SK else 3
                    return lv[:, 38 + n:39 + n]

                def head_norm(g):
                    dve.wait_ge(qk_s, l * 5 + g + 1)
                    r, r2 = rr[:, g % 2], seed2[g % 2]
                    c.link(V.scalar_tensor_tensor(r2, r2, -0.5, rv[:, g % 2], ALU.mult, ALU.mult))
                    c.link(V.scalar_tensor_tensor(r, r2, 1.5, r, ALU.add, ALU.mult))
                    for i in range(2):
                        ch = groups[g] + i
                        ins = V.scalar_tensor_tensor(proj[:, ch], proj[:, ch], gain_of(ch), rr[:, g % 2, i * S:(i + 1) * S],
                                                     ALU.mult, ALU.mult)
                    ins.then_inc(qk_n, 1)
                    dve.wait_ge(qk_n, l * 5 + g + 1)

                def rope(g):
                    pair = proj[:, groups[g]:groups[g] + 2]
                    dve.wait_ge(qk_n, l * 5 + g + 1)
                    dve.wait_ge(qk_rot, l * 5 + g + 1)
                    c.done(V.tensor_tensor(rot[:].rearrange("p (c t) -> p c t", c=2),
                                           mx[:, 1 + g % 2].rearrange("p (c t) -> p c t", c=2), sin2, ALU.mult))
                    c.link(V.tensor_tensor(pair, pair, cos2, ALU.mult))
                    V.tensor_tensor(pair, pair, rot[:].rearrange("p (c t) -> p c t", c=2), ALU.add).then_inc(qk_rope, 1)
                    dve.wait_ge(qk_rope, l * 5 + g + 1)

                def arguments(h):
                    i = h % 2
                    dve.wait_ge(f_bcsb, l * 3 + h // 2 + 1)
                    if h >= 2:
                        dve.wait_ge(ml_w, l * 4 + h - 1)
                    V.scalar_tensor_tensor(marg[:, i, 0:S], mbc[:, h], nucol[:, h:h + 1], con[:, K_MT:K_MT + S],
                                           ALU.add, ALU.add)
                    V.scalar_tensor_tensor(marg[:, i, S:384], mbc[:, h, P:S], nucol[:, 4 + h:5 + h], con[:, K_MT:K_MT + P],
                                           ALU.add, ALU.add).then_inc(ml_arg, 1)
                    dve.wait_ge(ml_arg, l * 4 + h + 1)

                def weigh(h):
                    dve.wait_ge(ml_s, l * 4 + h + 1)
                    dve.wait_ge(ml_w, l * 4 + h + 1)
                    V.scalar_tensor_tensor(mw[:, h % 2], mx[:, h % 2, 0:384], HD ** -0.5, mw[:, h % 2],
                                           ALU.mult, ALU.mult).then_inc(ml_p, 1)
                    dve.wait_ge(ml_p, l * 4 + h + 1)

                dve.wait_ge(chain_n, l * 6 + 3)
                to_sbuf(0, 1)
                dve.wait_ge(acc_free, u0 + 2)
                c.done(V.tensor_scalar(gi[:], gi[:], lgate[:, 0:1], None, ALU.add))
                c.link(V.tensor_scalar(gf[:], gf[:], lgate[:, 1:2], None, ALU.add))
                V.scalar_tensor_tensor(g_a[:], gf[:], -1.0, gf[:], ALU.mult, ALU.min).then_inc(f_abs, 1)
                dve.wait_ge(f_abs, l + 1)
                to_sbuf(2)
                dve.wait_ge(f_ln, l + 1)
                c.link(V.scalar_tensor_tensor(gf[:], gf[:], 0.0, g_a[:], ALU.min, ALU.subtract))
                c.link(V.tensor_tensor_scan(g_F[:], ones4[:], gf[:], 0.0, ALU.mult, ALU.add))
                c.link(V.tensor_tensor(g_u[:], gi[:], g_F[:], ALU.subtract))
                V.tensor_tensor_scan(g_M[:], ones4[:], g_u[:], 0.0, ALU.mult, ALU.max).then_inc(f_M, 1)
                dve.wait_ge(f_M, l + 1)
                V.tensor_tensor(g_G[:], g_F[:], g_M[:], ALU.add).then_inc(f_G, 1)
                dve.wait_ge(f_G, l + 1)
                to_sbuf(3, 4, 5)
                V.tensor_copy(nx_a[:], vecT[:, ds(l * KT + V_LN1 + KT, KT)]).then_inc(nxa_ready, 1)
                c.done(V.scalar_tensor_tensor(nx[:, 0:KT], modT[:, KT:2 * KT], 1.0, vecT[:, V_N1:V_N1 + KT], ALU.add, ALU.mult))
                V.tensor_copy(nx[:, KT:], modT[:, 0:KT]).then_inc(nx_ready, 1)
                dve.wait_ge(acc_free, u0 + 6)
                marks = {}
                convolve(0)
                convolve(1)
                to_sbuf(6)
                convolve(2)
                to_sbuf(7)
                convolve(3)
                dve.wait_ge(f_uc, l + 1)
                V.tensor_scalar(nucol[:], mx[:, 3, 0:8], -1.0, None, ALU.mult).then_inc(f_ucsb, 1)
                dve.wait_ge(f_ucsb, l + 1)
                arguments(0)
                arguments(1)
                to_sbuf(8, 9)
                weigh(0)
                to_sbuf(10)
                arguments(2)
                weigh(1)
                to_sbuf(11)
                arguments(3)
                weigh(2)
                weigh(3)
                to_sbuf(12)
                dve.wait_ge(ml_nd, l * 4 + 4)
                dve.wait_ge(f_bcsb, l * 3 + 3)
                c.link(V.scalar_tensor_tensor(r_tmp[:], mx[:, 3], -1.0, ebc, ALU.mult, ALU.max))
                c.link(V.tensor_tensor(r_tmp[:], mx[:, 3], r_tmp[:], ALU.max))
                to_sbuf(13)
                c.link(V.reciprocal(r_tmp[:], r_tmp[:]))
                to_sbuf(14)
                c.link(V.tensor_tensor(mh, mx[:, 2], r_tmp[:], ALU.mult))
                dve.wait_ge(ml_xo, l + 1)
                V.tensor_tensor(mh, mh, proj[:, C_XO:C_XO + 2].rearrange("p c t -> p (c t)"),
                                ALU.mult).then_inc(ml_h, 1)
                dve.wait_ge(ml_h, l + 1)
                to_sbuf(15)
                dve.wait_ge(ml_ss, l + 1)
                V.tensor_scalar(rv[:, 0], mx[:, 0], HD * EPS, None, ALU.add).then_inc(ml_v, 1)
                dve.wait_ge(ml_v, l + 1)
                dve.wait_ge(ml_rs, l + 1)
                refine(c, rr[:, 0], rv[:, 0], r_tmp[:])
                for k in range(2):
                    c.link(V.scalar_tensor_tensor(mh[:, k * S:(k + 1) * S], mh[:, k * S:(k + 1) * S], lv[:, 36 + k:37 + k],
                                                  rr[:, 0, k * S:(k + 1) * S], ALU.mult, ALU.mult))
                mh2 = mh.rearrange("p (c t) -> p c t", c=2)
                c.link(V.tensor_copy(y_hi[:, 3:5], mh2))
                V.tensor_tensor(y_lo[:, 3:5], mh2, y_hi[:, 3:5].bitcast(F32), ALU.subtract).then_inc(ml_y, 1)
                dve.wait_ge(ml_y, l + 1)
                to_sbuf(16, 17)
                head_norm(0)
                to_sbuf(18, 19)
                head_norm(1)
                rope(0)
                to_sbuf(20, 21)
                head_norm(2)
                rope(1)
                to_sbuf(22, 23)
                head_norm(3)
                rope(2)
                head_norm(4)
                rope(3)

                def maxima(h):
                    i = h % 2
                    mask = K_MCA if h < 6 else K_MSW
                    dve.wait_ge(at_s, l * 12 + h + 1)
                    if h >= 2:
                        dve.wait_ge(at_e, l * 12 + h - 1)
                    V.tensor_tensor(sm[:, i], mx[:, i, 0:384], con[:, mask:mask + 384], ALU.add).then_inc(at_m, 1)
                    dve.wait_ge(at_m, l * 12 + h + 1)
                    c.done(V.tensor_reduce(st_mx[:, i, 0:1], sm[:, i, 0:P], AX, ALU.max))
                    c.link(V.tensor_reduce(st_mx[:, i, 1:2], sm[:, i, P:384], AX, ALU.max))
                    if h >= 6:
                        ins = V.tensor_scalar(st_nb[:, i], st_mx[:, i], -HD ** -0.5, lnegsink[:, h - 6:h - 5], ALU.mult, ALU.min)
                    else:
                        ins = V.tensor_scalar(st_nb[:, i], st_mx[:, i], -HD ** -0.5, None, ALU.mult)
                    ins.then_inc(at_nb, 1)
                    dve.wait_ge(at_nb, l * 12 + h + 1)

                def probabilities(h):
                    i = h % 2
                    dve.wait_ge(at_e, l * 12 + h + 1)
                    if h >= 6:
                        c.link(V.tensor_tensor(st_den[:, i], st_den[:, i], st_es[:, i], ALU.add))
                    c.link(V.reciprocal(st_rec[:, i], st_den[:, i]))
                    V.tensor_scalar(pr[:, i, 0:P], pr[:, i, 0:P], st_rec[:, i, 0:1], None, ALU.mult)
                    V.tensor_scalar(pr[:, i, P:384], pr[:, i, P:384], st_rec[:, i, 1:2], None, ALU.mult).then_inc(at_p, 1)
                    dve.wait_ge(at_p, l * 12 + h + 1)

                def outputs(h):
                    k = h // 2 if h < 6 else 5 + (h - 6) // 2
                    b = h % 2 * HD
                    dve.wait_ge(at_hi, l * 12 + h + 1)
                    o = mx[b:b + HD, 3, 0:S]
                    V.tensor_tensor(y_lo[b:b + HD, k], o, y_hi[b:b + HD, k].bitcast(F32), ALU.subtract).then_inc(at_y, 1)
                    dve.wait_ge(at_y, l * 12 + h + 1)

                maxima(0)
                rope(4)
                maxima(1)
                for h in range(12):
                    probabilities(h)
                    if h + 2 < 12:
                        maxima(h + 2)
                    if h >= 1:
                        outputs(h - 1)
                outputs(11)
                V.memset(spare[:], 0.0).then_inc(chain_a, CHAIN_A - c.n)
                assert c.n < CHAIN_A

                dve.wait_ge(slab_used, (q0 + 7) * 4 + 4 + SLOTS)
                for k in range(KT):
                    V.tensor_tensor(xT[:, k], acc[:, k // 2, k % 2 * S:(k % 2 + 1) * S], xT[:, k], ALU.add).then_inc(acc_free, 1)
                norm_scaled(l * 2 + 1, lambda k: lv[:, 8 + k:9 + k])
                with dve.Fori(0, 4) as it:
                    for half in range(2):
                        a = it * 2 + half

                        def low(j):
                            unit = it * 8 + half * 4 + j
                            dve.wait_ge(u_hi_ready, l * 32 + unit + 1)
                            dve.wait_ge(chain_up, l * 32 + unit + 1)
                            V.tensor_tensor(u_lo[:, ds(unit, 1)], tmp4[:, 2 + j % 2:3 + j % 2], u_hi[:, ds(unit, 1)].bitcast(F32),
                                            ALU.subtract).then_inc(u_ready, 1)

                        ada_products(l, a, half, it)
                        for j in range(4):
                            i = j % 2
                            unit = it * 8 + half * 4 + j
                            dve.wait_ge(slab_used, (q0 + 8) * 4 + unit + 1 + SLOTS)
                            if j == 0:
                                dve.wait_ge(chain_n, l * 6 + 6)
                            V.scalar_tensor_tensor(tmp4[:, i], acc[:, j, 0:S], 0.0, rstd[:], ALU.max, ALU.mult).then_inc(acc_free, 1)
                            if j >= 1:
                                low(j - 1)
                            dve.wait_ge(acc_free, u0 + 32 + unit + 1)
                            V.tensor_tensor(tmp4[:, 2 + i], tmp4[:, i], tmp4[:, i], ALU.mult).then_inc(chain_up, 1)
                        low(3)
                        ada_columns(l, a, half)
                with dve.Fori(0, 2) as it:
                    for n in range(4):
                        for r in range(2):
                            ada_products(l, it * 8 + 8 + 2 * n + r, r, it * 4 + 4 + n)
                            if r == 0:
                                ada_columns(l, it * 8 + 8 + 2 * n, 0)
                        k = ds(it * 4 + n, 1)
                        dve.wait_ge(slab_used, (q0 + 16 + it * 4 + n) * 4 + 4 + SLOTS)
                        V.tensor_tensor(xT[:, k], acc[:, n, 0:S].unsqueeze(1), xT[:, k], ALU.add).then_inc(acc_free, 1)
                        ada_columns(l, it * 8 + 9 + 2 * n, 1)

            dve.wait_ge(s_con2, 16)
            dve.wait_ge(s_grp, 16)
            dve.wait_ge(ada_out, LAYERS * ADA)
            with dve.Fori(0, LAYERS) as l:
                c = Chain(dve, chain_b, l * CHAIN_B)
                q0 = l * B_QUADS + LAYERS * A_QUADS
                u0 = l * B_UNITS + LAYERS * A_UNITS + KT
                dve.wait_ge(acc_free, u0)
                norm_scaled(l * 2 + 4, lambda k: nx[:, k:k + 1], nx[:, KT:])
                c.done(V.tensor_copy(lgrp[:], wgrp[:, ds(l * 4, 4)]))
                c.done(V.tensor_copy(lv[:, 0:4], vecT[:, ds(l * 4 + V_PSC, 4)]))
                c.link(V.tensor_copy(lm[:], modT[:, ds(l * MOD, MOD)]))
                V.scalar_tensor_tensor(lv[:, 16:24], lm[:, 32:40], 1.0, vecT[:, ds(l * 8 + V_N2, 8)], ALU.add, ALU.mult).then_inc(g_ready, 1)

                def unit_out(to, i, j):
                    V.tensor_copy(shift_w[:, j:j + 1], acc[:, j, S:S + 1])
                    V.tensor_tensor(to, acc[:, j, 0:S].unsqueeze(1), rstd[:].unsqueeze(1), ALU.mult).then_inc(chain_ev, 1)
                    dve.wait_ge(chain_ev, l * B_PROJ + i + 1)
                    V.tensor_scalar(to, to, shift_w[:, j:j + 1], None, ALU.add).then_inc(acc_free, 1)

                with dve.Fori(0, 4) as it:
                    for j in range(4):
                        if j == 0:
                            dve.wait_ge(chain_n, l * 8 + 16)
                        dve.wait_ge(slab_used, (q0 + it) * 4 + j + 1 + SLOTS)
                        unit_out(projb[:, ds(it * 4 + j, 1)], it * 4 + j, j)

                def to_sbuf(*chunks):
                    for i in chunks:
                        dve.wait_ge(slab_used, (q0 + i // 4) * 4 + i % 4 + 1 + SLOTS)
                        unit_out(projb[:, i:i + 1], i, i % 4)

                dve.wait_ge(acc_free, u0 + 16)
                def rope2(g):
                    pair = projb[:, 2 * g:2 * g + 2]
                    r3 = rotb[:].rearrange("p (c t) -> p c t", c=2)
                    dve.wait_ge(b_rot, l * 4 + g + 1)
                    c.done(V.tensor_tensor(r3, mx[:, g % 2].rearrange("p (c t) -> p c t", c=2), sin2, ALU.mult))
                    c.link(V.tensor_tensor(pair, pair, cos2, ALU.mult))
                    V.tensor_tensor(pair, pair, r3, ALU.add).then_inc(b_rope, 1)
                    dve.wait_ge(b_rope, l * 4 + g + 1)

                def decayed(h):
                    i = h % 2
                    dec = con[:, K_DEC + h * S:K_DEC + (h + 1) * S]
                    dve.wait_ge(b_s, l * 8 + h + 1)
                    if h >= 2:
                        dve.wait_ge(b_ret, l * 4 + h // 2)
                    V.tensor_tensor(pb[:, i, 0:S], mx[:, i, 0:S], dec, ALU.mult)
                    V.tensor_tensor(pb[:, i, S:384], mx[:, i, S:384], dec[:, 0:P], ALU.mult).then_inc(b_p, 1)
                    dve.wait_ge(b_p, l * 8 + h + 1)

                def mean_squares(q):
                    dve.wait_ge(b_ss, l * 4 + q + 1)
                    V.tensor_scalar(bv[:], mx[:, 3], 1.0 / P, EPS, ALU.mult, ALU.add).then_inc(b_r, 1)
                    dve.wait_ge(b_r, l * 4 + q + 1)

                def gated(q):
                    g2 = projb[:, B_G + 2 * q:B_G + 2 * q + 2].rearrange("p c t -> p (c t)")
                    dve.wait_ge(b_rs, l * 4 + q + 1)
                    refine(c, rb[:], bv[:], b_tmp[:])
                    c.link(V.tensor_tensor(rb[:], mx[:, 2], rb[:], ALU.mult))
                    dve.wait_ge(b_gx, l + 1)
                    c.link(V.tensor_tensor(rb[:], rb[:], g2, ALU.mult))
                    r3 = rb[:].rearrange("p (c t) -> p c t", c=2)
                    c.link(V.tensor_copy(y_hi[:, 2 * q:2 * q + 2], r3))
                    V.tensor_tensor(y_lo[:, 2 * q:2 * q + 2], r3, y_hi[:, 2 * q:2 * q + 2].bitcast(F32),
                                    ALU.subtract).then_inc(b_y, 1)
                    dve.wait_ge(b_y, l * 4 + q + 1)

                def pooled(g):
                    src = projb[:, B_PIN + g]
                    c.link(V.tensor_copy(pad[:, 0, 16:], src))
                    for n in range(g + 1):
                        a, b = n % 2, 1 - n % 2
                        step = 1 << n
                        c.link(V.tensor_tensor(pad[:, b, 16:], pad[:, a, 16:], pad[:, a, 16 - step:16 + S - step], ALU.add))
                    sums = pad[:, (g + 1) % 2, 16:]
                    cnt = con[:, K_CNT + 16 * g:K_CNT + 16 * (g + 1)]
                    c.done(V.tensor_tensor(b_tmp[:, 0:16], sums[:, 0:16], cnt, ALU.mult))
                    c.link(V.scalar_tensor_tensor(src[:, 16:], sums[:, 16:], 1.0 / (2 << g), src[:, 16:], ALU.mult, ALU.subtract))
                    V.tensor_tensor(src[:, 0:16], b_tmp[:, 0:16], src[:, 0:16], ALU.subtract).then_inc(b_pool, 1)
                    dve.wait_ge(b_pool, l * 4 + g + 1)

                c.link(V.memset(pad[:], 0.0))
                rope2(0)
                rope2(1)
                to_sbuf(16)
                rope2(2)
                to_sbuf(17)
                rope2(3)
                to_sbuf(18)
                decayed(0)
                decayed(1)
                to_sbuf(19, 20)
                for q in range(4):
                    mean_squares(q)
                    to_sbuf(21 + 5 * q, 22 + 5 * q)
                    if q + 1 < 4:
                        decayed(2 * q + 2)
                        decayed(2 * q + 3)
                    if q == 0:
                        to_sbuf(23)
                        gated(q)
                        to_sbuf(24, 25)
                    else:
                        gated(q)
                        to_sbuf(23 + 5 * q, 24 + 5 * q, 25 + 5 * q)
                    if q >= 2:
                        if q == 2:
                            dve.wait_ge(acc_free, u0 + B_PIN + 4)
                        pooled(2 * q - 4)
                        pooled(2 * q - 3)
                to_sbuf(*range(41, 44))
                for g in range(4):
                    dve.wait_ge(b_grp, l * 4 + g + 1)
                    c.link(V.tensor_scalar(rb[:, 0:S], mx[:, g, 0:S], lv[:, g:g + 1], None, ALU.mult))
                    c.link(V.tensor_copy(h_hi[:, g, 0:S], rb[:, 0:S]))
                    V.tensor_tensor(h_lo[:, g, 0:S], rb[:, 0:S], h_hi[:, g, 0:S].bitcast(F32), ALU.subtract).then_inc(b_z, 1)
                    dve.wait_ge(b_z, l * 4 + g + 1)
                V.memset(spare[:], 0.0).then_inc(chain_b, CHAIN_B - c.n)
                assert c.n < CHAIN_B

                with dve.Fori(0, 2) as it:
                    for j in range(4):
                        k = ds(it * 4 + j + B_ARET, 1)
                        dve.wait_ge(b_ax, l * 2 + 1)
                        dve.wait_ge(slab_used, (q0 + 11 + it) * 4 + j + 1 + SLOTS)
                        V.tensor_tensor(projb[:, k], acc[:, j, 0:S].unsqueeze(1), projb[:, k], ALU.mult).then_inc(acc_free, 1)
                for j in range(4):
                    e = Chain(dve, chain_pool, (l * 4 + j) * 2)
                    ap2 = projb[:, B_APOOL + 2 * j:B_APOOL + 2 * j + 2]
                    ar2 = projb[:, B_ARET + 2 * j:B_ARET + 2 * j + 2]
                    dve.wait_ge(b_ax, l * 2 + 2)
                    dve.wait_ge(slab_used, (q0 + 13) * 4 + j + 1 + SLOTS)
                    V.tensor_tensor(ap2, acc[:, j].rearrange("p (c t) -> p c t", c=2), ap2, ALU.mult).then_inc(acc_free, 1)
                    dve.wait_ge(acc_free, u0 + B_PROJ + B_RET + j + 1)
                    e.link(V.tensor_tensor(ap2, ap2, ar2, ALU.add))
                    e.link(V.tensor_copy(y_hi[:, 2 * j:2 * j + 2], ap2))
                    V.tensor_tensor(y_lo[:, 2 * j:2 * j + 2], ap2, y_hi[:, 2 * j:2 * j + 2].bitcast(F32),
                                    ALU.subtract).then_inc(b_mrg, 1)
                    dve.wait_ge(b_mrg, l * 4 + j + 1)
                for j in range(8):
                    dve.wait_ge(slab_used, (q0 + 14) * 4 + j + 1 + SLOTS)
                    V.scalar_tensor_tensor(xT[:, j], acc[:, j % 4, 0:S], lm[:, 16 + j:17 + j], xT[:, j], ALU.mult,
                                           ALU.add).then_inc(acc_free, 1)
                dve.wait_ge(g_ready, l + LAYERS + 1)
                norm_scaled(l * 2 + 5, lambda k: lv[:, 16 + k:17 + k], lm[:, 24:32])
                with dve.Fori(0, 11) as it:
                    for i in range(2):
                        unit = it * 2 + i
                        e = Chain(dve, chain_ffn, (l * 22 + unit) * 2)
                        to = ds(unit, 1)
                        gate, up = tmp4[:, i], tmp4[:, 2 + i]
                        if i == 0:
                            dve.wait_ge(chain_n, l * 8 + 20)
                        dve.wait_ge(slab_used, (q0 + 16 + it) * 4 + 2 * i + 1 + SLOTS)
                        V.tensor_copy(shift_w[:, 2 * i:2 * i + 1], acc[:, 2 * i, S:S + 1])
                        V.tensor_tensor(gate, acc[:, 2 * i, 0:S], rstd[:], ALU.mult).then_inc(g_scaled, 1)
                        dve.wait_ge(slab_used, (q0 + 16 + it) * 4 + 2 * i + 2 + SLOTS)
                        V.tensor_copy(shift_w[:, 2 * i + 1:2 * i + 2], acc[:, 2 * i + 1, S:S + 1])
                        e.link(V.tensor_tensor(up, acc[:, 2 * i + 1, 0:S], rstd[:], ALU.mult))
                        dve.wait_ge(g_exp, l * 22 + unit + 1)
                        V.scalar_tensor_tensor(up, up, shift_w[:, 2 * i + 1:2 * i + 2], gate, ALU.add, ALU.mult).then_inc(acc_free, 2)
                        dve.wait_ge(acc_free, u0 + 64 + unit * 2 + 2)
                        e.link(V.tensor_copy(u_hi[:, to], tmp4[:, 2 + i:3 + i]))
                        V.tensor_tensor(u_lo[:, to], tmp4[:, 2 + i:3 + i], u_hi[:, to].bitcast(F32),
                                        ALU.subtract).then_inc(g_used, 1)
                c = Chain(dve, chain_nx, l)
                c.done(V.scalar_tensor_tensor(nx[:, 0:KT], modT[:, ds(l * MOD + MOD + KT, KT)], 1.0,
                                              vecT[:, ds(l * KT + V_N1 + KT, KT)], ALU.add, ALU.mult))
                V.tensor_copy(nx[:, KT:], modT[:, ds(l * MOD + MOD, KT)]).then_inc(nx_ready, 1)
                for n in range(8):
                    dve.wait_ge(slab_used, (q0 + 27 + n) * 4 + 4 + SLOTS)
                    V.scalar_tensor_tensor(xT[:, n], acc[:, n % 4, 0:S], lm[:, 40 + n:41 + n], xT[:, n], ALU.mult,
                                           ALU.add).then_inc(acc_free, 1)

            norm_rstd(Chain(dve, chain_n, 12 + 4 * 4), 8, width=2)
            for b in range(4):
                t = b // 2
                dve.wait_ge(fin_t, b + 1)
                V.tensor_scalar(raw[:, t, b % 2 * 4:(b % 2 + 1) * 4].rearrange("p k n -> p (k n)"), acc[:, b], rstd[:, t:t + 1], None,
                                ALU.mult).then_inc(fin_sb, 1)

        @block.tensor
        def _(pe):
            mm = nc.tensor.matmul

            h_hi_of = lambda k: h_hi[:, k, 0:S]
            h_lo_of = lambda k: h_lo[:, k, 0:S]

            def slab(Q, j, rhs_hi, rhs_lo, outp, first=True, last=True, kts=KT, lhs=None, before=None):
                pe.wait_ge(lo_ready, Q * 4 + j + 1 + SLOTS)
                for k in range(kts):
                    if before:
                        before(k)
                    wh, wl = (w_hi[:, j, k], w_lo[:, j, k]) if lhs is None else lhs(k)
                    mm(outp, wh, rhs_hi(k), start=first and k == 0, stop=False)
                    mm(outp, wh, rhs_lo(k), start=False, stop=False)
                    ins = mm(outp, wl, rhs_hi(k), start=False, stop=last and k == kts - 1)
                return ins

            def norm_sum(v):
                pe.wait_ge(n_acc, v * KT + KT)
                mm(mx[:, 0, 0:S], one, ssq[:], start=True, stop=True).then_inc(n_ss, 1)

            def dense(q, n, rhs, unit0, ready, width=S):
                with pe.Fori(0, n) as it:
                    pe.wait_ge(*ready)
                    for j in range(4):
                        pe.wait_ge(acc_free, unit0 + it * 4 + j + 1)
                        slab(q + it, j, lambda k: rhs[0][:, k], lambda k: rhs[1][:, k], acc[:, j, 0:width]).then_inc(slab_used, 1)

            def ada_partitions(l, a, slot):
                pe.wait_ge(ada_sum, l * ADA + a + 1 + 2)
                for half in range(2):
                    ins = mm(mx[:, 3, 2 * slot + half:2 * slot + half + 1], ada_acc[:, slot, half * P:(half + 1) * P],
                             one[:, 0:1], start=True, stop=True)
                ins.then_inc(ada_col, 1)

            pe.wait_ge(s_con, 16)
            pe.wait_ge(s_x, 16)
            for b in range(4):
                for k in range(2):
                    for t in range(2):
                        kt = 2 * b + k
                        ins = nc.tensor.transpose(mx[:, b, (2 * k + t) * P:(2 * k + t + 1) * P],
                                                  xtok[:, t, kt * P:(kt + 1) * P], ident)
                ins.then_inc(boot_t, 1)
            pe.wait_ge(s_rows, 9 * 16)
            nc.tensor.transpose(acc[:, 0, 0:P], rows[:, 0], ident).then_inc(boot_t, 1)
            pe.wait_ge(s_rows2, 10 * 16)
            nc.tensor.transpose(acc[:, 1, 0:VECS - P], rows[0:VECS - P, 1], con[0:VECS - P, K_ID:K_ID + VECS - P]).then_inc(boot_t, 1)
            pe.wait_ge(s_small, 48)
            mm(acc[:, 2, 0:12], one[0:1, :], sinkrow[:], start=True, stop=True).then_inc(boot_t, 1)
            pe.wait_ge(boot_v, 5)
            pe.wait_ge(s_con, 32)

            with pe.Fori(0, LAYERS) as l:
                q0 = l * A_QUADS
                u0 = l * A_UNITS + KT - SLOTS
                def project(*slabs):
                    for i in slabs:
                        pe.wait_ge(acc_free, u0 + i + 1)
                        slab(q0 + i // 4, i % 4, h_hi_of, h_lo_of, acc[:, i % 4, 0:S],
                             before=(lambda k: pe.wait_ge(h_ready, l * 16 + k + 1)) if i == 0 else None).then_inc(slab_used, 1)

                def values(b):
                    pe.wait_ge(acc_free, u0 + SLOTS + (10, 18, 24)[b])
                    if b == 0:
                        pe.wait_ge(f_bcsb, l * 3 + 2)
                    if b == 1:
                        pe.wait_ge(ml_y, l + 1)
                    if b == 2:
                        pe.wait_ge(v_sb, l * 3 + 2)
                    for n, ch in enumerate(V_PAIRS[b]):
                        for t in range(2):
                            ins = nc.tensor.transpose(mx[:, 3 if b else 2, (2 * n + t) * P:(2 * n + t + 1) * P],
                                                      proj[:, ch, t * P:(t + 1) * P], ident)
                    ins.then_inc(v_t, 1)

                groups = QK_GROUPS

                def sums(g):
                    pe.wait_ge(qk_sq, l * 5 + g + 1)
                    if g >= 1:
                        pe.wait_ge(qk_r, l * 5 + g)
                    else:
                        pe.wait_ge(ml_v, l + 1)
                    mm(mx[:, 0], blk, sqq[:, g % 2], start=True, stop=True).then_inc(qk_ss, 1)

                def partners(g):
                    pe.wait_ge(qk_n, l * 5 + g + 1)
                    if g >= 2:
                        pe.wait_ge(qk_rope, l * 5 + g - 1)
                    mm(mx[:, 1 + g % 2], rotm, proj[:, groups[g]:groups[g] + 2].rearrange("p c t -> p (c t)"),
                       start=True, stop=True).then_inc(qk_rot, 1)

                def ml_scores(h):
                    k, b = h // 2, h % 2 * HD
                    if h == 0:
                        pe.wait_ge(cv_silu, l + 1)
                        pe.wait_ge(f_bcsb, l * 3 + 3)
                    if h >= 2:
                        pe.wait_ge(ml_p, l * 4 + h - 1)
                    for a, t, n in ((0, 0, S), (S, P, P)):
                        ins = mm(mx[:, h % 2, a:a + n], cv[b:b + HD, 2 + k, t:t + P], cv[b:b + HD, k, t:t + n],
                                 start=True, stop=True)
                    ins.then_inc(ml_s, 1)

                def ml_outputs(h):
                    k, b = h // 2, h % 2 * HD
                    pe.wait_ge(ml_p, l * 4 + h + 1)
                    if h == 0:
                        pe.wait_ge(f_ucsb, l + 1)
                        pe.wait_ge(v_sb, l * 3 + 1)
                    for bank in (2, 3):
                        for t, (a, n) in enumerate(((0, S), (S, P))):
                            lhs = vtok[:, 0, 2 * k + t, b:b + HD] if bank == 2 else one[:, 0:HD]
                            ins = mm(mx[b:b + HD, bank, k * S + t * P:(k + 1) * S], lhs, mw[:, h % 2, a:a + n],
                                     start=t == 0, stop=t == 1)
                    ins.then_inc(ml_nd, 1)

                def out_slab(w, half):
                    k = W_ORDER[w]
                    pe.wait_ge(lo_ready, (q0 + 6) * 4 + w + 1 + SLOTS)
                    if w == 0:
                        pe.wait_ge(ml_y, l + 1)
                        pe.wait_ge(acc_free, u0 + A_PROJ + SLOTS)
                    if w >= 2:
                        pe.wait_ge(at_y, l * 12 + 2 * (w - 1))
                    for n in range(4 * half, 4 * half + 4):
                        o = acc[:, n // 2, n % 2 * S:(n % 2 + 1) * S]
                        mm(o, w_hi[:, w % 4, n], y_hi[:, k], start=w == 0 and n % 2 == 0, stop=False)
                        mm(o, w_hi[:, w % 4, n], y_lo[:, k], start=False, stop=False)
                        ins = mm(o, w_lo[:, w % 4, n], y_hi[:, k], start=False, stop=w == KT - 1 and n % 2 == 1)
                    if half:
                        ins.then_inc(slab_used, 1)

                project(0, 1)
                norm_sum(l * 2)
                project(2, 3, 4, 5)
                pe.wait_ge(f_M, l + 1)
                for n in range(2):
                    for i in range(2):
                        h = 2 * n + i
                        ins = mm(mx[:, 1 + n, i * S:(i + 1) * S], con[0:4, K_SEL + h * P:K_SEL + (h + 1) * P], g_M[:],
                                 start=True, stop=True)
                    ins.then_inc(f_bc, 1)
                project(6)
                for t in range(2):
                    ins = mm(mx[:, 3, 4 * t:4 * t + 4], g_u[:, t * P:(t + 1) * P], con[0:4, K_ID:K_ID + 4], start=True, stop=True)
                ins.then_inc(f_uc, 1)
                pe.wait_ge(f_E, l + 1)
                for n in range(2):
                    ins = mm(mx[:, 0, n * S:(n + 1) * S], con[0:4, K_PAIR + n * P:K_PAIR + (n + 1) * P], g_E[:],
                             start=True, stop=True)
                ins.then_inc(f_bc, 1)
                project(7, 8)
                ml_scores(0)
                project(9)
                ml_scores(1)
                values(0)
                project(10)
                ml_outputs(0)
                project(11)
                ml_scores(2)
                ml_outputs(1)
                ml_scores(3)
                project(12)
                ml_outputs(2)
                ml_outputs(3)
                project(13, 14, 15)
                pe.wait_ge(ml_sq, l + 1)
                mm(mx[:, 0], blk, sqq[:, 0], start=True, stop=True).then_inc(ml_ss, 1)
                project(16)
                sums(0)
                project(17)
                sums(1)
                project(18)
                partners(0)
                project(19)
                values(1)
                sums(2)
                project(20)
                partners(1)
                project(21)
                sums(3)
                project(22)
                partners(2)
                project(23)
                sums(4)
                out_slab(0, 0)
                out_slab(0, 1)
                partners(3)
                values(2)
                partners(4)
                def at_scores(h):
                    i, b = h % 2, h % 2 * HD
                    if h == 0:
                        pe.wait_ge(qk_r, l * 5 + 5)
                        pe.wait_ge(qk_rope, l * 5 + 3)
                    if h == 6:
                        pe.wait_ge(swp_sb, l + 1)
                    if h >= 2:
                        pe.wait_ge(at_m, l * 12 + h - 1)
                    if h < 6:
                        q, key = proj[b:b + HD, C_MQ + h // 2], proj[b:b + HD, C_MK + h // 2]
                    else:
                        g = h - 6
                        q = proj[b:b + HD, C_SQ + g // 2]
                        key = proj[b:b + HD, C_SK] if g // 3 * HD == b else skswap[b:b + HD]
                    mm(mx[:, i, 0:P], q[:, 0:P], key[:, 0:P], start=True, stop=True)
                    mm(mx[:, i, P:384], q[:, P:S], key, start=True, stop=True).then_inc(at_s, 1)

                at_scores(0)
                pe.wait_ge(qk_rope, l * 5 + 5)
                pe.wait_ge(v_sb, l * 3 + 3)
                mm(mx[:, 3, 0:S], swpm, proj[:, C_SK], start=True, stop=True).then_inc(swp_t, 1)
                at_scores(1)
                for h in range(12):
                    i, b = h % 2, h % 2 * HD
                    if h + 2 < 12:
                        at_scores(h + 2)
                    pe.wait_ge(at_p, l * 12 + h + 1)
                    if h >= 1:
                        pe.wait_ge(at_pt, l * 12 + h)
                    else:
                        pe.wait_ge(swp_sb, l + 1)
                    for n, a in enumerate((0, P, 2 * P)):
                        ins = nc.tensor.transpose(mx[:, 2, a:a + P], pr[:, i, a:a + P], ident)
                    ins.then_inc(at_t, 1)
                    if h >= 1:
                        out_slab((h + 1) // 2, (h + 1) % 2)
                    pe.wait_ge(at_pt, l * 12 + h + 1)
                    if h >= 2:
                        pe.wait_ge(at_y, l * 12 + h - 1)
                    if h < 6:
                        v = lambda t: vtok[:, 1 + h // 4, 2 * (h // 2 % 2) + t, b:b + HD]
                    else:
                        v = lambda t: vtok[:, 2, 2 + t, (h - 6) // 3 * HD:(h - 6) // 3 * HD + HD]
                    mm(mx[b:b + HD, 3, 0:S], v(0), pT[:, i, 0:S], start=True, stop=False)
                    mm(mx[b:b + HD, 3, P:S], v(1), pT[:, i, S:384], start=False, stop=True).then_inc(at_o, 1)

                out_slab(6, 1)
                out_slab(7, 0)
                out_slab(7, 1)

                def up(it, half, first=False):
                    for j in range(4):
                        pe.wait_ge(acc_free, u0 + 32 + it * 8 + half * 4 + j + 1)
                        slab(q0 + 8 + it * 2 + half, j, h_hi_of, h_lo_of, acc[:, j, 0:S],
                             before=(lambda k: pe.wait_ge(h_ready, l * 16 + KT + k + 1)) if first and j == 0 else None).then_inc(slab_used, 1)
                        if first and j == 1:
                            norm_sum(l * 2 + 1)
                    ada_partitions(l, it * 2 + half, half)

                up(0, 0, True)
                up(0, 1)
                with pe.Fori(1, 4) as it:
                    up(it, 0)
                    up(it, 1)
                with pe.Fori(0, 2) as it:
                    for n in range(4):
                        pe.wait_ge(acc_free, u0 + 64 + it * 4 + n + 1)
                        for j in range(4):
                            pe.wait_ge(u_ready, l * 32 + (j + 1) * KT)
                            slab(q0 + 16 + it * 4 + n, j, lambda k: u_hi[:, j * KT + k], lambda k: u_lo[:, j * KT + k],
                                 acc[:, n, 0:S], j == 0, j == 3).then_inc(slab_used, 1)
                            if j % 2:
                                ada_partitions(l, it * 8 + 8 + 2 * n + j // 2, j // 2)

            with pe.Fori(0, LAYERS) as l:
                q0 = l * B_QUADS + LAYERS * A_QUADS
                u0 = l * B_UNITS + LAYERS * A_UNITS + KT - SLOTS

                def project(*chunks):
                    for i in chunks:
                        pe.wait_ge(acc_free, u0 + i + 1)
                        slab(q0 + i // 4, i % 4, lambda k: h_hi[:, k], lambda k: h_lo[:, k], acc[:, i % 4, 0:S + 2],
                             before=(lambda k: pe.wait_ge(h_ready, l * 16 + 32 + k + 1)) if i == 0 else None).then_inc(slab_used, 1)

                project(0, 1)
                norm_sum(l * 2 + 4)
                project(2, 3)
                dense(q0 + 1, 3, (h_hi, h_lo), u0 + 4, (h_ready, l * 16 + 32 + KT), S + 2)

                def partners2(g):
                    if g >= 2:
                        pe.wait_ge(b_rope, l * 4 + g - 1)
                    mm(mx[:, g % 2], rotm, projb[:, 2 * g:2 * g + 2].rearrange("p c t -> p (c t)"),
                       start=True, stop=True).then_inc(b_rot, 1)

                def values2(g):
                    if g >= 2:
                        pe.wait_ge(b_vsb, l * 4 + g - 1)
                    for n in range(2):
                        for t in range(2):
                            ins = nc.tensor.transpose(mx[:, 2 + g % 2, (2 * n + t) * P:(2 * n + t + 1) * P],
                                                      projb[:, B_V + 2 * g + n, t * P:(t + 1) * P], ident)
                    ins.then_inc(b_vt, 1)

                def ret_scores(h):
                    k, b = h // 2, h % 2 * HD
                    if h >= 2:
                        pe.wait_ge(b_p, l * 8 + h - 1)
                    for a, t, n in ((0, 0, S), (S, P, P)):
                        ins = mm(mx[:, h % 2, a:a + n], projb[b:b + HD, B_K + k, t:t + P], projb[b:b + HD, B_Q + k, t:t + n],
                                 start=True, stop=True)
                    ins.then_inc(b_s, 1)

                def ret_outputs(q):
                    if q >= 1:
                        pe.wait_ge(b_y, l * 4 + q)
                    for i in range(2):
                        h = 2 * q + i
                        pe.wait_ge(b_p, l * 8 + h + 1)
                        for t, (a, n) in enumerate(((0, S), (S, P))):
                            ins = mm(mx[:, 2, i * S + t * P:(i + 1) * S], vtokb[:, h // 2, 2 * (h % 2) + t], pb[:, i, a:a + n],
                                     start=t == 0, stop=t == 1)
                    ins.then_inc(b_ret, 1)

                def grouped(g):
                    pe.wait_ge(b_pool, l * 4 + g + 1)
                    mm(mx[:, g, 0:S], lgrp[:, g], projb[:, B_PIN + g], start=True, stop=True).then_inc(b_grp, 1)

                pe.wait_ge(acc_free, u0 + SLOTS + 8)
                partners2(0)
                partners2(1)
                project(16)
                pe.wait_ge(acc_free, u0 + SLOTS + 16)
                values2(0)
                values2(1)
                project(17)
                partners2(2)
                project(18)
                partners2(3)
                project(19)
                values2(2)
                values2(3)
                project(20)
                pe.wait_ge(b_rope, l * 4 + 4)
                ret_scores(0)
                ret_scores(1)
                project(21, 22)
                pe.wait_ge(b_vsb, l * 4 + 4)
                for q in range(4):
                    ret_outputs(q)
                    project(23 + 5 * q)
                    if q + 1 < 4:
                        ret_scores(2 * q + 2)
                        ret_scores(2 * q + 3)
                    pe.wait_ge(b_sq, l * 4 + q + 1)
                    mm(mx[:, 3], one, sqb[:], start=True, stop=True).then_inc(b_ss, 1)
                    project(*range(24 + 5 * q, 28 + 5 * q))
                grouped(0)
                grouped(1)
                project(43)
                grouped(2)
                grouped(3)
                dense(q0 + 11, 2, (y_hi, y_lo), u0 + 44, (b_y, l * 4 + 4))
                pe.wait_ge(b_z, l * 4 + 4)
                for j in range(4):
                    pe.wait_ge(acc_free, u0 + 52 + j + 1)
                    flat = [w[:, j].rearrange("p k n -> p (k n)") for w in (w_hi, w_lo)]
                    for n in range(2):
                        ins = slab(q0 + 13, j, h_hi_of, h_lo_of, acc[:, j, n * S:(n + 1) * S], kts=4,
                                   lhs=lambda k: [f[:, k * 256 + n * P:k * 256 + (n + 1) * P] for f in flat])
                    ins.then_inc(slab_used, 1)
                for j in range(8):
                    pe.wait_ge(acc_free, u0 + 56 + j + 1)
                    slab(q0 + 14 + j // 4, j % 4, lambda k: y_hi[:, k], lambda k: y_lo[:, k], acc[:, j % 4, 0:S],
                         before=(lambda k: pe.wait_ge(b_mrg, l * 4 + k // 2 + 1)) if j == 0 else None).then_inc(slab_used, 1)
                for j in range(4):
                    pe.wait_ge(acc_free, u0 + 64 + j + 1)
                    slab(q0 + 16, j, lambda k: h_hi[:, k], lambda k: h_lo[:, k], acc[:, j, 0:S + 2],
                         before=(lambda k: pe.wait_ge(h_ready, l * 16 + 32 + KT + k + 1)) if j == 0 else None).then_inc(slab_used, 1)
                    if j == 1:
                        norm_sum(l * 2 + 5)
                dense(q0 + 17, 10, (h_hi, h_lo), u0 + 68, (h_ready, l * 16 + 32 + 2 * KT), S + 2)
                with pe.Fori(0, 2) as it:
                    for n in range(4):
                        pe.wait_ge(acc_free, u0 + 108 + it * 4 + n + 1)
                        for j in range(4):
                            pe.wait_ge(g_used, l * 22 + FFO_AT[j] + FFO_PARTS[j] + 2)
                            slab(q0 + 27 + it * 4 + n, j, lambda k: u_hi[:, FFO_AT[j] + k], lambda k: u_lo[:, FFO_AT[j] + k],
                                 acc[:, n, 0:S], j == 0, j == 3, kts=FFO_PARTS[j]).then_inc(slab_used, 1)

            pe.wait_ge(acc_free, LAYERS * (A_UNITS + B_UNITS) + KT)
            for b in range(4):
                for n in range(4):
                    kt, t = 4 * (b % 2) + n, b // 2
                    if t == 0:
                        pe.wait_ge(fin_h, kt + 1)
                    ins = nc.tensor.transpose(acc[:, b, n * P:(n + 1) * P], hf[:, kt, t * P:(t + 1) * P], ident)
                ins.then_inc(fin_t, 1)
            pe.wait_ge(n_acc, 8 * KT + KT)
            for t in range(2):
                ins = mm(mx[:, 0, t:t + 1], ssq[:, t * P:(t + 1) * P], one[:, 0:1], start=True, stop=True)
            ins.then_inc(n_ss, 1)


_INS = ["x", "ln1", "w_in", "conv_w", "conv_b", "igate_b", "fgate_b", "mlstm_norm", "moba_q_norm", "moba_k_norm",
        "swa_q_norm", "swa_k_norm", "swa_sinks", "w_out", "ln2", "w_up", "w_down", "c_2", "w_ada_2", "b_ada_2",
        "norm1_2", "w_in_2", "w_ret_o_2", "w_pool_grp_2", "pool_scale_2", "w_pool_o_2", "w_out_2", "norm2_2",
        "w_ffn_in_2", "w_ffn_out_2", "final_norm_2"]


def kernel(**inputs):
    import numpy as np
    import concourse.bacc as bacc
    from concourse.bass_utils import run_bass_kernel_spmd

    nc = bacc.Bacc("TRN2", target_bir_lowering=False, num_devices=1)
    arrays = {"consts": shape_constants()}
    for name in _INS:
        arrays["in_" + name] = np.ascontiguousarray(inputs[name])
    args = [nc.dram_tensor(n, a.shape, mybir.dt.from_np(a.dtype), kind="ExternalInput").ap() for n, a in arrays.items()]
    result = nc.dram_tensor("out_0", (1, S, D), F32, kind="ExternalOutput").ap()
    program(nc, *args, result)
    r = run_bass_kernel_spmd(nc, [arrays], core_ids=[0])
    return r.results[0]["out_0"]
```
